# Optimizing a Trainium2 kernel written in Bass

```python
import math
import jax, jax.numpy as jnp
from jax import lax
import numpy as np

D_MODEL = 1024
BATCH = 1
SEQ = 256
DEPTH = 2
DEC_BATCH = 8
DEC_SEQ = 1
PAST_LEN = 2048
PAGE_SIZE = 128

H_A = 6
DK_A = 128
DV_A = 128
QK_A = H_A * DK_A
V_A = H_A * DV_A
CONV_W = 4
CONV_DIM = 2 * QK_A + V_A
GDN_CHUNK = 64
G_B = 6
CH_B = 128
D_B = G_B * CH_B
CHUNK_B = 128
N_MEM = 256
H_X = 4
DH_X = 64
D_X = H_X * DH_X
D_MIX = V_A + D_X
IN_A = CONV_DIM + V_A + 2 * H_A + D_X
IN_B = 2 * D_B + D_X
D_FF = 3584
N_EXP = 8
TOP_K = 2
N_A = (DEPTH + 1) // 2
N_B = DEPTH // 2
ALPHA = (2 * DEPTH) ** 0.25
BETA_INIT = (8 * DEPTH) ** -0.25
LN_EPS = 1e-5
RMS_EPS = 1e-6

kernel_name = "hybrid_gdn_gmlp_memxattn_deepnorm_step"

def layer_norm(x, g, b):
    xf = x.astype(jnp.float32)
    mu = jnp.mean(xf, axis=-1, keepdims=True)
    var = jnp.mean(jnp.square(xf - mu), axis=-1, keepdims=True)
    y = (xf - mu) * lax.rsqrt(var + LN_EPS) * g.astype(jnp.float32) + b.astype(jnp.float32)
    return y.astype(x.dtype)

def l2norm(x):
    return x * lax.rsqrt(jnp.sum(x * x, axis=-1, keepdims=True) + RMS_EPS)

def causal_conv_silu(xh, w):
    T = xh.shape[1] - (CONV_W - 1)
    y = sum(xh[:, j:j + T] * w[j] for j in range(CONV_W))
    return jax.nn.silu(y)

def gdn_chunked(q, k, v, g, beta, S0):
    B, T, H, _ = q.shape
    C = GDN_CHUNK
    N = T // C

    def to_chunks(t):
        return jnp.moveaxis(t.reshape(B, N, C, *t.shape[2:]), 3, 2)

    qc, kc, vc, gc, bc = (to_chunks(t) for t in (q, k, v, g, beta))
    gcum = jnp.cumsum(gc, axis=-1)
    idx = jnp.arange(C)
    causal = idx[:, None] >= idx[None, :]
    strict = idx[:, None] > idx[None, :]
    diff = gcum[..., :, None] - gcum[..., None, :]
    decay = jnp.exp(jnp.where(causal, diff, -jnp.inf))
    kb = kc * bc[..., None]
    A = jnp.where(strict, jnp.einsum('bnhik,bnhjk->bnhij', kb, kc) * decay, 0.0)
    eye = jnp.eye(C, dtype=jnp.float32)
    rhs = jnp.concatenate([vc * bc[..., None], kb * jnp.exp(gcum)[..., None]], axis=-1)
    sol = lax.linalg.triangular_solve(eye + A, rhs, left_side=True, lower=True)
    u_val, w_cum = sol[..., :DV_A], sol[..., DV_A:]
    attn_intra = jnp.einsum('bnhik,bnhjk->bnhij', qc, kc) * decay
    q_dec = qc * jnp.exp(gcum)[..., None]
    k_dec = kc * jnp.exp(gcum[..., -1:] - gcum)[..., None]
    g_last = jnp.exp(gcum[..., -1])
    xs = tuple(jnp.moveaxis(t, 1, 0) for t in (attn_intra, q_dec, k_dec, u_val, w_cum, g_last))

    def step(S, inp):
        attn, qd, kd, uv, wc, gl = inp
        vnew = uv - jnp.einsum('bhck,bhkv->bhcv', wc, S)
        o = jnp.einsum('bhck,bhkv->bhcv', qd, S) + jnp.einsum('bhij,bhjv->bhiv', attn, vnew)
        S = S * gl[..., None, None] + jnp.einsum('bhck,bhcv->bhkv', kd, vnew)
        return S, o

    S, o = lax.scan(step, S0, xs)
    o = jnp.transpose(o, (1, 0, 3, 2, 4)).reshape(B, T, H, DV_A)
    return o, S

def gdn_recurrent(q, k, v, g, beta, S0):
    def step(S, inp):
        qt, kt, vt, gt, bt = inp
        S = S * jnp.exp(gt)[..., None, None]
        u = bt[..., None] * (vt - jnp.einsum('bhk,bhkv->bhv', kt, S))
        S = S + jnp.einsum('bhk,bhv->bhkv', kt, u)
        return S, jnp.einsum('bhk,bhkv->bhv', qt, S)

    xs = tuple(jnp.moveaxis(t, 1, 0) for t in (q, k, v, g, beta))
    S, o = lax.scan(step, S0, xs)
    return jnp.moveaxis(o, 0, 1), S

def gdn_mixer(proj, conv_hist, conv_w, A_log, dt_bias, norm_w, S0, chunked):
    B, T, _ = proj.shape
    f32 = jnp.float32
    qkv_pre = proj[..., :CONV_DIM]
    z = proj[..., CONV_DIM:CONV_DIM + V_A]
    a = proj[..., CONV_DIM + V_A:CONV_DIM + V_A + H_A]
    bb = proj[..., CONV_DIM + V_A + H_A:]
    xh = jnp.concatenate([conv_hist.astype(qkv_pre.dtype), qkv_pre], axis=1)
    new_hist = xh[:, -(CONV_W - 1):]
    qkv = causal_conv_silu(xh, conv_w).astype(f32)
    q = l2norm(qkv[..., :QK_A].reshape(B, T, H_A, DK_A)) * (DK_A ** -0.5)
    k = l2norm(qkv[..., QK_A:2 * QK_A].reshape(B, T, H_A, DK_A))
    v = qkv[..., 2 * QK_A:].reshape(B, T, H_A, DV_A)
    g = -jnp.exp(A_log.astype(f32)) * jax.nn.softplus(a.astype(f32) + dt_bias.astype(f32))
    beta = jax.nn.sigmoid(bb.astype(f32))
    fn = gdn_chunked if chunked else gdn_recurrent
    o, S = fn(q, k, v, g, beta, S0.astype(f32))
    o = o * lax.rsqrt(jnp.mean(o * o, axis=-1, keepdims=True) + RMS_EPS) * norm_w.astype(f32)
    o = o * jax.nn.silu(z.astype(f32).reshape(B, T, H_A, DV_A))
    return o.reshape(B, T, V_A).astype(proj.dtype), new_hist, S.astype(proj.dtype)

def sgu_mixer(proj, ln_g, ln_b, w_s, b_s):
    B, T, _ = proj.shape
    u = jax.nn.gelu(proj[..., :D_B])
    v = layer_norm(jax.nn.gelu(proj[..., D_B:]), ln_g, ln_b)
    n = -(-T // CHUNK_B)
    pad = n * CHUNK_B - T
    vp = jnp.pad(v, ((0, 0), (0, pad), (0, 0))).reshape(B, n, CHUNK_B, G_B, CH_B)
    mask = jnp.tril(jnp.ones((CHUNK_B, CHUNK_B), dtype=bool))
    ws = jnp.where(mask, w_s, 0.0).astype(v.dtype)
    mixed = jnp.einsum('gij,bnjgc->bnigc', ws, vp) + b_s.T.astype(v.dtype)[None, None, :, :, None]
    mixed = mixed.reshape(B, n * CHUNK_B, D_B)[:, :T]
    return u * mixed, v

def mem_kv(mem, w_kv):
    B = mem.shape[0]
    kv = jnp.einsum('bmd,de->bme', mem, w_kv)
    return (kv[..., :D_X].reshape(B, N_MEM, H_X, DH_X),
            kv[..., D_X:].reshape(B, N_MEM, H_X, DH_X))

def cross_attend(xq, mk, mv):
    B, T, _ = xq.shape
    q = xq.reshape(B, T, H_X, DH_X)
    s = jnp.einsum('bthd,bmhd->bhtm', q, mk).astype(jnp.float32) * (DH_X ** -0.5)
    p = jax.nn.softmax(s, axis=-1).astype(mv.dtype)
    return jnp.einsum('bhtm,bmhd->bthd', p, mv).reshape(B, T, D_X)

def swiglu(x, w_gu, w_down):
    F = w_down.shape[-2]
    gu = x @ w_gu
    return (jax.nn.silu(gu[..., :F]) * gu[..., F:]) @ w_down

def moe_swiglu(x, w_router, w_gu, w_down):
    logits = jnp.einsum('btd,de->bte', x, w_router).astype(jnp.float32)
    top_val, top_idx = lax.top_k(logits, TOP_K)
    gates = jax.nn.softmax(top_val, axis=-1)
    combine = jnp.einsum('btk,btke->bte', gates,
                         jax.nn.one_hot(top_idx, N_EXP, dtype=jnp.float32)).astype(x.dtype)
    y = jnp.zeros_like(x)
    for e in range(N_EXP):
        y = y + combine[..., e:e + 1] * swiglu(x, w_gu[e], w_down[e])
    return y

def trunk(x, mem_k, mem_v, conv_hist, gdn_s0, chunked,
          a_w_in, a_conv_w, a_A_log, a_dt_bias, a_norm_w,
          b_w_in, b_ln_g, b_ln_b, b_w_s, b_b_s,
          w_out, ln1_g, ln1_b, ln2_g, ln2_b,
          ffn_w_gu, ffn_w_down, moe_router, moe_w_gu, moe_w_down):
    new_conv, new_s, sgu_v = [], [], []
    for i in range(DEPTH):
        j = i // 2
        if i % 2 == 0:
            proj = x @ a_w_in[j]
            mix, hist, S = gdn_mixer(proj[..., :IN_A - D_X], conv_hist[j], a_conv_w[j],
                                     a_A_log[j], a_dt_bias[j], a_norm_w[j], gdn_s0[j], chunked)
            new_conv.append(hist)
            new_s.append(S)
        else:
            proj = x @ b_w_in[j]
            mix, v = sgu_mixer(proj[..., :2 * D_B], b_ln_g[j], b_ln_b[j], b_w_s[j], b_b_s[j])
            sgu_v.append(v)
        xo = cross_attend(proj[..., -D_X:], mem_k[i], mem_v[i])
        h = jnp.concatenate([mix, xo], axis=-1) @ w_out[i]
        x = layer_norm(ALPHA * x + h, ln1_g[i], ln1_b[i])
        if i % 2 == 0:
            f = swiglu(x, ffn_w_gu[j], ffn_w_down[j])
        else:
            f = moe_swiglu(x, moe_router[j], moe_w_gu[j], moe_w_down[j])
        x = layer_norm(ALPHA * x + f, ln2_g[i], ln2_b[i])
    return x, jnp.stack(new_conv), jnp.stack(new_s), jnp.stack(sgu_v)

def setup_inputs(seed: int = 0) -> dict:
    key = jax.random.key(seed)
    ks = jax.random.split(key, 32)
    nrm = jax.random.normal
    f32 = jnp.float32
    dt = jnp.exp(jax.random.uniform(ks[9], (N_A, H_A)) * (math.log(0.1) - math.log(0.001)) + math.log(0.001))
    return {
        "x_prompt": nrm(ks[0], (BATCH, SEQ, D_MODEL), f32),
        "x_sample": nrm(ks[1], (DEC_BATCH, DEC_SEQ, D_MODEL), f32),
        "state_gdn": nrm(ks[2], (N_A, DEC_BATCH, H_A, DK_A, DV_A), f32) * DK_A ** -0.5,
        "state_conv": nrm(ks[3], (N_A, DEC_BATCH, CONV_W - 1, CONV_DIM), f32),
        "cache_mem_k": nrm(ks[4], (DEPTH, DEC_BATCH, N_MEM, H_X, DH_X), f32),
        "cache_mem_v": nrm(ks[5], (DEPTH, DEC_BATCH, N_MEM, H_X, DH_X), f32),
        "mem_prompt": nrm(ks[6], (BATCH, N_MEM, D_MODEL), f32),
        "a_w_in": nrm(ks[7], (N_A, D_MODEL, IN_A), f32) * D_MODEL ** -0.5,
        "a_conv_w": nrm(ks[8], (N_A, CONV_W, CONV_DIM), f32) * CONV_W ** -0.5,
        "a_A_log": jnp.log(jax.random.uniform(ks[10], (N_A, H_A), f32, 1.0, 16.0)),
        "a_dt_bias": dt + jnp.log(-jnp.expm1(-dt)),
        "a_norm_w": 1.0 + 0.02 * nrm(ks[11], (N_A, DV_A), f32),
        "b_w_in": nrm(ks[12], (N_B, D_MODEL, IN_B), f32) * D_MODEL ** -0.5,
        "b_ln_g": 1.0 + 0.02 * nrm(ks[13], (N_B, D_B), f32),
        "b_ln_b": 0.02 * nrm(ks[14], (N_B, D_B), f32),
        "b_w_s": nrm(ks[15], (N_B, G_B, CHUNK_B, CHUNK_B), f32) * CHUNK_B ** -0.5,
        "b_b_s": 1.0 + 0.02 * nrm(ks[16], (N_B, G_B, CHUNK_B), f32),
        "w_mem_kv": nrm(ks[17], (DEPTH, D_MODEL, 2 * D_X), f32) * D_MODEL ** -0.5,
        "w_out": nrm(ks[18], (DEPTH, D_MIX, D_MODEL), f32) * (D_MIX ** -0.5 * BETA_INIT),
        "ln1_g": 1.0 + 0.02 * nrm(ks[19], (DEPTH, D_MODEL), f32),
        "ln1_b": 0.02 * nrm(ks[20], (DEPTH, D_MODEL), f32),
        "ln2_g": 1.0 + 0.02 * nrm(ks[21], (DEPTH, D_MODEL), f32),
        "ln2_b": 0.02 * nrm(ks[22], (DEPTH, D_MODEL), f32),
        "ffn_w_gu": nrm(ks[23], (N_A, D_MODEL, 2 * D_FF), f32) * D_MODEL ** -0.5,
        "ffn_w_down": nrm(ks[24], (N_A, D_FF, D_MODEL), f32) * (D_FF ** -0.5 * BETA_INIT),
        "moe_router": nrm(ks[25], (N_B, D_MODEL, N_EXP), f32) * D_MODEL ** -0.5,
        "moe_w_gu": nrm(ks[26], (N_B, N_EXP, D_MODEL, 2 * D_FF), f32) * D_MODEL ** -0.5,
        "moe_w_down": nrm(ks[27], (N_B, N_EXP, D_FF, D_MODEL), f32) * (D_FF ** -0.5 * BETA_INIT),
    }

def reference(x_prompt, x_sample, state_gdn, state_conv, cache_mem_k, cache_mem_v, mem_prompt,
              a_w_in, a_conv_w, a_A_log, a_dt_bias, a_norm_w,
              b_w_in, b_ln_g, b_ln_b, b_w_s, b_b_s,
              w_mem_kv, w_out, ln1_g, ln1_b, ln2_g, ln2_b,
              ffn_w_gu, ffn_w_down, moe_router, moe_w_gu, moe_w_down):
    pk, pv = [], []
    for i in range(DEPTH):
        k_i, v_i = mem_kv(mem_prompt, w_mem_kv[i])
        pk.append(k_i)
        pv.append(v_i)
    p_mem_k = jnp.stack(pk)
    p_mem_v = jnp.stack(pv)
    p_hist0 = jnp.zeros((N_A, BATCH, CONV_W - 1, CONV_DIM), x_prompt.dtype)
    p_s0 = jnp.zeros((N_A, BATCH, H_A, DK_A, DV_A), jnp.float32)
    y_prompt, p_conv, p_gdn, _ = trunk(
        x_prompt, p_mem_k, p_mem_v, p_hist0, p_s0, True,
        a_w_in, a_conv_w, a_A_log, a_dt_bias, a_norm_w,
        b_w_in, b_ln_g, b_ln_b, b_w_s, b_b_s,
        w_out, ln1_g, ln1_b, ln2_g, ln2_b,
        ffn_w_gu, ffn_w_down, moe_router, moe_w_gu, moe_w_down)
    y_sample, s_conv, s_gdn, s_sgu_v = trunk(
        x_sample, cache_mem_k, cache_mem_v, state_conv, state_gdn, False,
        a_w_in, a_conv_w, a_A_log, a_dt_bias, a_norm_w,
        b_w_in, b_ln_g, b_ln_b, b_w_s, b_b_s,
        w_out, ln1_g, ln1_b, ln2_g, ln2_b,
        ffn_w_gu, ffn_w_down, moe_router, moe_w_gu, moe_w_down)
    return (y_prompt, y_sample, p_gdn, p_conv, p_mem_k, p_mem_v, s_gdn, s_conv, s_sgu_v)


_drawn_inputs = setup_inputs


def setup_inputs(seed=0):
    import zlib

    import numpy as np

    out = dict(_drawn_inputs(seed))
    spreads = {}
    factors = {'cache_mem_k': 2.888, 'a_norm_w': 8.0, 'b_ln_g': 20.95, 'b_ln_b': 21.388, 'b_b_s': 7.437}
    for name, (base, spread) in spreads.items():
        noise = np.random.default_rng([zlib.crc32(name.encode()), seed]).standard_normal(out[name].shape)
        drawn = base * np.exp(spread * noise) if base else spread * noise
        out[name] = __import__('jax').numpy.asarray(drawn.astype(out[name].dtype))
    for name, factor in factors.items():
        out[name] = (out[name] * factor).astype(out[name].dtype)
    return out
```

```python
from contextlib import ExitStack

import concourse.bass as bass
from concourse import mybir

F32 = mybir.dt.float32
U32 = mybir.dt.uint32
ALU = mybir.AluOpType
ACT = mybir.ActivationFunctionType
AX_X = mybir.AxisListType.X

P = 128
D = 1024
KT = D // P
SEQ = 256
NS = 8
NT = SEQ + NS
TT = SEQ // P
H = 6
CONV = 3 * H * P
CT = CONV // P
CW = 4
PADT = CW - 1
IN_A = CONV + H * P + 2 * H + 256
D_B = 768
GB = D_B // P
IN_B = 2 * D_B + 256
MEM = 256
MT = MEM // P
HX = 4
DH = 64
DX = HX * DH
XT_ = DX // P
FF = 3584
FC = 512
NG = FF // FC
NE = 8
CAP = 3 * P
DEPTH = 2
ALPHA = (2 * DEPTH) ** 0.25
LN_EPS = 1e-5
RMS_EPS = 1e-6
SLAB = KT * FC
SLOTS = 7
LENT = 3
SLABS_PER_FFN = 3 * NG


class Banks:

    def __init__(self):
        self.count = [0] * 8
        self.of = {}

    def add(self, name, bank):
        assert name not in self.of
        self.of[name] = (bank, self.count[bank])
        self.count[bank] += 1


def plan_banks():
    banks = Banks()
    add = banks.add
    for n in range(2):
        add(("params", n), n)
    for n in range(2 * TT):
        add(("x", n), 2 + n)
    add(("xs",), 6)
    for lay in range(DEPTH):
        for n in range(2 * MT):
            add(("mem", lay, n), (7, 0, 1, 2)[n])
        for mt in range(MT):
            add(("kv", lay, mt), 3 + mt)
        add(("kT", lay), 5)
        if lay == 0:
            for c in range(5):
                add(("hist", c), (6, 7, 0, 1, 2)[c])
            n = 0
            for c in range(CT + H):
                add(("proj", 0, c), n % 8)
                n += 1
            for c in ("a", "b", 0, 1):
                add(("projx", 0, c), n % 8)
                n += 1
            for c in range(5):
                add(("tail", c), n % 8)
                n += 1
            for c in range(2 * H):
                add(("norm", c), n % 8)
                n += 1
        else:
            for c in range(2 * GB):
                add(("proj", 1, c), c % 8)
            for c in range(2):
                add(("projx", 1, c), 4 + c)
        for h in range(HX):
            add(("score", lay, h), h)
        for h in range(HX):
            add(("pT", lay, h), 4 + h)
        for n in range(2):
            add(("pv", lay, n), n)
        for b in range(NS):
            add(("cacheT", lay, b), 4 + b % 2)
            if b == 0:
                add(("sscore", lay), 2)
        add(("spT", lay), 3)
        add(("spv", lay), 6)
        if lay == 0:
            add(("sgate",), 7)
            add(("sdot",), 0)
            add(("sread",), 1)
            for n in range(2):
                add(("krow", n), 2 + n)
                add(("urow", n), 4 + n)
            for h in range(H):
                for n in range(2):
                    add(("outer", h, n), (6 + n) if h % 2 == 0 else n)
            for n in range(TT):
                for i in range(2):
                    add(("gb", n, i), i)
                for i in range(2):
                    add(("bb", n, i), 2 + i)
                add(("gcol", n), 4)
                for i in range(2):
                    add(("kk", n, i), 5 + i)
                for i in range(2):
                    add(("qk", n, i), (7, 0)[i])
                for i in range(2):
                    add(("ktok", n, i), 1 + i)
                for i in range(2):
                    add(("vtok", n, i), 3 + i)
                for i in range(2):
                    add(("xinit", n, i), 5 + i)
                for s in range(1, 7):
                    for i in range(2):
                        add(("Y", n, s, i), i)
                    if s < 6:
                        for i in range(2):
                            add(("dX", n, s, i), 2 + i)
                    for i in range(2):
                        add(("dXT", n, s, i), 4 + i)
                if n:
                    for i in range(2):
                        add(("wT", n, i), 6 + i)
                for i in range(2):
                    add(("vnew", n, i), i)
                for i in range(2):
                    add(("o", n, i), 2 + i)
                for i in range(2):
                    add(("S", n, i), 4 + i)
            for h in range(H):
                add(("rms", h), h)
        else:
            add(("vmean",), 7)
            for n in range(2):
                add(("wsT", n), 5 + n)
            add(("vvar",), 0)
            for n in range(4):
                add(("vtokT", n), 1 + n)
            for n in range(2):
                add(("vtokS", n), 5 + n)
            add(("mixrow",), 7)
            for g in range(GB):
                add(("mixed", g), g)
        for c in range(KT):
            add(("out", lay, c), c)
        add(("ln_mean", lay, 0), 0)
        add(("ln_var", lay, 0), 1)
        if lay == 0:
            for c in range(NG + 1):
                if c < NG:
                    for f in range(4):
                        add(("gate", c, f), 2 * (f % 2))
                        add(("up", c, f), 2 * (f % 2) + 1)
                if c:
                    for d in range(KT):
                        add(("down", c - 1, d), 4 + d % 4)
            add(("ln_mean", lay, 1), 0)
            add(("ln_var", lay, 1), 1)
    for n in range(2 * TT):
        add(("x1tok", n), 2 + n)
    for n in range(2):
        add(("x1tokS", n), 6 + n)
    add(("logits",), 0)
    add(("rank",), 1)
    return banks.of


def plan_slabs():
    slabs = [("kv", 0)] + [("in", 0, c) for c in range(7)] + [("out", 0, c) for c in range(2)]
    slots = [n % LENT for n in range(len(slabs))]
    for c in range(NG + 1):
        slabs += [("gate", c), ("up", c)] * (c < NG) + [("down", c - 1)] * (c > 0)
    slots += [(1, 3, 4, 5, 6, 2, 0)[j % SLOTS] for j in range(SLABS_PER_FFN)]
    slabs += [("kv", 1)] + [("in", 1, c) for c in range(4)] + [("out", 1, c) for c in range(2)]
    slots += [(1, 2, 0)[j % 3] for j in range(7)]
    plan, last, landed = {}, {}, [0] * SLOTS
    for n, (what, slot) in enumerate(zip(slabs, slots)):
        plan[what] = (n, slot, landed[slot] + 1, last.get(slot, "lent" if slot >= LENT else None))
        landed[slot] += 1
        last[slot] = n
    return plan, last, landed


def expert_order():
    order = []
    for c in range(NG + 1):
        order += [("gate", c), ("up", c)] * (c < NG) + [("down", c - 1)] * (c > 0)
    return order


EXPERT_SLOTS = (2, 3, 4, 5, 6, 0, 1)


def hybrid_step(nc, a, out, xy):
    bank_of = plan_banks()
    slab_of, slot_last, slot_landed = plan_slabs()
    n_static = len(slab_of)

    with ExitStack() as ctx:
        names = {}

        def sig(name):
            if name not in names:
                names[name] = ctx.enter_context(nc.semaphore(name))
            return names[name]

        total = 53000
        sb = ctx.enter_context(nc.sbuf_tensor("sb", [P, total], F32))
        ps = ctx.enter_context(nc.psum_tensor("ps", [P, 8, 512], F32))
        at = [0]

        def place(*shape, base=None):
            n = 1
            for s in shape:
                n *= s
            if base is None:
                off = at[0]
                at[0] += n
            else:
                off = base
            assert off + n <= total, (off, n)
            ap = sb[:, off:off + n]
            if len(shape) == 2:
                ap = ap.rearrange("p (a b) -> p a b", a=shape[0])
            if len(shape) == 3:
                ap = ap.rearrange("p (a b c) -> p a b c", a=shape[0], b=shape[1])
            return ap

        ring = [place(SLAB) for _ in range(SLOTS)]
        lent0 = LENT * SLAB
        xT = place(KT, NT)
        mixT = place(KT, NT)
        y0 = at[0]
        yT = place(KT, NT)
        sq0 = at[0]
        sq = place(KT, NT)
        ident = place(P)
        ones = place(P)
        strictT = place(P)
        causalT = place(P)
        stage_mask = place(7, P)
        pcol1 = place(85)
        pcol2 = place(64)
        conv_col = pcol1[:, 0:CW * CT].rearrange("p (j c) -> p j c", j=CW)
        bln_g, bln_b, norm_w = pcol1[:, 72:78], pcol1[:, 78:84], pcol1[:, 84:85]
        ln_col = pcol2.rearrange("p (w l k) -> p w l k", w=4, l=DEPTH)
        gc = place(NT)
        beta = place(NT)
        gpar = place(4)
        tok_g = place(H)
        tok_b = place(H)
        tok_eg = place(H)
        tok_beg = place(H)
        tok_kd = place(H)
        glast = place(H)
        eglast = place(H)
        attn_max = place(8)
        attn_sum = place(8)
        eps_rms = place(1)
        eps_ln = place(1)
        mu = place(NT)
        rstd = place(NT)
        arena0 = at[0]
        qkv = place(CT, NT)
        zs = place(H, NT)
        xq = place(XT_, NT)
        kv0 = at[0]
        kv = place(MT, 2 * DX)
        kT = place(XT_, MEM)
        g0 = at[0]
        attnT = place(H, P)
        AT = place(H, P)
        X = place(H, P)
        XT = place(H, P)
        kdec = place(H, P)
        S = place(H, P)
        tails = place(CONV, base=g0)
        memT = place(KT, MEM, base=g0 + CONV)
        p_att = place(2 * HX, MEM, base=g0)
        pT_att = place(HX, MT, SEQ, base=g0 + 2 * HX * MEM)
        Y = place(H, P, base=sq0)
        AmT = place(H, P, base=sq0 + H * P)
        vb = place(H, P, base=y0)
        kbg = place(H, P, base=y0 + H * P)
        memrows = place(MT, D, base=y0)
        KTs = place(2, XT_, MEM, base=y0)
        hs = place(CT, NS * CW, base=y0 + 1024)
        qpad = place(XT_, NS, 4 * NS, base=y0 + 1600)
        gate_a, gate_n, gate_e, gate_l, gate_g = (mixT[0:H, i, :] for i in range(5))
        state = place(NS * H, P, base=lent0)
        pre = place(CT, PADT + NT, base=lent0 + 6144)
        xrows = place(3, D, base=lent0 + 6144)
        prow = place(2, P, base=lent0)
        krow = place(H, P, base=lent0 + 6144)
        urow = place(H, P, base=lent0 + 6912)
        udiag = place(2, NS * P, base=lent0 + 7680)
        sv0 = lent0 + 9728
        s_eg, s_be, s_sk, s_u, s_o, s_kq = (place(H, NS, base=sv0 + 48 * i) for i in range(6))
        Kc = place(2, MT, DX, base=lent0 + 10950)
        ps_att = place(MEM, base=lent0 + 11974)
        pTs = place(MT, 4 * NS, base=lent0 + 12230 - 64 + 58)
        histrows = place(CONV, base=lent0 + 12288)
        Vc = place(NS, MT, DX, base=lent0 + 12288)
        hid = [place(4, NT, base=0) for _ in range(2)]
        hid = [mixT[:, 0:4, :], mixT[:, 4:8, :]]
        silu_t = place(2, NT, base=arena0)
        uT = place(GB, NT, base=arena0)
        vT = place(GB, NT, base=arena0 + 1584)
        vtok = place(3, D_B, base=arena0 + 3168)
        wsT = place(GB, P, base=arena0 + 5472)
        wsrows = place(GB, P, base=sq0)
        bsrow = place(P, base=arena0 + 12800)
        rowcol = place(2 * GB, base=arena0 + 12928)
        assert arena0 + 5472 + 768 <= kv0
        assert arena0 + 12500 <= total
        x1tok = place(3, D, base=arena0)
        Xe = place(D, base=arena0 + 3072)
        XeT = place(KT, P, base=arena0 + 4096)
        hsil = place(2, FC, base=arena0 + 5120)
        hgu = place(2, FC, base=arena0 + 6144)
        hTe = place(2, 4, P, base=arena0 + 7168)
        yout = place(D, base=arena0 + 8192)
        router = place(KT, NE, base=arena0 + 9216)
        r0 = arena0 + 9280
        lg, oh1, oh2, Msel, rbase = (place(3, NE, base=r0 + 24 * i) for i in range(5))
        mx8 = place(3, NE, base=r0 + 120)
        idxf = place(3, NE, base=r0 + 144)
        iota8 = place(NE, base=r0 + 168)
        base8 = place(NE, base=r0 + 176)
        valid = place(3, base=r0 + 184)
        dtop = place(3, base=r0 + 187)
        g1 = place(3, base=r0 + 190)
        g2 = place(3, base=r0 + 193)
        den = place(3, base=r0 + 196)
        dstf = place(2, 3, base=r0 + 200)
        tmp24 = place(3, NE, base=r0 + 206)
        Mall = place(NE, base=r0 + 230)
        ln_bc = place(2, D, base=arena0 + 9600)
        idx8 = ctx.enter_context(nc.sbuf_tensor("idx8", [P, 3, NE], U32))
        dst = ctx.enter_context(nc.sbuf_tensor("dst", [P, 2, 3], U32))
        counts = ctx.enter_context(nc.sbuf_tensor("counts", [P, NE], U32))
        turn = ctx.enter_context(nc.sbuf_tensor("turn", [P, 2 * NE + 1], U32))
        zeros = mixT[:, :, :].rearrange("p a b -> p (a b)")[:, 0:D]
        yk = [place(2, D, base=sq0), None]
        yk = [place(D, base=sq0), place(D, base=y0)]
        acc = place(D, base=sq0 + D)
        stats = place(2, 6, base=r0 + 240)
        mv = place(2, base=r0 + 252)
        rs1 = place(1, base=r0 + 254)
        over = place(2 * NE, base=r0 + 256)
        turns = place(2 * NE + 1, base=r0 + 272)
        assert r0 + 289 <= arena0 + 9600

        bank_full = [sig(f"bank{b}_full") for b in range(8)]
        bank_free = [sig(f"bank{b}_free") for b in range(8)]
        landed = [sig(f"slot{s}_landed") for s in range(SLOTS)]
        slabs_used = sig("slabs_used")

        def slab(what):
            return ring[slab_of[what][1]]

        def wait_slab(eng, what):
            _, slot, count, _ = slab_of[what]
            eng.wait_ge(landed[slot], 16 * count)

        def take(eng, *name):
            bank, before = bank_of[name]
            eng.wait_ge(bank_full[bank], before + 1)
            return ps[:, bank, :]

        def free(ins, *name):
            return ins.then_inc(bank_free[bank_of[name][0]], 1)

        def pair(name, i):
            return name[:, 3 * i:3 * i + 3, :].rearrange("p a b -> p (a b)")

        class Chain:

            def __init__(self, eng, name):
                self.eng, self.sem, self.n = eng, sig(name), 0

            def __call__(self, ins):
                self.n += 1
                ins.then_inc(self.sem, 1)
                self.eng.wait_ge(self.sem, self.n)

            def settle(self, name):
                self.eng.sem_inc(sig(name), 1)

        block = ctx.enter_context(nc.Block())

        def w_in_source(what):
            kind = what[0]
            if kind == "kv":
                src = a["w_mem_kv"][what[1]]
                c0, n = 0, 2 * DX
            elif kind == "in":
                src = a["a_w_in" if what[1] == 0 else "b_w_in"][0]
                c0 = what[2] * FC
                n = min(FC, (IN_A if what[1] == 0 else IN_B) - c0)
            elif kind == "out":
                src = a["w_out"][what[1]]
                c0, n = what[2] * FC, FC
            elif kind in ("gate", "up"):
                src = a["ffn_w_gu"][0]
                c0, n = what[1] * FC + (FF if kind == "up" else 0), FC
            else:
                src = a["ffn_w_down"][0][what[1] * FC:(what[1] + 1) * FC]
                return src.rearrange("(k p) n -> p k n", p=P), 4, D
            return src[:, c0:c0 + n].rearrange("(k p) n -> p k n", p=P), KT, n

        def as_slab(ap, k, n):
            return ap[:, 0:k * n].rearrange("p (k n) -> p k n", k=k)

        @block.sync
        def _(sp):
            for what, (n, slot, count, before) in slab_of.items():
                if before == "lent":
                    sp.wait_ge(sig("gdn_lent_back"), 1)
                elif before is not None:
                    sp.wait_ge(slabs_used, before + 1)
                src, k, cols = w_in_source(what)
                sp.dma_start(as_slab(ring[slot], k, cols), src).then_inc(landed[slot], 16)

            def expert_slab(e, j, count, floor):
                kind, c = expert_order()[j]
                slot = EXPERT_SLOTS[j % SLOTS]
                if kind == "down":
                    src = a["moe_w_down"][0][bass.ds(e, 1)][0][c * FC:(c + 1) * FC].rearrange("(k p) n -> p k n", p=P)
                    view = as_slab(ring[slot], 4, D)
                else:
                    c0 = c * FC + (FF if kind == "up" else 0)
                    src = a["moe_w_gu"][0][bass.ds(e, 1)][0][:, c0:c0 + FC].rearrange("(k p) n -> p k n", p=P)
                    view = as_slab(ring[slot], KT, FC)
                if floor is not None:
                    sp.wait_ge(slabs_used, floor)
                sp.dma_start(view, src).then_inc(landed[slot], 16)

            for j in range(SLOTS):
                slot = EXPERT_SLOTS[j]
                if slot >= LENT:
                    sp.wait_ge(sig("attn1_lent_back"), 1)
                expert_slab(0, j, None, None if slot >= LENT else slot_last[slot] + 1)
            with sp.Fori(0, NE - 1) as e:
                for j in range(SLOTS, SLABS_PER_FFN + SLOTS):
                    ee, jj = (e, j) if j < SLABS_PER_FFN else (e + 1, j - SLABS_PER_FFN)
                    expert_slab(ee, jj, None, e * SLABS_PER_FFN + (n_static + j - SLOTS + 1))
            for j in range(SLOTS, SLABS_PER_FFN):
                expert_slab(NE - 1, j, None, (NE - 1) * SLABS_PER_FFN + n_static + j - SLOTS + 1)
            sp.wait_ge(sig("routed"), 1)
            for chunk in (1, 2):
                with sp.Fori(0, NE) as e:
                    n_tok = sp.value_load(counts[0:1, bass.ds(e, 1)], min_val=0, max_val=NT)
                    t = sp.value_load(turn[0:1, bass.ds(e + (chunk - 1) * NE, 1)], min_val=NE, max_val=3 * NE)
                    with sp.If(n_tok > chunk * P):
                        for j in range(SLABS_PER_FFN):
                            expert_slab(e, j, None, t * SLABS_PER_FFN + (n_static + j - SLOTS + 1))
            sp.wait_ge(sig("y_out"), 16 * 3)
            for s in range(DEPTH):
                sp.wait_ge(sig(f"cache_out{s}"), 32)
            sp.wait_ge(sig("state_out"), 16)
            sp.wait_ge(sig("pstate_out"), 16)
            sp.wait_ge(sig("conv_out"), 48)
            sp.wait_ge(sig("sgu_out"), 16)

        @block.gpsimd
        def _(pool):
            step = Chain(pool, "pool_step")
            pool.memset(ident, 0.0)
            pool.memset(eps_rms, RMS_EPS)
            pool.memset(eps_ln, LN_EPS)
            step(pool.memset(ones, 1.0))
            step(pool.affine_select(out=ident, in_=ident, pattern=[[-1, P]], compare_op=ALU.not_equal, fill=1.0, base=0, channel_multiplier=1))
            pool.sem_inc(sig("consts"), 1)
            sc = a["state_conv"][0].rearrange("b j c -> (b j) c")
            pool.dma_start(histrows[0:NS * PADT, :], sc).then_inc(sig("hist_landed"), 16)
            pool.dma_start(gpar[0:H, 0:1], a["a_A_log"].rearrange("a h -> h a")).then_inc(sig("gpar_landed"), 16)
            pool.dma_start(gpar[0:H, 1:2], a["a_dt_bias"].rearrange("a h -> h a")).then_inc(sig("gpar_landed"), 16)
            pool.dma_start(out["s_state_conv"][0, :, 0:PADT - 1, :], a["state_conv"][0, :, 1:PADT, :]).then_inc(sig("conv_out"), 16)
            step(pool.affine_select(out=strictT, in_=ones, pattern=[[1, P]], compare_op=ALU.is_gt, fill=0.0, base=0, channel_multiplier=-1))
            step(pool.affine_select(out=causalT, in_=ones, pattern=[[1, P]], compare_op=ALU.is_ge, fill=0.0, base=0, channel_multiplier=-1))
            same = [ident] + [stage_mask[:, s, :] for s in range(6)] + [ones]
            for s in range(1, 7):
                b = 1 << s
                v = same[s].rearrange("p (n b) -> p n b", b=b)
                o = ones.rearrange("p (n b) -> p n b", b=b)
                step(pool.affine_select(out=v, in_=o, pattern=[[-b, P // b], [0, b]], compare_op=ALU.is_ge, fill=0.0, base=0, channel_multiplier=1))
                step(pool.affine_select(out=v, in_=v, pattern=[[b, P // b], [0, b]], compare_op=ALU.is_ge, fill=0.0, base=b - 1, channel_multiplier=-1))
            for s in range(6, -1, -1):
                lower = same[s]
                step(pool.tensor_tensor(stage_mask[:, s, :], same[s + 1], lower, ALU.subtract))
                step(pool.tensor_tensor(stage_mask[:, s, :], stage_mask[:, s, :], strictT, ALU.mult))
                if s:
                    pass
            pool.sem_inc(sig("masks"), 1)
            pool.wait_ge(sig("params_in"), 1)
            pool.dma_start(state, a["state_gdn"][0].rearrange("b h k v -> k (b h) v")).then_inc(sig("state_landed"), 16)
            pool.wait_ge(sig("xrows_read"), 1)
            step(pool.memset(pre[:, :, 0:PADT], 0.0))
            pool.sem_inc(sig("pre_zero"), 1)

            def values(lay):
                for b in range(NS):
                    pool.dma_start(Vc[:, b], a["cache_mem_v"][lay, b].rearrange("(t p) h d -> p t (h d)", p=P)).then_inc(sig(f"v{lay}_landed"), 16)

            def keys(lay):
                for b in range(NS):
                    if b >= 2:
                        pool.wait_ge(bank_full[bank_of[("cacheT", lay, b - 2)][0]], bank_of[("cacheT", lay, b - 2)][1] + 1)
                    pool.dma_start(Kc[:, b % 2], a["cache_mem_k"][lay, b].rearrange("(t p) h d -> p t (h d)", p=P)).then_inc(sig(f"k{b % 2}_landed"), 16)

            def kv_out(lay):
                pool.wait_ge(sig("kv_rows"), lay + 1)
                for name, c0 in (("p_cache_mem_k", 0), ("p_cache_mem_v", DX)):
                    pool.dma_start(out[name][lay, 0].rearrange("(t p) h d -> p t (h d)", p=P), kv[:, :, c0:c0 + DX]).then_inc(sig(f"cache_out{lay}"), 16)

            kv_out(0)
            pool.wait_ge(sig("hist_done"), 1)
            values(0)
            pool.wait_ge(sig("tails_ready"), 1)
            pool.dma_start(out["p_state_conv"][0, 0], tails[0:PADT, :]).then_inc(sig("conv_out"), 16)
            pool.dma_start(out["s_state_conv"][0, :, PADT - 1, :], tails[PADT:PADT + NS, :]).then_inc(sig("conv_out"), 16)
            keys(0)
            pool.wait_ge(sig("state_landed"), 16)
            pool.wait_ge(sig("s_rows"), 1)
            st = state.rearrange("p (b h) v -> p b h v", h=H)
            for h in range(H):
                if h >= 2:
                    pool.wait_ge(bank_full[bank_of[("outer", h - 2, 1)][0]], bank_of[("outer", h - 2, 1)][1] + 1)
                ud = udiag[0:NS, h % 2, :].rearrange("p (b v) -> p b v", b=NS)
                pool.tensor_tensor(ud, urow[0:NS, h, :].unsqueeze(1).to_broadcast([NS, NS, P]),
                                   ident[0:NS, 0:NS].unsqueeze(2).to_broadcast([NS, NS, P]), ALU.mult).then_inc(sig("udiag_ready"), 1)
                pool.tensor_tensor(st[:, :, h, :], st[:, :, h, :], s_eg[:, h, :].unsqueeze(2).to_broadcast([P, NS, P]), ALU.mult).then_inc(sig("state_decayed"), 1)
            pool.wait_ge(sig("state_new"), H)
            pool.dma_start(out["s_state_gdn"][0].rearrange("b h k v -> k (b h) v"), state).then_inc(sig("state_out"), 16)
            for n in range(TT):
                pool.wait_ge(sig("A_ready"), n + 1)
                for s in range(1, 7):
                    if s > 1 or n:
                        prev = ("Y", n, s - 1, 1) if s > 1 else ("Y", n - 1, 6, 1)
                        pool.wait_ge(bank_full[bank_of[prev][0]], bank_of[prev][1] + 1)
                    if s == 1 and n:
                        pool.wait_ge(sig("w_done"), n)
                    pool.tensor_tensor(AmT, AT, stage_mask[:, s, :].unsqueeze(1).to_broadcast([P, H, P]), ALU.mult).then_inc(sig("AmT_ready"), 1)
            pool.wait_ge(sig("S_ready"), TT)
            pool.dma_start(out["p_state_gdn"][0, 0].rearrange("h k v -> k h v"), S).then_inc(sig("pstate_out"), 16)
            pool.wait_ge(sig("state_out"), 16)
            pool.wait_ge(sig("attn_done"), 1)
            pool.sem_inc(sig("gdn_lent_back"), 1)
            pool.wait_ge(slabs_used, slab_of[("down", NG - 1)][0] + 1)
            pool.wait_ge(sig("pstate_out"), 16)
            pool.dma_start(bsrow[0:GB, :], a["b_b_s"][0]).then_inc(sig("bs_landed"), 16)
            pool.wait_ge(sig("x_ready"), 2)
            pool.dma_start(memrows, a["mem_prompt"][0].rearrange("(t p) d -> p t d", p=P)).then_inc(sig("mem1_landed"), 16)
            pool.dma_start(wsrows, a["b_w_s"][0].rearrange("g i j -> i g j")).then_inc(sig("ws_landed"), 16)
            pool.wait_ge(sig("mem_read"), 2)
            kv_out(1)
            values(1)
            keys(1)
            pool.wait_ge(sig("vtok_ready"), 1)
            pool.dma_start(out["s_sgu_v"][0].rearrange("b t d -> (b t) d"), vtok[0:NS, 2, :]).then_inc(sig("sgu_out"), 16)
            pool.wait_ge(sig("attn_done"), 2)
            pool.sem_inc(sig("attn1_lent_back"), 1)
            pool.wait_ge(sig("mixer1_done"), 1)
            pool.dma_start(router, a["moe_router"][0].rearrange("(k p) e -> p k e", p=P)).then_inc(sig("router_landed"), 16)
            pool.iota(iota8, [[1, NE]], base=0, channel_multiplier=0, allow_small_or_imprecise_dtypes=True)
            pool.iota(base8, [[CAP, NE]], base=0, channel_multiplier=0, allow_small_or_imprecise_dtypes=True)
            step(pool.memset(valid, 1.0))
            step(pool.affine_select(out=valid[:, 2:3], in_=valid[:, 2:3], pattern=[[0, 1]], compare_op=ALU.is_ge, fill=0.0, base=NS - 1, channel_multiplier=-1))
            pool.sem_inc(sig("route_consts"), 1)
            pool.wait_ge(sig("fill_done"), 16)
            pool.wait_ge(sig("routed"), 1)
            pool.wait_ge(sig("x1tok_ready"), 6)
            for tt in range(3):
                np_ = P if tt < 2 else NS
                for k in range(2):
                    pool.indirect_dma_start(out=xy[:, :], out_offset=bass.IndirectOffsetOnAxis(ap=dst[0:np_, k, tt:tt + 1], axis=0),
                                            in_=x1tok[0:np_, tt, :], in_offset=None).then_inc(sig("scattered"), 16)
            pool.wait_ge(sig("scattered"), 16 * 6)

            pool.sem_inc(sig("rows_sorted"), 1)
            pool.wait_ge(sig("routed"), 1)
            runs = pool.value_load(turn[0:1, 2 * NE:2 * NE + 1], min_val=NE, max_val=3 * NE)
            pool.wait_ge(sig("y_stored"), runs * 16 + 16)
            pool.sem_inc(sig("pool_turn"), 1)
            for tt in range(3):
                np_ = P if tt < 2 else NS
                if tt:
                    pool.wait_ge(sig("yk_read"), tt)
                for k in range(2):
                    pool.indirect_dma_start(out=yk[k][0:np_, :], out_offset=None, in_=xy[:, :],
                                            in_offset=bass.IndirectOffsetOnAxis(ap=dst[0:np_, k, tt:tt + 1], axis=0)).then_inc(sig("gathered"), 16)
                pool.wait_ge(sig("gathered"), 32 * (tt + 1))

        @block.scalar
        def _(act):
            step = Chain(act, "act_step")
            conv_rows = a["a_conv_w"][0].rearrange("j (c p) -> (j c) p", p=P)
            act.dma_start(prow[0:72, 0, :], conv_rows).then_inc(sig("params_landed"), 16)
            act.dma_start(prow[72:78, 0, :], a["b_ln_g"][0].rearrange("(k p) -> k p", p=P)).then_inc(sig("params_landed"), 16)
            act.dma_start(prow[78:84, 0, :], a["b_ln_b"][0].rearrange("(k p) -> k p", p=P)).then_inc(sig("params_landed"), 16)
            act.dma_start(prow[84:85, 0, :], a["a_norm_w"]).then_inc(sig("params_landed"), 16)
            for w, name in enumerate(("ln1_g", "ln1_b", "ln2_g", "ln2_b")):
                act.dma_start(prow[16 * w:16 * w + 16, 1, :], a[name].rearrange("l (k p) -> (l k) p", p=P)).then_inc(sig("params_landed"), 16)
            act.dma_start(xrows[:, 0:TT, :], a["x_prompt"][0].rearrange("(t p) d -> p t d", p=P)).then_inc(sig("x_landed"), 16)
            act.dma_start(xrows[0:NS, TT, :], a["x_sample"].rearrange("b t d -> (b t) d")).then_inc(sig("x_landed"), 16)
            act.dma_start(memrows, a["mem_prompt"][0].rearrange("(t p) d -> p t d", p=P)).then_inc(sig("mem0_landed"), 16)

            def mem_kv(lay):
                for mt in range(MT):
                    src = take(act, "kv", lay, mt)
                    if mt == 0 and lay:
                        act.wait_ge(sig("cache_out0"), 32)
                    ins = free(act.activation(kv[:, mt, :], src, ACT.Copy), "kv", lay, mt)
                bank, before = bank_of[("kv", lay, MT - 1)]
                act.wait_ge(bank_free[bank], before + 1)
                bank, before = bank_of[("kv", lay, 0)]
                act.wait_ge(bank_free[bank], before + 1)
                act.sem_inc(sig("kv_rows"), 1)

            mem_kv(0)
            act.wait_ge(sig("pre_zero"), 1)
            for c in range(CT):
                free(act.activation(pre[:, c, PADT:], take(act, "proj", 0, c)[:, 0:NT], ACT.Copy), "proj", 0, c)
                bank, before = bank_of[("proj", 0, c)]
                act.wait_ge(bank_free[bank], before + 1)
                act.activation(qkv[:, c, 0:SEQ], pre[:, c, 0:SEQ], ACT.Copy, scale=conv_col[:, 0, c:c + 1]).then_inc(sig("conv_begun"), 1)
            for h in range(H):
                free(act.activation(zs[:, h, :], take(act, "proj", 0, CT + h)[:, 0:NT], ACT.Silu), "proj", 0, CT + h)
            for c in range(CT):
                act.wait_ge(sig("conv_sum"), c + 1)
                act.activation(qkv[:, c, 0:SEQ], qkv[:, c, 0:SEQ], ACT.Silu).then_inc(sig("conv_silu"), 1)
            act.wait_ge(sig("conv_sample"), 1)
            act.activation(qkv[:, :, SEQ:], qkv[:, :, SEQ:], ACT.Silu).then_inc(sig("conv_silu"), 1)
            act.wait_ge(sig("gate_abs"), 1)
            step(act.activation(gate_e, gate_n, ACT.Exp))
            act.activation(gate_l, gate_e, ACT.Ln, bias=1.0).then_inc(sig("gate_log"), 1)
            act.activation(gpar[0:H, 2:3], gpar[0:H, 0:1], ACT.Exp).then_inc(sig("gate_log"), 1)
            free(act.activation(beta[0:H, :], take(act, "projx", 0, "b")[0:H, 0:NT], ACT.Exp, scale=-1.0), "projx", 0, "b")
            act.wait_ge(bank_free[bank_of[("projx", 0, "b")][0]], bank_of[("projx", 0, "b")][1] + 1)
            act.sem_inc(sig("beta_exp"), 1)
            for half in range(2):
                act.wait_ge(sig("conv_silu"), CT + 1)
                if half:
                    bank, before = bank_of[("norm", H - 1)]
                    act.wait_ge(bank_full[bank], before + 1)
                    act.wait_ge(sig("qk_normed"), 1)
                act.activation(sq[:, 0:H, :], qkv[:, H * half:H * half + H, :], ACT.Square).then_inc(sig("qk_squared"), 1)
                for h in range(H):
                    src = take(act, "norm", H * half + h)
                    free(act.activation(sq[:, h, :], src[:, 0:NT], ACT.Sqrt, bias=eps_rms), "norm", H * half + h)
                for h in range(H):
                    bank, before = bank_of[("norm", H * half + h)]
                    act.wait_ge(bank_free[bank], before + 1)
                act.sem_inc(sig("qk_root"), 1)

            def attend(lay):
                for h in range(HX):
                    act.wait_ge(sig("attn_max_ready"), HX * lay + h + 1)
                    if h == 0 and lay == 0:
                        act.wait_ge(sig("conv_out"), 48)
                    src = take(act, "score", lay, h).rearrange("p (t m) -> p t m", t=TT)
                    for tt in range(TT):
                        n = TT * h + tt
                        ins = act.activation(p_att[:, n, :], src[:, tt, :], ACT.Exp, bias=attn_max[:, n:n + 1], scale=DH ** -0.5, accum_out=attn_sum[:, n:n + 1])
                        if tt == TT - 1:
                            free(ins, "score", lay, h)
                for h in range(HX):
                    bank, before = bank_of[("score", lay, h)]
                    act.wait_ge(bank_free[bank], before + 1)
                act.sem_inc(sig("attn_exp"), 1)
                for h in range(HX):
                    free(act.activation(pT_att[:, h].rearrange("p m t -> p (m t)"), take(act, "pT", lay, h), ACT.Copy), "pT", lay, h)
                for b in range(NS):
                    src = take(act, "cacheT", lay, b)
                    if b >= 2:
                        act.wait_ge(sig("sscored"), NS * lay + b - 1)
                    free(act.activation(KTs[:, b % 2].rearrange("p k m -> p (k m)"), src, ACT.Copy), "cacheT", lay, b)
                act.wait_ge(sig("ss_max"), lay + 1)
                src = take(act, "sscore", lay)
                free(act.activation(ps_att[0:4 * NS, :], src[0:4 * NS, 0:MEM], ACT.Exp, bias=attn_max[0:4 * NS, 0:1], scale=DH ** -0.5, accum_out=attn_sum[0:4 * NS, 0:1]), "sscore", lay)
                act.wait_ge(bank_free[bank_of[("sscore", lay)][0]], bank_of[("sscore", lay)][1] + 1)
                act.sem_inc(sig("ss_exp"), 1)

            attend(0)
            src = take(act, "sgate")
            act.activation(s_eg.rearrange("p h b -> p (h b)"), src[:, 0:H * NS], ACT.Exp).then_inc(sig("s_eg_ready"), 1)
            for n in range(TT):
                act.wait_ge(sig("diff_ready"), n + 1)
                act.activation(attnT, attnT, ACT.Exp).then_inc(sig("decay_exp"), 1)
                for i in range(2):
                    act.wait_ge(sig("q_scale_free"), 2 * n + i + 1)
                    free(act.activation(pair(Y, i), take(act, "gb", n, i)[:, 0:3 * P], ACT.Exp), "gb", n, i)
                    bank, before = bank_of[("gb", n, i)]
                    act.wait_ge(bank_free[bank], before + 1)
                act.sem_inc(sig("q_scale"), 1)
                act.wait_ge(sig("tok_ready"), n + 1)
                act.activation(tok_eg, tok_g, ACT.Exp)
                act.activation(tok_kd, tok_kd, ACT.Exp)
                act.activation(eglast, glast, ACT.Exp).then_inc(sig("tok_exp"), 1)
                for s in range(1, 7):
                    for i in range(2):
                        src = take(act, "Y", n, s, i)[:, 0:3 * P]
                        if s == 1:
                            act.wait_ge(sig("q_scaled"), n + 1)
                        free(act.activation(pair(Y, i), src, ACT.Copy), "Y", n, s, i)
                if n:
                    for i in range(2):
                        src = take(act, "wT", n, i)[:, 0:3 * P]
                        free(act.activation(pair(AmT, i), src, ACT.Copy, scale=-1.0), "wT", n, i)
                for i in range(2):
                    src = take(act, "vnew", n, i)[:, 0:3 * P]
                    free(act.activation(pair(Y, i), src, ACT.Copy), "vnew", n, i)
                for i in range(2):
                    src = take(act, "o", n, i)[:, 0:3 * P].rearrange("p (h t) -> p h t", h=3)
                    free(act.activation(mixT[:, 3 * i:3 * i + 3, n * P:(n + 1) * P], src, ACT.Copy), "o", n, i)
            for i in range(2):
                bank, before = bank_of[("o", TT - 1, i)]
                act.wait_ge(bank_free[bank], before + 1)
            act.wait_ge(sig("s_mixed"), 1)
            act.wait_ge(sig("S_ready"), TT)
            act.activation(sq[:, 0:H, :], mixT[:, 0:H, :], ACT.Square).then_inc(sig("o_squared"), 1)
            for h in range(H):
                free(act.activation(sq[:, h, :], take(act, "rms", h)[:, 0:NT], ACT.Sqrt, bias=eps_rms, scale=1.0 / P), "rms", h)
            for h in range(H):
                bank, before = bank_of[("rms", h)]
                act.wait_ge(bank_free[bank], before + 1)
            act.sem_inc(sig("o_root"), 1)

            def norm(lay, which, count):
                free(act.activation(mu, take(act, "ln_mean", lay, which)[:, 0:NT], ACT.Copy, scale=1.0 / D), "ln_mean", lay, which)
                bank, before = bank_of[("ln_mean", lay, which)]
                act.wait_ge(bank_free[bank], before + 1)
                act.sem_inc(sig("ln_mu"), 1)
                act.wait_ge(sig("ln_centered"), count)
                act.activation(sq, yT, ACT.Square).then_inc(sig("ln_squared"), 1)
                free(act.activation(rstd, take(act, "ln_var", lay, which)[:, 0:NT], ACT.Sqrt, bias=eps_ln, scale=1.0 / D), "ln_var", lay, which)
                bank, before = bank_of[("ln_var", lay, which)]
                act.wait_ge(bank_free[bank], before + 1)
                act.sem_inc(sig("ln_root"), 1)
                act.wait_ge(sig("ln_scaled"), count)
                for k in range(KT):
                    ins = act.activation(xT[:, k, :], yT[:, k, :], ACT.Identity, bias=ln_col[:, 2 * which + 1, lay, k:k + 1], scale=ln_col[:, 2 * which, lay, k:k + 1])
                ins.then_inc(sig("x_ready"), 1)

            norm(0, 0, 1)
            for c in range(NG):
                for f in range(4):
                    n = 4 * c + f
                    src = take(act, "gate", c, f)
                    if n >= 2:
                        act.wait_ge(sig("hid_ready"), n - 1)
                    free(act.activation(silu_t[:, f % 2, :], src[:, 0:NT], ACT.Silu), "gate", c, f)
            norm(0, 1, 2)
            mem_kv(1)
            for c in range(2 * GB):
                dst_t = uT[:, c, :] if c < GB else vT[:, c - GB, :]
                free(act.activation(dst_t, take(act, "proj", 1, c)[:, 0:NT], ACT.Gelu_apprx_tanh), "proj", 1, c)
            for c in range(GB, 2 * GB):
                bank, before = bank_of[("proj", 1, c)]
                act.wait_ge(bank_free[bank], before + 1)
            act.sem_inc(sig("uv_ready"), 1)
            attend(1)
            free(act.activation(mu, take(act, "vmean")[:, 0:NT], ACT.Copy, scale=1.0 / D_B), "vmean")
            act.wait_ge(bank_free[bank_of[("vmean",)][0]], bank_of[("vmean",)][1] + 1)
            act.sem_inc(sig("v_mu"), 1)
            act.wait_ge(sig("v_centered"), 1)
            act.wait_ge(sig("ws_read"), 1)
            act.activation(sq[:, 0:GB, :], vT, ACT.Square).then_inc(sig("v_squared"), 1)
            free(act.activation(rstd, take(act, "vvar")[:, 0:NT], ACT.Sqrt, bias=eps_ln, scale=1.0 / D_B), "vvar")
            act.wait_ge(bank_free[bank_of[("vvar",)][0]], bank_of[("vvar",)][1] + 1)
            act.sem_inc(sig("v_root"), 1)
            act.wait_ge(sig("v_scaled"), 1)
            for k in range(GB):
                ins = act.activation(vT[:, k, :], vT[:, k, :], ACT.Identity, bias=bln_b[:, k:k + 1], scale=bln_g[:, k:k + 1])
            ins.then_inc(sig("v_ready"), 1)
            norm(1, 0, 3)
            act.wait_ge(sig("mixer1_done"), 1)
            act.dma_start(ln_bc[:, 0, :], a["ln2_g"][DEPTH - 1].partition_broadcast(P)).then_inc(sig("ln_bc_landed"), 16)
            act.dma_start(ln_bc[:, 1, :], a["ln2_b"][DEPTH - 1].partition_broadcast(P)).then_inc(sig("ln_bc_landed"), 16)
            act.wait_ge(sig("zeros_ready"), 1)
            act.dma_start(xy.rearrange("(p r) d -> p r d", p=P), zeros.unsqueeze(1).to_broadcast([P, NE * CAP // P, D])).then_inc(sig("fill_done"), 16)
            act.wait_ge(sig("top_diff"), 1)
            act.activation(dtop, dtop, ACT.Exp).then_inc(sig("top_exp"), 1)

            def expert(t, then=None):
                for c in range(NG):
                    prev = t * NG + (NG if c == 0 else NG - 1 if c == 1 else NG + c - 1)
                    act.wait_ge(sig("gu_done"), t * NG + (c + 1))
                    act.wait_ge(sig("h_ready"), prev)
                    act.activation(hsil[:, c % 2, :], ps[:, c % 2, :], ACT.Silu).then_inc(sig("silu_ready"), 1)
                    if c:
                        hidden_T(t, c - 1)
                    if c == 1 and then:
                        then()
                hidden_T(t, NG - 1)

            def hidden_T(t, c):
                act.wait_ge(sig("T_done"), t * (NG + 2) + (c + 3))
                act.activation(hTe[:, c % 2].rearrange("p f s -> p (f s)"), ps[:, 4 + c % 2, :], ACT.Copy).then_inc(sig("hT_ready"), 1)

            def load_x(e, chunk, done):
                act.wait_ge(sig("xe_read"), done)
                act.dma_start(Xe, xy[bass.ds(e * CAP + chunk * P, P), :]).then_inc(sig("xe_landed"), 16)

            def store_y(e, chunk, t):
                act.wait_ge(sig("y_copied"), t + 2)
                act.dma_start(xy[bass.ds(e * CAP + chunk * P, P), :], yout).then_inc(sig("y_stored"), 16)

            act.wait_ge(sig("rows_sorted"), 1)
            load_x(0, 0, 1)
            with act.Fori(0, NE - 1) as e:
                expert(e, lambda: load_x(e + 1, 0, e + 2))
                store_y(e, 0, e)
            expert(NE - 1)
            store_y(NE - 1, 0, NE - 1)
            for chunk in (1, 2):
                with act.Fori(0, NE) as e:
                    n_tok = act.value_load(counts[0:1, bass.ds(e, 1)], min_val=0, max_val=NT)
                    t = act.value_load(turn[0:1, bass.ds(e + (chunk - 1) * NE, 1)], min_val=NE, max_val=3 * NE)
                    with act.If(n_tok > chunk * P):
                        load_x(e, chunk, t + 1)
                        expert(t)
                        store_y(e, chunk, t)
            for tt in range(3):
                np_ = P if tt < 2 else NS
                act.wait_ge(sig("fin_var"), tt + 1)
                act.activation(rs1[0:np_, :], mv[0:np_, 1:2], ACT.Sqrt, bias=eps_ln[0:np_, :]).then_inc(sig("fin_root"), 1)
                act.wait_ge(sig("fin_ready"), tt + 1)
                dstp = out["y_prompt"][0, tt * P:(tt + 1) * P, :] if tt < 2 else out["y_sample"].rearrange("b t d -> (b t) d")
                act.dma_start(dstp, acc[0:np_, :]).then_inc(sig("y_out"), 16)

        @block.vector
        def _(dve):
            step = Chain(dve, "dve_step")

            def tt_(o, x0, x1, op):
                return dve.tensor_tensor(o, x0, x1, op)

            def settle(name, *uses):
                for u in uses:
                    bank, before = bank_of[u]
                    dve.wait_ge(bank_free[bank], before + 1)
                dve.sem_inc(sig(name), 1)

            free(dve.tensor_copy(pcol1, take(dve, "params", 0)[:, 0:85]), "params", 0)
            free(dve.tensor_copy(pcol2, take(dve, "params", 1)[:, 0:64]), "params", 1)
            settle("params_in", ("params", 0), ("params", 1))
            for n in range(2 * TT):
                tt, kg = divmod(n, 2)
                src = take(dve, "x", n).rearrange("p (k t) -> p k t", k=4)
                free(dve.tensor_copy(xT[:, 4 * kg:4 * kg + 4, tt * P:(tt + 1) * P], src), "x", n)
            free(dve.tensor_copy(xT[:, :, SEQ:NT], take(dve, "xs")[:, 0:KT * NS].rearrange("p (k t) -> p k t", k=KT)), "xs")
            settle("x_in", *[("x", n) for n in range(2 * TT)], ("xs",))
            dve.sem_inc(sig("xrows_read"), 1)

            def mem_rows(lay):
                for n in range(2 * MT):
                    tt, kg = divmod(n, 2)
                    src = take(dve, "mem", lay, n).rearrange("p (k t) -> p k t", k=4)
                    free(dve.tensor_copy(memT[:, 4 * kg:4 * kg + 4, tt * P:(tt + 1) * P], src), "mem", lay, n)
                settle("mem_in", *[("mem", lay, n) for n in range(2 * MT)])
                dve.sem_inc(sig("mem_read"), 1)
                free(dve.tensor_copy(kT.rearrange("p a b -> p (a b)"), take(dve, "kT", lay)), "kT", lay)
                settle("kT_ready", ("kT", lay))

            mem_rows(0)
            hs4 = hs.rearrange("p c (b j) -> p c b j", j=CW)
            for n in range(5):
                nt_ = min(4, CT - 4 * n)
                src = take(dve, "hist", n)[:, 0:nt_ * NS * PADT].rearrange("p (c b j) -> p c b j", c=nt_, b=NS)
                for q in range(nt_):
                    ins = dve.tensor_copy(hs4[:, 4 * n + q, :, 0:PADT], src[:, q])
                free(ins, "hist", n)
            settle("hist_done", *[("hist", n) for n in range(5)])
            for c in range(CT):
                dve.wait_ge(sig("conv_begun"), c + 1)
                for j in range(1, CW):
                    ins = dve.scalar_tensor_tensor(qkv[:, c, 0:SEQ], pre[:, c, j:j + SEQ], conv_col[:, j, c:c + 1], qkv[:, c, 0:SEQ], ALU.mult, ALU.add)
                    if j < CW - 1:
                        step(ins)
                ins.then_inc(sig("conv_sum"), 1)
            step(dve.tensor_copy(hs4[:, :, :, PADT], pre[:, :, PADT + SEQ:]))
            scr = mixT.rearrange("p a b -> p (a b)")[:, 1400:1400 + CT * NS].rearrange("p (c b) -> p c b", c=CT)
            smp = qkv[:, :, SEQ:]
            for j in range(CW):
                w = conv_col[:, j, :].unsqueeze(2).to_broadcast([P, CT, NS])
                step(tt_(smp if j == 0 else scr, hs4[:, :, :, j], w, ALU.mult))
                if j:
                    step(tt_(smp, smp, scr, ALU.add))
            dve.sem_inc(sig("conv_sample"), 1)
            dve.wait_ge(sig("gpar_landed"), 32)
            step(free(dve.tensor_scalar(gate_a, take(dve, "projx", 0, "a")[0:H, 0:NT], gpar[0:H, 1:2], None, ALU.add), "projx", 0, "a")
                 if False else dve.tensor_scalar(gate_a, take(dve, "projx", 0, "a")[0:H, 0:NT], gpar[0:H, 1:2], None, ALU.add))
            free(dve.scalar_tensor_tensor(gate_n, gate_a, -1.0, gate_a, ALU.mult, ALU.min), "projx", 0, "a")
            settle("gate_abs", ("projx", 0, "a"))
            dve.wait_ge(sig("gate_log"), 2)
            step(dve.scalar_tensor_tensor(gate_g, gate_a, 0.0, gate_l, ALU.max, ALU.add))
            step(dve.tensor_scalar(gate_g, gate_g, gpar[0:H, 2:3], -1.0, ALU.mult, ALU.mult))
            for n in range(TT):
                dve.tensor_tensor_scan(gc[0:H, n * P:(n + 1) * P], ones[0:H, :], gate_g[:, n * P:(n + 1) * P], 0.0, ALU.mult, ALU.add)
            step(dve.tensor_copy(gc[0:H, SEQ:], gate_g[:, SEQ:]))
            dve.wait_ge(sig("beta_exp"), 1)
            step(dve.tensor_scalar(beta[0:H, :], beta[0:H, :], 1.0, None, ALU.add))
            step(dve.reciprocal(beta[0:H, :], beta[0:H, :]))
            dve.sem_inc(sig("gates_ready"), 1)
            for i in range(2):
                free(dve.tensor_copy(xq[:, i, :], take(dve, "projx", 0, i)[:, 0:NT]), "projx", 0, i)
            settle("xq_ready", ("projx", 0, 0), ("projx", 0, 1))
            nr = PADT + NS
            for n in range(5):
                nt_ = min(4, CT - 4 * n)
                free(dve.tensor_copy(tails[0:nr, 4 * n * P:(4 * n + nt_) * P], take(dve, "tail", n)[0:nr, 0:nt_ * P]), "tail", n)
            settle("tails_ready", *[("tail", n) for n in range(5)])
            for half in range(2):
                dve.wait_ge(sig("qk_root"), half + 1)
                step(dve.reciprocal(sq[:, 0:H, :], sq[:, 0:H, :]))
                v = qkv[:, H * half:H * half + H, :]
                step(dve.scalar_tensor_tensor(v.rearrange("p a b -> p (a b)"), v.rearrange("p a b -> p (a b)"), P ** -0.5 if half == 0 else 1.0,
                                              sq[:, 0:H, :].rearrange("p a b -> p (a b)"), ALU.mult, ALU.mult))
                dve.sem_inc(sig("qk_normed"), 1)

            def attend(lay):
                for h in range(HX):
                    src = take(dve, "score", lay, h).rearrange("p (t m) -> p t m", t=TT)
                    step(dve.tensor_reduce(attn_max[:, TT * h:TT * h + TT], src, AX_X, ALU.max))
                    dve.tensor_scalar(attn_max[:, TT * h:TT * h + TT], attn_max[:, TT * h:TT * h + TT], -DH ** -0.5, None, ALU.mult).then_inc(sig("attn_max_ready"), 1)
                dve.wait_ge(sig("attn_exp"), lay + 1)
                step(dve.reciprocal(attn_sum, attn_sum))
                step(tt_(p_att, p_att, attn_sum.unsqueeze(2).to_broadcast([P, 2 * HX, MEM]), ALU.mult))
                dve.sem_inc(sig("attn_p"), 1)
                step(dve.memset(qpad, 0.0))
                for h in range(HX):
                    r = slice(DH * (h % 2), DH * (h % 2) + DH)
                    q0 = y0 + 1600 + (h // 2) * NS * 4 * NS
                    diag = sb[r, q0 + h:q0 + h + 36 * (NS - 1) + 1:36]
                    ins = dve.tensor_copy(diag, xq[r, h // 2, SEQ:NT])
                step(ins)
                dve.sem_inc(sig("qpad_ready"), 1)
                for n in range(2):
                    free(dve.tensor_copy(mixT[:, 6 + n, 0:SEQ], take(dve, "pv", lay, n)[:, 0:SEQ]), "pv", lay, n)
                r = slice(0, 4 * NS)
                src = take(dve, "sscore", lay)
                step(dve.tensor_reduce(attn_max[r, 0:1], src[r, 0:MEM], AX_X, ALU.max))
                step(dve.tensor_scalar(attn_max[r, 0:1], attn_max[r, 0:1], -DH ** -0.5, None, ALU.mult))
                dve.sem_inc(sig("ss_max"), 1)
                dve.wait_ge(sig("ss_exp"), lay + 1)
                step(dve.reciprocal(attn_sum[r, 0:1], attn_sum[r, 0:1]))
                step(dve.tensor_scalar(ps_att[r, :], ps_att[r, :], attn_sum[r, 0:1], None, ALU.mult))
                dve.sem_inc(sig("ss_p"), 1)
                free(dve.tensor_copy(pTs.rearrange("p a b -> p (a b)"), take(dve, "spT", lay)[:, 0:MT * 4 * NS]), "spT", lay)
                settle("ss_pT", ("spT", lay))
                src = take(dve, "spv", lay)[:, 0:XT_ * NS * 4].rearrange("p (k b h) -> p k b h", k=XT_, h=4)
                for h in range(HX):
                    r = slice(DH * (h % 2), DH * (h % 2) + DH)
                    ins = dve.tensor_copy(mixT[r, 6 + h // 2, SEQ:NT], src[r, h // 2, :, h])
                free(ins, "spv", lay)
                settle("attn_done", ("spv", lay), ("pv", lay, 0), ("pv", lay, 1))

            attend(0)
            q_s, k_s, v_s = (qkv[:, H * i:H * i + H, SEQ:] for i in range(3))
            src = take(dve, "sgate")
            dve.wait_ge(sig("s_eg_ready"), 1)
            free(dve.tensor_copy(s_be, src[:, H * NS:2 * H * NS].rearrange("p (h b) -> p h b", h=H)), "sgate")
            step(tt_(s_kq, q_s, k_s, ALU.mult))
            dve.sem_inc(sig("s_prod"), 1)
            rd = take(dve, "sread")[:, 0:2 * H * NS].rearrange("p (h b r) -> p h b r", h=H, r=2)
            step(tt_(s_sk, rd[:, :, :, 1], s_eg, ALU.mult))
            step(free(tt_(s_o, rd[:, :, :, 0], s_eg, ALU.mult), "sread") if False else tt_(s_o, rd[:, :, :, 0], s_eg, ALU.mult))
            step(tt_(s_u, v_s, s_sk, ALU.subtract))
            step(tt_(s_u, s_u, s_be, ALU.mult))
            dot = take(dve, "sdot")[:, 0:H * NS].rearrange("p (h b) -> p h b", h=H)
            step(tt_(s_sk, dot, s_u, ALU.mult))
            free(tt_(mixT[:, 0:H, SEQ:], s_o, s_sk, ALU.add), "sread")
            settle("s_mixed", ("sread",))
            dve.sem_inc(sig("s_u_ready"), 1)
            bank, before = bank_of[("sdot",)]
            dve.sem_inc(bank_free[bank], 1)
            for n in range(2):
                free(dve.tensor_copy(krow[0:NS, 3 * n:3 * n + 3, :].rearrange("p a b -> p (a b)"), take(dve, "krow", n)[0:NS, 0:3 * P]), "krow", n)
            for n in range(2):
                free(dve.tensor_copy(urow[0:NS, 3 * n:3 * n + 3, :].rearrange("p a b -> p (a b)"), take(dve, "urow", n)[0:NS, 0:3 * P]), "urow", n)
            settle("s_rows", ("krow", 0), ("krow", 1), ("urow", 0), ("urow", 1))
            st = state.rearrange("p (b h) v -> p b h v", h=H)
            for h in range(H):
                dve.wait_ge(sig("state_decayed"), h + 1)
                for n in range(2):
                    half = st[:, 4 * n:4 * n + 4, h, :]
                    free(tt_(half, half, take(dve, "outer", h, n).rearrange("p (b v) -> p b v", b=4), ALU.add), "outer", h, n)
                settle("state_new", ("outer", h, 0), ("outer", h, 1))
            for n in range(TT):
                chunk = slice(n * P, (n + 1) * P)
                src = take(dve, "gcol", n)
                dve.tensor_copy(tok_g, src[:, 0:H])
                free(dve.tensor_copy(tok_b, src[:, H:2 * H]), "gcol", n)
                for i in range(2):
                    gbp = take(dve, "gb", n, i)[:, 0:3 * P].rearrange("p (h t) -> p h t", h=3)
                    dve.tensor_copy(glast[:, 3 * i:3 * i + 3], gbp[:, :, P - 1])
                bank, before = bank_of[("gcol", n)]
                dve.wait_ge(bank_free[bank], before + 1)
                for i in range(2):
                    gbp = take(dve, "gb", n, i)[:, 0:3 * P].rearrange("p (h t) -> p h t", h=3)
                    for h in range(3):
                        ins = dve.tensor_scalar(attnT[:, 3 * i + h, :], gbp[:, h, :], tok_g[:, 3 * i + h:3 * i + h + 1], 0.0, ALU.subtract, ALU.min)
                step(ins)
                dve.sem_inc(sig("diff_ready"), 1)
                dve.sem_inc(sig("q_scale_free"), 2)
                step(tt_(tok_kd, glast, tok_g, ALU.subtract))
                dve.sem_inc(sig("tok_ready"), 1)
                dve.wait_ge(sig("decay_exp"), n + 1)
                for i in range(2):
                    step(free(tt_(pair(AT, i), pair(attnT, i), take(dve, "bb", n, i)[:, 0:3 * P], ALU.mult), "bb", n, i) if False else tt_(pair(AT, i), pair(attnT, i), take(dve, "bb", n, i)[:, 0:3 * P], ALU.mult))
                    bank, before = bank_of[("bb", n, i)]
                    dve.sem_inc(bank_free[bank], 1)
                for i in range(2):
                    free(tt_(pair(AT, i), pair(AT, i), take(dve, "kk", n, i)[:, 0:3 * P], ALU.mult), "kk", n, i)
                settle("A_ready", ("kk", n, 0), ("kk", n, 1))
                step(tt_(XT, AT, stage_mask[:, 0, :].unsqueeze(1).to_broadcast([P, H, P]), ALU.mult))
                step(tt_(XT, ident.unsqueeze(1).to_broadcast([P, H, P]), XT, ALU.subtract))
                dve.sem_inc(sig("XT_ready"), 1)
                step(tt_(attnT, attnT, causalT.unsqueeze(1).to_broadcast([P, H, P]), ALU.mult))
                for i in range(2):
                    free(tt_(pair(attnT, i), pair(attnT, i), take(dve, "qk", n, i)[:, 0:3 * P], ALU.mult), "qk", n, i)
                dve.wait_ge(sig("q_scale"), n + 1)
                bank, before = bank_of[("qk", n, 1)]
                dve.wait_ge(bank_full[bank], before + 1)
                tt_(qkv[:, 0:H, chunk], qkv[:, 0:H, chunk], Y, ALU.mult).then_inc(sig("q_scaled"), 1)
                dve.wait_ge(sig("tok_exp"), n + 1)
                step(tt_(tok_beg, tok_b, tok_eg, ALU.mult))
                for i in range(2):
                    src = take(dve, "ktok", n, i)[:, 0:3 * P].rearrange("p (h t) -> p h t", h=3)
                    tt_(kdec[:, 3 * i:3 * i + 3, :], src, tok_kd[:, 3 * i:3 * i + 3].unsqueeze(2).to_broadcast([P, 3, P]), ALU.mult)
                    free(tt_(kbg[:, 3 * i:3 * i + 3, :], src, tok_beg[:, 3 * i:3 * i + 3].unsqueeze(2).to_broadcast([P, 3, P]), ALU.mult), "ktok", n, i)
                for i in range(2):
                    src = take(dve, "vtok", n, i)[:, 0:3 * P].rearrange("p (h t) -> p h t", h=3)
                    free(tt_(vb[:, 3 * i:3 * i + 3, :], src, tok_b[:, 3 * i:3 * i + 3].unsqueeze(2).to_broadcast([P, 3, P]), ALU.mult), "vtok", n, i)
                for i in range(2):
                    free(dve.tensor_copy(pair(X, i), take(dve, "xinit", n, i)[:, 0:3 * P]), "xinit", n, i)
                settle("X_ready", ("xinit", n, 0), ("xinit", n, 1))
                for s in range(1, 7):
                    if s < 6:
                        for i in range(2):
                            free(tt_(pair(X, i), pair(X, i), take(dve, "dX", n, s, i)[:, 0:3 * P], ALU.subtract), "dX", n, s, i)
                    for i in range(2):
                        free(tt_(pair(XT, i), pair(XT, i), take(dve, "dXT", n, s, i)[:, 0:3 * P], ALU.subtract), "dXT", n, s, i)
                for i in range(2):
                    src = take(dve, "S", n, i)[:, 0:3 * P]
                    if n == 0:
                        ins = free(dve.tensor_copy(pair(S, i), src), "S", n, i)
                    else:
                        for h in range(3):
                            ins = dve.scalar_tensor_tensor(S[:, 3 * i + h, :], S[:, 3 * i + h, :], eglast[:, 3 * i + h:3 * i + h + 1], src[:, h * P:(h + 1) * P], ALU.mult, ALU.add)
                        free(ins, "S", n, i)
                settle("S_ready", ("S", n, 0), ("S", n, 1))
            dve.wait_ge(sig("o_root"), 1)
            step(dve.reciprocal(sq[:, 0:H, :], sq[:, 0:H, :]))
            om = mixT[:, 0:H, :].rearrange("p a b -> p (a b)")
            step(tt_(om, om, sq[:, 0:H, :].rearrange("p a b -> p (a b)"), ALU.mult))
            step(dve.scalar_tensor_tensor(om, om, norm_w, zs.rearrange("p a b -> p (a b)"), ALU.mult, ALU.mult))
            dve.sem_inc(sig("mix_ready"), 1)

            def residual(lay):
                for c in range(KT):
                    free(dve.scalar_tensor_tensor(yT[:, c, :], xT[:, c, :], ALPHA, take(dve, "out", lay, c)[:, 0:NT], ALU.mult, ALU.add), "out", lay, c)
                settle("res_ready", *[("out", lay, c) for c in range(KT)])

            def norm(lay, count):
                dve.wait_ge(sig("ln_mu"), count)
                step(tt_(yT, yT, mu.unsqueeze(1).to_broadcast([P, KT, NT]), ALU.subtract))
                dve.sem_inc(sig("ln_centered"), 1)
                dve.wait_ge(sig("ln_root"), count)
                step(dve.reciprocal(rstd, rstd))
                step(tt_(yT, yT, rstd.unsqueeze(1).to_broadcast([P, KT, NT]), ALU.mult))
                dve.sem_inc(sig("ln_scaled"), 1)

            residual(0)
            norm(0, 1)
            for c in range(NG + 1):
                if c < NG:
                    for f in range(4):
                        bank, before = bank_of[("gate", c, f)]
                        dve.wait_ge(bank_free[bank], before + 1)
                        if f == 0 and c >= 2:
                            bank, before = bank_of[("down", c - 2, KT - 1)]
                            dve.wait_ge(bank_full[bank], before + 1)
                        free(tt_(hid[c % 2][:, f, :], silu_t[:, f % 2, :], take(dve, "up", c, f)[:, 0:NT], ALU.mult), "up", c, f)
                        bank, before = bank_of[("up", c, f)]
                        dve.wait_ge(bank_free[bank], before + 1)
                        dve.sem_inc(sig("hid_ready"), 1)
                if c:
                    for d in range(KT):
                        src = take(dve, "down", c - 1, d)[:, 0:NT]
                        if c == 1:
                            if d == 0:
                                dve.wait_ge(sig("x_ready"), 1)
                            free(dve.scalar_tensor_tensor(yT[:, d, :], xT[:, d, :], ALPHA, src, ALU.mult, ALU.add), "down", c - 1, d)
                        else:
                            free(tt_(yT[:, d, :], yT[:, d, :], src, ALU.add), "down", c - 1, d)
            settle("res_ready", *[("down", NG - 1, d) for d in range(KT)])
            norm(0, 2)
            mem_rows(1)
            for i in range(2):
                free(dve.tensor_copy(xq[:, i, :], take(dve, "projx", 1, i)[:, 0:NT]), "projx", 1, i)
            settle("xq_ready", ("projx", 1, 0), ("projx", 1, 1))
            attend(1)
            dve.wait_ge(sig("v_mu"), 1)
            step(tt_(vT, vT, mu.unsqueeze(1).to_broadcast([P, GB, NT]), ALU.subtract))
            dve.sem_inc(sig("v_centered"), 1)
            for n in range(2):
                free(tt_(wsT[:, 3 * n:3 * n + 3, :], take(dve, "wsT", n)[:, 0:3 * P].rearrange("p (g t) -> p g t", g=3), causalT.unsqueeze(1).to_broadcast([P, 3, P]), ALU.mult), "wsT", n)
            settle("ws_ready", ("wsT", 0), ("wsT", 1))
            dve.sem_inc(sig("ws_read"), 1)
            dve.wait_ge(sig("v_root"), 1)
            step(dve.reciprocal(rstd, rstd))
            step(tt_(vT, vT, rstd.unsqueeze(1).to_broadcast([P, GB, NT]), ALU.mult))
            dve.sem_inc(sig("v_scaled"), 1)
            for n in range(4):
                tt, half = divmod(n, 2)
                free(dve.tensor_copy(vtok[:, tt, 3 * P * half:3 * P * half + 3 * P], take(dve, "vtokT", n)[:, 0:3 * P]), "vtokT", n)
            for n in range(2):
                free(dve.tensor_copy(vtok[0:NS, 2, 3 * P * n:3 * P * n + 3 * P], take(dve, "vtokS", n)[0:NS, 0:3 * P]), "vtokS", n)
            settle("vtok_ready", *[("vtokT", n) for n in range(4)], ("vtokS", 0), ("vtokS", 1))
            step(free(dve.tensor_copy(rowcol, take(dve, "mixrow")[:, 0:2 * GB]), "mixrow") if False else dve.tensor_copy(rowcol, take(dve, "mixrow")[:, 0:2 * GB]))
            bank, before = bank_of[("mixrow",)]
            dve.sem_inc(bank_free[bank], 1)
            for g in range(GB):
                dve.tensor_scalar(mixT[:, g, SEQ:], vT[:, g, SEQ:], rowcol[:, g:g + 1], rowcol[:, GB + g:GB + g + 1], ALU.mult, ALU.add)
                free(tt_(mixT[:, g, 0:SEQ], take(dve, "mixed", g)[:, 0:SEQ], uT[:, g, 0:SEQ], ALU.mult), "mixed", g)
                bank, before = bank_of[("mixed", g)]
                dve.wait_ge(bank_free[bank], before + 1)
            step(tt_(mixT[:, 0:GB, SEQ:], mixT[:, 0:GB, SEQ:], uT[:, :, SEQ:], ALU.mult))
            dve.sem_inc(sig("mix_ready"), 1)
            dve.sem_inc(sig("mixer1_done"), 1)
            residual(1)
            step(dve.memset(zeros, 0.0))
            dve.sem_inc(sig("zeros_ready"), 1)
            norm(1, 3)
            for n in range(2 * TT):
                tt, kg = divmod(n, 2)
                src = take(dve, "x1tok", n)
                free(dve.tensor_copy(x1tok[:, tt, 512 * kg:512 * kg + 512], src), "x1tok", n)
                dve.wait_ge(bank_free[bank_of[("x1tok", n)][0]], bank_of[("x1tok", n)][1] + 1)
                dve.sem_inc(sig("x1tok_ready"), 1)
            for n in range(2):
                free(dve.tensor_copy(x1tok[0:NS, 2, 512 * n:512 * n + 512], take(dve, "x1tokS", n)[0:NS, :]), "x1tokS", n)
                dve.wait_ge(bank_free[bank_of[("x1tokS", n)][0]], bank_of[("x1tokS", n)][1] + 1)
                dve.sem_inc(sig("x1tok_ready"), 1)
            step(dve.memset(lg, 0.0))
            src = take(dve, "logits")[:, 0:3 * NE].rearrange("p (t e) -> p t e", t=3)
            dve.tensor_copy(lg[:, 0:2, :], src[:, 0:2, :])
            step(dve.tensor_copy(lg[0:NS, 2, :], src[0:NS, 2, :]))
            bank, before = bank_of[("logits",)]
            dve.sem_inc(bank_free[bank], 1)
            for t in range(3):
                step(dve.max(mx8[:, t, :], lg[:, t, :]))
                step(dve.max_index(idx8[:, t, :], mx8[:, t, :], lg[:, t, :]))
            step(dve.tensor_copy(idxf, idx8[:, :, :]))
            step(tt_(dtop, mx8[:, :, 1], mx8[:, :, 0], ALU.subtract))
            dve.sem_inc(sig("top_diff"), 1)
            dve.wait_ge(sig("route_consts"), 1)
            for t in range(3):
                dve.tensor_scalar(oh1[:, t, :], iota8, idxf[:, t, 0:1], valid[:, t:t + 1], ALU.is_equal, ALU.mult)
                step(dve.tensor_scalar(oh2[:, t, :], iota8, idxf[:, t, 1:2], valid[:, t:t + 1], ALU.is_equal, ALU.mult))
            step(tt_(Msel, oh1, oh2, ALU.add))
            step(tt_(Mall, Msel[:, 0, :], Msel[:, 1, :], ALU.add))
            step(tt_(Mall, Mall, Msel[:, 2, :], ALU.add))
            dve.sem_inc(sig("sel_ready"), 1)
            dve.wait_ge(sig("top_exp"), 1)
            step(dve.tensor_scalar(den, dtop, 1.0, None, ALU.add))
            step(dve.reciprocal(g1, den))
            step(tt_(g2, dtop, g1, ALU.mult))
            src = take(dve, "rank")[:, 0:4 * NE].rearrange("p (t e) -> p t e", t=4)
            dve.tensor_copy(counts[:, :], src[:, 3, :])
            for chunk in (1, 2):
                ins = dve.tensor_scalar(over[:, (chunk - 1) * NE:chunk * NE], src[:, 3, :], float(chunk * P), None, ALU.is_gt)
            step(ins)
            step(dve.tensor_tensor_scan(turns[:, 1:], ones[:, 0:2 * NE], over, float(NE), ALU.mult, ALU.add))
            step(dve.memset(turns[:, 0:1], float(NE)))
            step(dve.tensor_copy(turn[:, :], turns))
            step(tt_(rbase, src[:, 0:3, :], base8.unsqueeze(1).to_broadcast([P, 3, NE]), ALU.add))
            for k, oh in enumerate((oh1, oh2)):
                step(tt_(tmp24, oh, rbase, ALU.mult))
                step(dve.tensor_reduce(dstf[:, k, :], tmp24, AX_X, ALU.add))
            step(dve.tensor_copy(dst[:, :, :], dstf))
            dve.sem_inc(bank_free[bank_of[("rank",)][0]], 1)
            dve.sem_inc(sig("routed"), 1)
            dve.sem_inc(sig("h_ready"), NG)
            dve.sem_inc(sig("xe_evac"), 2)
            dve.sem_inc(sig("y_copied"), 1)
            dve.sem_inc(sig("y_stored"), 16)

            def expert(t):
                for n in range(2):
                    dve.wait_ge(sig("T_done"), t * (NG + 2) + (n + 1))
                    dve.tensor_copy(XeT[:, 4 * n:4 * n + 4, :].rearrange("p k s -> p (k s)"), ps[:, 4 + n, :]).then_inc(sig("xe_evac"), 1)
                for c in range(NG):
                    dve.wait_ge(sig("silu_ready"), t * NG + (c + 1))
                    if c >= 2:
                        dve.wait_ge(sig("T_done"), t * (NG + 2) + (c + 1))
                    tt_(hgu[:, c % 2, :], hsil[:, c % 2, :], ps[:, 2 + c % 2, :], ALU.mult).then_inc(sig("h_ready"), 1)
                dve.wait_ge(sig("y_done"), t + 1)
                dve.wait_ge(sig("y_stored"), t * 16 + 16)
                dve.tensor_copy(yout.rearrange("p (a b) -> p a b", a=2), ps[:, 6:8, :]).then_inc(sig("y_copied"), 1)

            with dve.Fori(0, NE) as e:
                expert(e)
            for chunk in (1, 2):
                with dve.Fori(0, NE) as e:
                    n_tok = dve.value_load(counts[0:1, bass.ds(e, 1)], min_val=0, max_val=NT)
                    t = dve.value_load(turn[0:1, bass.ds(e + (chunk - 1) * NE, 1)], min_val=NE, max_val=3 * NE)
                    with dve.If(n_tok > chunk * P):
                        expert(t)
            dve.wait_ge(sig("ln_bc_landed"), 32)
            for t in range(3):
                r = slice(0, P if t < 2 else NS)
                dve.wait_ge(sig("gathered"), 32 * (t + 1))
                if t:
                    dve.wait_ge(sig("y_out"), 16 * t)
                step(dve.tensor_scalar(acc[r, :], x1tok[r, t, :], ALPHA, None, ALU.mult))
                step(dve.scalar_tensor_tensor(acc[r, :], yk[0][r, :], g1[r, t:t + 1], acc[r, :], ALU.mult, ALU.add))
                step(dve.scalar_tensor_tensor(acc[r, :], yk[1][r, :], g2[r, t:t + 1], acc[r, :], ALU.mult, ALU.add))
                dve.sem_inc(sig("yk_read"), 1)
                for i in range(2):
                    ins = dve.bn_stats(stats[r, i, :], acc[r, 512 * i:512 * i + 512])
                step(ins)
                step(dve.bn_aggr(mv[r, :], stats[r].rearrange("p a b -> p (a b)")))
                dve.sem_inc(sig("fin_var"), 1)
                dve.wait_ge(sig("fin_root"), t + 1)
                step(dve.reciprocal(rs1[r, :], rs1[r, :]))
                step(dve.tensor_scalar(acc[r, :], acc[r, :], mv[r, 0:1], rs1[r, :], ALU.subtract, ALU.mult))
                step(tt_(acc[r, :], acc[r, :], ln_bc[r, 0, :], ALU.mult))
                step(tt_(acc[r, :], acc[r, :], ln_bc[r, 1, :], ALU.add))
                dve.sem_inc(sig("fin_ready"), 1)

        @block.tensor
        def _(pe):
            def bank(*name):
                b, before = bank_of[name]
                if before:
                    pe.wait_ge(bank_free[b], before)
                return ps[:, b, :]

            def full(ins, *name):
                ins.then_inc(bank_full[bank_of[name][0]], 1)

            def used(ins):
                ins.then_inc(slabs_used, 1)

            def tr(o, i, n=P):
                return pe.transpose(o, i, ident[0:n, 0:n])

            def mm(o, l, r, start, stop):
                return pe.matmul(o, l, r, start=start, stop=stop)

            pe.wait_ge(sig("consts"), 1)
            pe.wait_ge(sig("params_landed"), 16 * 8)
            full(tr(bank("params", 0)[:, 0:85], prow[0:85, 0, :], 85), "params", 0)
            full(tr(bank("params", 1)[:, 0:64], prow[0:64, 1, :], 64), "params", 1)
            pe.wait_ge(sig("x_landed"), 32)
            for n in range(2 * TT):
                tt, kg = divmod(n, 2)
                o = bank("x", n)
                for q in range(4):
                    ins = tr(o[:, q * P:(q + 1) * P], xrows[:, tt, (4 * kg + q) * P:(4 * kg + q + 1) * P])
                full(ins, "x", n)
            o = bank("xs")
            for k in range(KT):
                ins = tr(o[:, k * NS:(k + 1) * NS], xrows[0:NS, TT, k * P:(k + 1) * P], NS)
            full(ins, "xs")

            def mem_kv(lay):
                pe.wait_ge(sig(f"mem{lay}_landed"), 16)
                for n in range(2 * MT):
                    tt, kg = divmod(n, 2)
                    o = bank("mem", lay, n)
                    for q in range(4):
                        ins = tr(o[:, q * P:(q + 1) * P], memrows[:, tt, (4 * kg + q) * P:(4 * kg + q + 1) * P])
                    full(ins, "mem", lay, n)
                pe.wait_ge(sig("mem_in"), lay + 1)
                wait_slab(pe, ("kv", lay))
                w = as_slab(slab(("kv", lay)), KT, 2 * DX)
                for mt in range(MT):
                    o = bank("kv", lay, mt)
                    for k in range(KT):
                        ins = mm(o, memT[:, k, mt * P:(mt + 1) * P], w[:, k, :], k == 0, k == KT - 1)
                    full(ins, "kv", lay, mt)
                b, before = bank_of[("kv", lay, MT - 1)]
                pe.wait_ge(sig("kv_rows"), lay + 1)
                used(pe.nop()) if False else pe.sem_inc(slabs_used, 1)
                o = bank("kT", lay)
                for ft in range(XT_):
                    for mt in range(MT):
                        ins = tr(o[:, (ft * MT + mt) * P:(ft * MT + mt + 1) * P], kv[:, mt, ft * P:(ft + 1) * P])
                full(ins, "kT", lay)

            def project(o, w, c0, m, act_t):
                for k in range(KT):
                    ins = mm(o[0:m, 0:NT], w[:, k, c0:c0 + m], act_t[:, k, :], k == 0, k == KT - 1)
                return ins

            mem_kv(0)
            pe.wait_ge(sig("hist_landed"), 16)
            for n in range(5):
                o = bank("hist", n)
                for q in range(min(4, CT - 4 * n)):
                    ins = tr(o[:, q * 24:(q + 1) * 24], histrows[0:24, (4 * n + q) * P:(4 * n + q + 1) * P], 24)
                full(ins, "hist", n)
            pe.wait_ge(sig("x_in"), 1)
            for c in range(CT + H):
                what = ("in", 0, c // 4)
                if c % 4 == 0:
                    wait_slab(pe, what)
                ins = project(bank("proj", 0, c), as_slab(slab(what), KT, FC), (c % 4) * P, P, xT)
                full(ins, "proj", 0, c)
                if c % 4 == 3:
                    b, before = bank_of[("proj", 0, c)]
                    pe.wait_ge(bank_full[b], before + 1)
                    pe.sem_inc(slabs_used, 1)
            wait_slab(pe, ("in", 0, 6))
            w = as_slab(slab(("in", 0, 6)), KT, IN_A - 6 * FC)
            for name, c0, m in (("a", 0, H), ("b", H, H), (0, 2 * H, P), (1, 2 * H + P, P)):
                full(project(bank("projx", 0, name), w, c0, m, xT), "projx", 0, name)
            b, before = bank_of[("projx", 0, 1)]
            pe.wait_ge(bank_full[b], before + 1)
            pe.sem_inc(slabs_used, 1)
            nr = PADT + NS
            pe.wait_ge(sig("conv_begun"), CT)
            for n in range(5):
                o = bank("tail", n)
                for q in range(min(4, CT - 4 * n)):
                    ins = tr(o[0:nr, q * P:(q + 1) * P], pre[:, 4 * n + q, SEQ:SEQ + nr])
                full(ins, "tail", n)
            for c in range(2 * H):
                if c % H == 0:
                    pe.wait_ge(sig("qk_squared"), c // H + 1)
                full(mm(bank("norm", c)[:, 0:NT], ones, sq[:, c % H, :], True, True), "norm", c)

            def attend(lay):
                pe.wait_ge(sig("xq_ready"), lay + 1)
                pe.wait_ge(sig("kT_ready"), lay + 1)
                for h in range(HX):
                    r = slice(DH * (h % 2), DH * (h % 2) + DH)
                    o = bank("score", lay, h)
                    for tt in range(TT):
                        ins = mm(o[:, tt * MEM:(tt + 1) * MEM], xq[r, h // 2, tt * P:(tt + 1) * P], kT[r, h // 2, :], True, True)
                    full(ins, "score", lay, h)
                pe.wait_ge(sig("attn_p"), lay + 1)
                for h in range(HX):
                    o = bank("pT", lay, h)
                    for mt in range(MT):
                        for tt in range(TT):
                            ins = tr(o[:, mt * SEQ + tt * P:mt * SEQ + (tt + 1) * P], p_att[:, TT * h + tt, mt * P:(mt + 1) * P])
                    full(ins, "pT", lay, h)
                for n in range(2):
                    o = bank("pv", lay, n)
                    for h in (2 * n, 2 * n + 1):
                        b, before = bank_of[("pT", lay, h)]
                        pe.wait_ge(bank_free[b], before + 1)
                        r = slice(DH * (h % 2), DH * (h % 2) + DH)
                        for mt in range(MT):
                            ins = mm(o[r, 0:SEQ], kv[:, mt, DX + h * DH:DX + (h + 1) * DH], pT_att[:, h, mt, :], mt == 0, mt == MT - 1)
                    full(ins, "pv", lay, n)
                pe.wait_ge(sig("qpad_ready"), lay + 1)

                def keys(b):
                    pe.wait_ge(sig(f"k{b % 2}_landed"), 16 * (NS // 2 * lay + b // 2 + 1))
                    o = bank("cacheT", lay, b)
                    for k in range(XT_):
                        for mt in range(MT):
                            ins = tr(o[:, (k * MT + mt) * P:(k * MT + mt + 1) * P], Kc[:, b % 2, mt, k * P:(k + 1) * P])
                    full(ins, "cacheT", lay, b)

                keys(0)
                o = bank("sscore", lay)
                for b in range(NS):
                    if b + 1 < NS:
                        keys(b + 1)
                    bk, before = bank_of[("cacheT", lay, b)]
                    pe.wait_ge(bank_free[bk], before + 1)
                    for k in range(XT_):
                        last = b == NS - 1 and k == XT_ - 1
                        ins = pe.matmul(o[0:4 * NS, 0:MEM], qpad[:, k, b, :], KTs[:, b % 2, k, :], start=(b == 0 and k == 0), stop=last)
                        if k == XT_ - 1 and not last:
                            ins.then_inc(sig("sscored"), 1)
                full(ins, "sscore", lay)
                pe.wait_ge(bank_full[bank_of[("sscore", lay)][0]], bank_of[("sscore", lay)][1] + 1)
                pe.sem_inc(sig("sscored"), 1)
                pe.wait_ge(sig("ss_p"), lay + 1)
                o = bank("spT", lay)
                for mt in range(MT):
                    ins = tr(o[:, mt * 4 * NS:(mt + 1) * 4 * NS], ps_att[0:4 * NS, mt * P:(mt + 1) * P], 4 * NS)
                full(ins, "spT", lay)
                pe.wait_ge(sig("ss_pT"), lay + 1)
                pe.wait_ge(sig(f"v{lay}_landed"), 16 * NS)
                o = bank("spv", lay)
                for k in range(XT_):
                    for b in range(NS):
                        for mt in range(MT):
                            ins = mm(o[:, (k * NS + b) * 4:(k * NS + b) * 4 + 4], Vc[:, b, mt, k * P:(k + 1) * P], pTs[:, mt, 4 * b:4 * b + 4], mt == 0, mt == MT - 1)
                full(ins, "spv", lay)

            attend(0)
            pe.wait_ge(sig("gates_ready"), 1)
            pe.wait_ge(sig("qk_normed"), 2)
            o = bank("sgate")
            for i, v in enumerate((gc, beta)):
                for h in range(H):
                    ins = mm(o[:, (i * H + h) * NS:(i * H + h + 1) * NS], ident[0:H, h:h + 1].to_broadcast([H, P]), v[0:H, SEQ:NT], True, True)
            full(ins, "sgate")
            pe.wait_ge(sig("s_prod"), 1)
            full(mm(bank("sdot")[:, 0:H * NS], ones, s_kq.rearrange("p h b -> p (h b)"), True, True), "sdot")
            pe.wait_ge(sig("state_landed"), 16)
            o = bank("sread")
            for h in range(H):
                for b in range(NS):
                    n = (h * NS + b) * 2
                    ins = mm(o[:, n:n + 2], state[:, b * H + h, :], qkv[:, h:h + H + 1:H, SEQ + b], True, True)
            full(ins, "sread")
            for n in range(2):
                o = bank("krow", n)
                for q in range(3):
                    ins = tr(o[0:NS, q * P:(q + 1) * P], qkv[:, H + 3 * n + q, SEQ:NT])
                full(ins, "krow", n)
            pe.wait_ge(sig("s_u_ready"), 1)
            for n in range(2):
                o = bank("urow", n)
                for q in range(3):
                    ins = tr(o[0:NS, q * P:(q + 1) * P], s_u[:, 3 * n + q, :])
                full(ins, "urow", n)
            pe.wait_ge(sig("s_rows"), 1)
            for h in range(H):
                pe.wait_ge(sig("udiag_ready"), h + 1)
                for n in range(2):
                    full(mm(bank("outer", h, n), krow[0:NS, h, :], udiag[0:NS, h % 2, 512 * n:512 * n + 512], True, True), "outer", h, n)
            pe.wait_ge(sig("masks"), 1)
            for n in range(TT):
                chunk = slice(n * P, (n + 1) * P)
                for name, v in (("gb", gc), ("bb", beta)):
                    for i in range(2):
                        o = bank(name, n, i)
                        for q in range(3):
                            ins = mm(o[:, q * P:(q + 1) * P], ident[0:H, 3 * i + q:3 * i + q + 1].to_broadcast([H, P]), v[0:H, chunk], True, True)
                        full(ins, name, n, i)
                o = bank("gcol", n)
                tr(o[:, 0:H], gc[0:H, chunk], H)
                full(tr(o[:, H:2 * H], beta[0:H, chunk], H), "gcol", n)

                def heads(name, left, right, trans=False, more=None):
                    for i in range(2):
                        o = bank(*name, i)
                        for q in range(3):
                            h = 3 * i + q
                            oh = o[:, q * P:(q + 1) * P]
                            if trans:
                                ins = tr(oh, left(h))
                            else:
                                ins = mm(oh, left(h), right(h), True, more is None)
                                if more is not None:
                                    ins = mm(oh, more[0](h), more[1](h), False, True)
                        full(ins, *name, i)

                kT_h = lambda h: qkv[:, H + h, chunk]
                heads(("kk", n), kT_h, kT_h)
                heads(("qk", n), kT_h, lambda h: qkv[:, h, chunk])
                heads(("ktok", n), kT_h, None, True)
                heads(("vtok", n), lambda h: qkv[:, 2 * H + h, chunk], None, True)
                pe.wait_ge(sig("XT_ready"), n + 1)
                heads(("xinit", n), lambda h: XT[:, h, :], None, True)
                pe.wait_ge(sig("X_ready"), n + 1)
                for s in range(1, 7):
                    pe.wait_ge(sig("AmT_ready"), 6 * n + s)
                    if s > 1:
                        for i in range(2):
                            for nm in ("dX", "dXT"):
                                b, before = bank_of[(nm, n, s - 1, i)]
                                pe.wait_ge(bank_free[b], before + 1)
                    heads(("Y", n, s), lambda h: AmT[:, h, :], lambda h: X[:, h, :])
                    for i in range(2):
                        b, before = bank_of[("Y", n, s, i)]
                        pe.wait_ge(bank_free[b], before + 1)
                    if s < 6:
                        heads(("dX", n, s), lambda h: XT[:, h, :], lambda h: Y[:, h, :])
                    heads(("dXT", n, s), lambda h: Y[:, h, :], lambda h: XT[:, h, :])
                for i in range(2):
                    b, before = bank_of[("dXT", n, 6, i)]
                    pe.wait_ge(bank_free[b], before + 1)
                if n:
                    heads(("wT", n), lambda h: kbg[:, h, :], lambda h: XT[:, h, :])
                    for i in range(2):
                        b, before = bank_of[("wT", n, i)]
                        pe.wait_ge(bank_free[b], before + 1)
                    pe.wait_ge(sig("S_ready"), n)
                    heads(("vnew", n), lambda h: XT[:, h, :], lambda h: vb[:, h, :], more=(lambda h: AmT[:, h, :], lambda h: S[:, h, :]))
                else:
                    heads(("vnew", n), lambda h: XT[:, h, :], lambda h: vb[:, h, :])
                for i in range(2):
                    b, before = bank_of[("vnew", n, i)]
                    pe.wait_ge(bank_free[b], before + 1)
                pe.sem_inc(sig("w_done"), 1)
                heads(("o", n), lambda h: Y[:, h, :], lambda h: attnT[:, h, :],
                      more=(lambda h: S[:, h, :], lambda h: qkv[:, h, chunk]) if n else None)
                heads(("S", n), lambda h: kdec[:, h, :], lambda h: Y[:, h, :])
            pe.wait_ge(sig("o_squared"), 1)
            for h in range(H):
                full(mm(bank("rms", h)[:, 0:NT], ones, sq[:, h, :], True, True), "rms", h)

            def w_out(lay):
                pe.wait_ge(sig("mix_ready"), lay + 1)
                pe.wait_ge(sig("attn_done"), lay + 1)
                for c in range(KT):
                    what = ("out", lay, c // 4)
                    if c % 4 == 0:
                        wait_slab(pe, what)
                    full(project(bank("out", lay, c), as_slab(slab(what), KT, FC), (c % 4) * P, P, mixT), "out", lay, c)
                    if c % 4 == 3:
                        b, before = bank_of[("out", lay, c)]
                        pe.wait_ge(bank_full[b], before + 1)
                        pe.sem_inc(slabs_used, 1)

            def norm(lay, which, count):
                pe.wait_ge(sig("res_ready"), count)
                o = bank("ln_mean", lay, which)
                for k in range(KT):
                    ins = mm(o[:, 0:NT], ones, yT[:, k, :], k == 0, k == KT - 1)
                full(ins, "ln_mean", lay, which)
                pe.wait_ge(sig("ln_squared"), count)
                o = bank("ln_var", lay, which)
                for k in range(KT):
                    ins = mm(o[:, 0:NT], ones, sq[:, k, :], k == 0, k == KT - 1)
                full(ins, "ln_var", lay, which)
                pe.wait_ge(sig("x_ready"), count)

            w_out(0)
            norm(0, 0, 1)
            for c in range(NG + 1):
                if c < NG:
                    wait_slab(pe, ("gate", c))
                    wait_slab(pe, ("up", c))
                    wg, wu = (as_slab(slab((n, c)), KT, FC) for n in ("gate", "up"))
                    for f in range(4):
                        full(project(bank("gate", c, f), wg, f * P, P, xT), "gate", c, f)
                        full(project(bank("up", c, f), wu, f * P, P, xT), "up", c, f)
                    b, before = bank_of[("up", c, 3)]
                    pe.wait_ge(bank_full[b], before + 1)
                    pe.sem_inc(slabs_used, 2)
                if c:
                    wait_slab(pe, ("down", c - 1))
                    w = as_slab(slab(("down", c - 1)), 4, D)
                    pe.wait_ge(sig("hid_ready"), 4 * c)
                    for d in range(KT):
                        o = bank("down", c - 1, d)
                        for f in range(4):
                            ins = mm(o[:, 0:NT], w[:, f, d * P:(d + 1) * P], hid[(c - 1) % 2][:, f, :], f == 0, f == 3)
                        full(ins, "down", c - 1, d)
                    b, before = bank_of[("down", c - 1, KT - 1)]
                    pe.wait_ge(bank_full[b], before + 1)
                    pe.sem_inc(slabs_used, 1)
            norm(0, 1, 2)
            mem_kv(1)
            for c in range(2 * GB):
                what = ("in", 1, c // 4)
                if c % 4 == 0:
                    wait_slab(pe, what)
                full(project(bank("proj", 1, c), as_slab(slab(what), KT, FC), (c % 4) * P, P, xT), "proj", 1, c)
                if c % 4 == 3:
                    b, before = bank_of[("proj", 1, c)]
                    pe.wait_ge(bank_full[b], before + 1)
                    pe.sem_inc(slabs_used, 1)
            wait_slab(pe, ("in", 1, 3))
            w = as_slab(slab(("in", 1, 3)), KT, 2 * P)
            for i in range(2):
                full(project(bank("projx", 1, i), w, i * P, P, xT), "projx", 1, i)
            b, before = bank_of[("projx", 1, 1)]
            pe.wait_ge(bank_full[b], before + 1)
            pe.sem_inc(slabs_used, 1)
            attend(1)
            pe.wait_ge(sig("uv_ready"), 1)
            o = bank("vmean")
            for k in range(GB):
                ins = mm(o[:, 0:NT], ones, vT[:, k, :], k == 0, k == GB - 1)
            full(ins, "vmean")
            pe.wait_ge(sig("ws_landed"), 16)
            for n in range(2):
                o = bank("wsT", n)
                for q in range(3):
                    ins = tr(o[:, q * P:(q + 1) * P], wsrows[:, 3 * n + q, :])
                full(ins, "wsT", n)
            pe.wait_ge(sig("v_squared"), 1)
            o = bank("vvar")
            for k in range(GB):
                ins = mm(o[:, 0:NT], ones, sq[:, k, :], k == 0, k == GB - 1)
            full(ins, "vvar")
            pe.wait_ge(sig("v_ready"), 1)
            for n in range(4):
                tt, half = divmod(n, 2)
                o = bank("vtokT", n)
                for q in range(3):
                    ins = tr(o[:, q * P:(q + 1) * P], vT[:, 3 * half + q, tt * P:(tt + 1) * P])
                full(ins, "vtokT", n)
            for n in range(2):
                o = bank("vtokS", n)
                for q in range(3):
                    ins = tr(o[0:NS, q * P:(q + 1) * P], vT[:, 3 * n + q, SEQ:NT])
                full(ins, "vtokS", n)
            pe.wait_ge(sig("ws_ready"), 1)
            pe.wait_ge(sig("bs_landed"), 16)
            o = bank("mixrow")
            mm(o[:, 0:GB], ones[0:1, :], wsT[0:1, :, 0], True, True)
            for g in range(GB):
                ins = mm(o[:, GB + g:GB + g + 1], ident[0:GB, g:g + 1].to_broadcast([GB, P]), bsrow[0:GB, 0:1], True, True)
            full(ins, "mixrow")
            pe.wait_ge(sig("vtok_ready"), 1)
            for g in range(GB):
                o = bank("mixed", g)
                for tt in range(TT):
                    mm(o[:, tt * P:(tt + 1) * P], vtok[:, tt, g * P:(g + 1) * P], wsT[:, g, :], True, False)
                    ins = mm(o[:, tt * P:(tt + 1) * P], ident[0:GB, g:g + 1].to_broadcast([GB, P]), bsrow[0:GB, :], False, True)
                full(ins, "mixed", g)
            w_out(1)
            norm(1, 0, 3)
            pe.wait_ge(sig("mixer1_done"), 1)
            for n in range(2 * TT):
                tt, kg = divmod(n, 2)
                o = bank("x1tok", n)
                for q in range(4):
                    ins = tr(o[:, q * P:(q + 1) * P], xT[:, 4 * kg + q, tt * P:(tt + 1) * P])
                full(ins, "x1tok", n)
            for n in range(2):
                o = bank("x1tokS", n)
                for q in range(4):
                    ins = tr(o[0:NS, q * P:(q + 1) * P], xT[:, 4 * n + q, SEQ:NT])
                full(ins, "x1tokS", n)
            pe.wait_ge(sig("router_landed"), 16)
            o = bank("logits")
            for t in range(3):
                m = P if t < 2 else NS
                for k in range(KT):
                    ins = mm(o[0:m, t * NE:(t + 1) * NE], xT[:, k, t * P:t * P + m], router[:, k, :], k == 0, k == KT - 1)
            full(ins, "logits")
            pe.wait_ge(sig("sel_ready"), 1)
            o = bank("rank")
            for t in range(3):
                for u in range(t):
                    mm(o[:, t * NE:(t + 1) * NE], ones, Msel[:, u, :], u == 0, False)
                mm(o[:, t * NE:(t + 1) * NE], strictT, Msel[:, t, :], t == 0, True)
            full(mm(o[:, 3 * NE:4 * NE], ones, Mall, True, True), "rank")
            pe.wait_ge(sig("routed"), 1)
            for n in range(8):
                count = max([before for (bk, before) in bank_of.values() if bk == n]) + 1
                pe.wait_ge(bank_free[n], count)
            pe.sem_inc(sig("xe_read"), 1)
            NTU = NG + 2

            def expert(t):
                pe.wait_ge(sig("xe_landed"), t * 16 + 16)
                for n in range(2):
                    pe.wait_ge(sig("hT_ready"), t * NG + (1 + (NG if n == 0 else NG - 1)) - 1) if False else None
                    for q in range(4):
                        ins = tr(ps[:, 4 + n, q * P:(q + 1) * P], Xe[:, (4 * n + q) * P:(4 * n + q + 1) * P])
                    ins.then_inc(sig("T_done"), 1)
                order = expert_order()

                def landed_wait(kind, c):
                    j = order.index((kind, c))
                    slot = EXPERT_SLOTS[j % SLOTS]
                    pe.wait_ge(landed[slot], t * 48 + 16 * (slot_landed[slot] + j // SLOTS + 1))
                    return ring[slot]

                pe.wait_ge(sig("xe_evac"), t * 2 + 4)
                pe.sem_inc(sig("xe_read"), 1)
                for c in range(NG + 1):
                    if c < NG:
                        prev = NG if c == 0 else NG - 1 if c == 1 else NG + c - 1
                        pe.wait_ge(sig("h_ready"), t * NG + prev)
                        for kind, b in (("gate", c % 2), ("up", 2 + c % 2)):
                            w = as_slab(landed_wait(kind, c), KT, FC)
                            for k in range(KT):
                                ins = mm(ps[:, b, :], XeT[:, k, :], w[:, k, :], k == 0, k == KT - 1)
                        ins.then_inc(sig("gu_done"), 1)
                        pe.wait_ge(sig("gu_done"), t * NG + (c + 1))
                        pe.sem_inc(slabs_used, 2)
                    if c:
                        c1 = c - 1
                        pe.wait_ge(sig("h_ready"), t * NG + (NG + c1 + 1))
                        if c1 >= 2:
                            pe.wait_ge(sig("hT_ready"), t * NG + (c1 - 1))
                        for q in range(4):
                            ins = tr(ps[:, 4 + c1 % 2, q * P:(q + 1) * P], hgu[:, c1 % 2, q * P:(q + 1) * P])
                        ins.then_inc(sig("T_done"), 1)
                        pe.wait_ge(sig("hT_ready"), t * NG + (c1 + 1))
                        if c1 == 0:
                            pe.wait_ge(sig("y_copied"), t + 1)
                        w = as_slab(landed_wait("down", c1), 4, D)
                        for q in range(4):
                            for half in range(2):
                                ins = mm(ps[:, 6 + half, :], hTe[:, c1 % 2, q, :], w[:, q, 512 * half:512 * half + 512], c1 == 0 and q == 0, c1 == NG - 1 and q == 3)
                        ins.then_inc(sig("down_done"), 1)
                        pe.wait_ge(sig("down_done"), t * NG + (c1 + 1))
                        pe.sem_inc(slabs_used, 1)
                pe.sem_inc(sig("y_done"), 1)

            with pe.Fori(0, NE) as e:
                expert(e)
            for chunk in (1, 2):
                with pe.Fori(0, NE) as e:
                    n_tok = pe.value_load(counts[0:1, bass.ds(e, 1)], min_val=0, max_val=NT)
                    t = pe.value_load(turn[0:1, bass.ds(e + (chunk - 1) * NE, 1)], min_val=NE, max_val=3 * NE)
                    with pe.If(n_tok > chunk * P):
                        expert(t)


_INS = ["x_prompt", "x_sample", "state_gdn", "state_conv", "cache_mem_k", "cache_mem_v", "mem_prompt",
        "a_w_in", "a_conv_w", "a_A_log", "a_dt_bias", "a_norm_w", "b_w_in", "b_ln_g", "b_ln_b", "b_w_s",
        "b_b_s", "w_mem_kv", "w_out", "ln1_g", "ln1_b", "ln2_g", "ln2_b", "ffn_w_gu", "ffn_w_down",
        "moe_router", "moe_w_gu", "moe_w_down"]
_OUTS = {
    "y_prompt": (1, SEQ, D), "y_sample": (NS, 1, D), "p_state_gdn": (1, 1, H, P, P),
    "p_state_conv": (1, 1, PADT, CONV), "p_cache_mem_k": (DEPTH, 1, MEM, HX, DH),
    "p_cache_mem_v": (DEPTH, 1, MEM, HX, DH), "s_state_gdn": (1, NS, H, P, P),
    "s_state_conv": (1, NS, PADT, CONV), "s_sgu_v": (1, NS, 1, D_B),
}


def kernel(**inputs):
    import numpy as _np
    import concourse.bacc as _bacc
    from concourse.bass_utils import run_bass_kernel_spmd as _run

    nc = _bacc.Bacc("TRN2", target_bir_lowering=False, num_devices=1)
    arrays, a, out = {}, {}, {}
    for name in _INS:
        arrays[f"in_{name}"] = _np.ascontiguousarray(inputs[name])
        a[name] = nc.dram_tensor(f"in_{name}", arrays[f"in_{name}"].shape, F32, kind="ExternalInput").ap()
    for name, shape in _OUTS.items():
        out[name] = nc.dram_tensor(f"out_{name}", shape, F32, kind="ExternalOutput").ap()
    xy = nc.dram_tensor("sorted_rows", (NE * CAP, D), F32, kind="Internal").ap()
    hybrid_step(nc, a, out, xy)
    r = _run(nc, [arrays], core_ids=[0])
    return tuple(r.results[0][f"out_{name}"] for name in _OUTS)
```

```python
from contextlib import ExitStack

import concourse.bass as bass
from concourse import mybir

F32 = mybir.dt.float32
F32R = mybir.dt.float32r
U32 = mybir.dt.uint32
ALU = mybir.AluOpType
ACT = mybir.ActivationFunctionType
AX_X = mybir.AxisListType.X

P = 128
D = 1024
KT = D // P
SEQ = 256
NS = 8
NT = SEQ + NS
TT = SEQ // P
H = 6
CONV = 3 * H * P
CT = CONV // P
CW = 4
PADT = CW - 1
IN_A = CONV + H * P + 2 * H + 256
D_B = 768
GB = D_B // P
IN_B = 2 * D_B + 256
MEM = 256
MT = MEM // P
HX = 4
DH = 64
DX = HX * DH
XT_ = DX // P
FF = 3584
FC = 512
NG = FF // FC
NE = 8
CAP = 3 * P
DEPTH = 2
ALPHA = (2 * DEPTH) ** 0.25
LN_EPS = 1e-5
RMS_EPS = 1e-6
SLAB = KT * FC
SLOTS = 3
UNIT = SLAB // 2
HALVES = 2 * SLOTS
UNITS = 6 * NG
SPLITS = 3


class Banks:

    def __init__(self):
        self.count = [0] * 8
        self.of = {}

    def add(self, name, bank):
        assert name not in self.of
        self.of[name] = (bank, self.count[bank])
        self.count[bank] += 1


def plan_banks():
    banks = Banks()
    add = banks.add
    for n in range(2):
        add(("params", n), n)
    for n in range(2 * TT):
        add(("x", n), 2 + n)
    add(("xs",), 6)
    for lay in range(DEPTH):
        for n in range(2 * MT):
            add(("mem", lay, n), (7, 0, 1, 2)[n])
        for mt in range(MT):
            add(("kv", lay, mt), 3 + mt)
        add(("kT", lay), 5)
        if lay == 0:
            for c in range(5):
                add(("hist", c), (6, 7, 0, 1, 2)[c])
            n = 0
            for c in range(CT + H):
                add(("proj", 0, c), n % 8)
                n += 1
            for c in ("a", "b", 0, 1):
                add(("projx", 0, c), n % 8)
                n += 1
            for c in range(5):
                add(("tail", c), n % 8)
                n += 1
            for c in range(2 * H):
                add(("norm", c), n % 8)
                n += 1
        else:
            for c in range(2 * GB):
                add(("proj", 1, c), c % 8)
            for c in range(2):
                add(("projx", 1, c), 4 + c)
        for h in range(HX):
            add(("score", lay, h), h)
        for h in range(HX):
            add(("pT", lay, h), 4 + h)
        for n in range(2):
            add(("pv", lay, n), n)
        for b in range(NS):
            add(("cacheT", lay, b), 4 + b % 2)
            if b == 0:
                add(("sscore", lay), 2)
        add(("spT", lay), 3)
        add(("spv", lay), 6)
        if lay == 0:
            add(("sgate",), 7)
            add(("sdot",), 0)
            add(("sread",), 1)
            for n in range(2):
                add(("krow", n), 2 + n)
                add(("urow", n), 4 + n)
            for h in range(H):
                for n in range(2):
                    add(("outer", h, n), (6 + n) if h % 2 == 0 else n)
            for n in range(TT):
                for i in range(2):
                    add(("gb", n, i), i)
                for i in range(2):
                    add(("bb", n, i), 2 + i)
                add(("gcol", n), 4)
                for i in range(2):
                    add(("kk", n, i), 5 + i)
                for i in range(2):
                    add(("qk", n, i), (7, 0)[i])
                for i in range(2):
                    add(("ktok", n, i), 1 + i)
                for i in range(2):
                    add(("vtok", n, i), 3 + i)
                for i in range(2):
                    add(("xinit", n, i), 5 + i)
                for s in range(1, 7):
                    for i in range(2):
                        add(("Y", n, s, i), i)
                    if s < 6:
                        for i in range(2):
                            add(("dX", n, s, i), 2 + i)
                    for i in range(2):
                        add(("dXT", n, s, i), 4 + i)
                if n:
                    for i in range(2):
                        add(("wT", n, i), 6 + i)
                for i in range(2):
                    add(("vnew", n, i), i)
                for i in range(2):
                    add(("o", n, i), 2 + i)
                for i in range(2):
                    add(("S", n, i), 4 + i)
            for h in range(H):
                add(("rms", h), h)
        else:
            add(("vmean",), 7)
            for n in range(2):
                add(("wsT", n), 5 + n)
            add(("vvar",), 0)
            for n in range(4):
                add(("vtokT", n), 1 + n)
            for n in range(2):
                add(("vtokS", n), 5 + n)
            add(("mixrow",), 7)
            for g in range(GB):
                add(("mixed", g), g)
        for c in range(KT):
            add(("out", lay, c), c)
        add(("ln_mean", lay, 0), 0)
        add(("ln_var", lay, 0), 1)
        if lay == 0:
            for c in range(NG + 1):
                if c < NG:
                    for f in range(4):
                        add(("gate", c, f), 2 * (f % 2))
                        add(("up", c, f), 2 * (f % 2) + 1)
                if c:
                    for d in range(KT):
                        add(("down", c - 1, d), 4 + d % 4)
            add(("ln_mean", lay, 1), 0)
            add(("ln_var", lay, 1), 1)
    for n in range(2 * TT):
        add(("x1tok", n), 2 + n)
    for n in range(2):
        add(("x1tokS", n), 6 + n)
    add(("logits",), 0)
    add(("rank",), 1)
    return banks.of


def plan_slabs():
    mixer = [[("kv", lay)] + [("in", lay, c) for c in range(7 if lay == 0 else 4)] + [("out", lay, c) for c in range(2)]
             for lay in range(DEPTH)]
    plan, landed, n = {}, [0] * SLOTS, 0
    for lay in range(DEPTH):
        last = {}
        for j, what in enumerate(mixer[lay]):
            slot = j % SLOTS if lay == 0 else (1, 2, 0)[j % SLOTS]
            landed[slot] += 1
            plan[what] = (n, slot, landed[slot], last.get(slot))
            last[slot] = n
            n += 1
    return plan


def unit_order():
    order = []
    for c in range(NG + 1):
        if c < NG:
            order += [("gate", c, 0), ("up", c, 0), ("gate", c, 1), ("up", c, 1)]
        if c:
            order += [("down", c - 1, 0), ("down", c - 1, 1)]
    return order


ORDER = unit_order()
DENSE_HALVES = (2, 3, 4, 5, 0, 1)
EXPERT_HALVES = (4, 5, 0, 1, 2, 3)


def hybrid_step(nc, a, out, xy):
    bank_of = plan_banks()
    slab_of = plan_slabs()

    with ExitStack() as ctx:
        names = {}

        def sig(name):
            if name not in names:
                names[name] = ctx.enter_context(nc.semaphore(name))
            return names[name]

        total = 53000
        sb = ctx.enter_context(nc.sbuf_tensor("sb", [P, total], F32))
        sb_base = nc.sbuf_base - 4 * total
        ps = ctx.enter_context(nc.psum_tensor("ps", [P, 8, 512], F32))
        at = [0]

        def place(*shape, base=None):
            n = 1
            for s in shape:
                n *= s
            if base is None:
                off = at[0]
                at[0] += n
            else:
                off = base
            assert off + n <= total, (off, n)
            ap = sb[:, off:off + n]
            if len(shape) == 2:
                ap = ap.rearrange("p (a b) -> p a b", a=shape[0])
            if len(shape) == 3:
                ap = ap.rearrange("p (a b c) -> p a b c", a=shape[0], b=shape[1])
            return ap

        def alias(name, *shape, base, dtype=F32):
            return nc.alloc_sbuf_tensor_at(name, [P, *shape], dtype, offset=sb_base + 4 * base)

        def place_r(name, *shape, base):
            return alias(name, *shape, base=base, dtype=F32R)

        ring = [place(SLAB) for _ in range(SLOTS)]
        lent0 = at[0]
        at[0] += 4 * SLAB
        half_slots = alias("half_slots", HALVES, UNIT, base=0)
        halves = [half_slots[:, h, :] for h in range(HALVES)]
        split_w = place_r("split_w", SPLITS, 2, UNIT, base=lent0)
        ex0 = lent0 + SPLITS * 2 * UNIT
        split_xe = place_r("split_xe", 2, KT, P, base=ex0)
        split_he = place_r("split_he", 2, 2, 4, P, base=ex0 + 2 * D)
        xT = place(KT, NT)
        mixT = place(KT, NT)
        y0 = at[0]
        yT = place(KT, NT)
        sq0 = at[0]
        sq = place(KT, NT)
        ident = place(P)
        ones = place(P)
        strictT = place(P)
        causalT = place(P)
        stage_mask = place(7, P)
        pcol1 = place(85)
        pcol2 = place(64)
        conv_col = pcol1[:, 0:CW * CT].rearrange("p (j c) -> p j c", j=CW)
        bln_g, bln_b, norm_w = pcol1[:, 72:78], pcol1[:, 78:84], pcol1[:, 84:85]
        ln_col = pcol2.rearrange("p (w l k) -> p w l k", w=4, l=DEPTH)
        gc = place(NT)
        beta = place(NT)
        gpar = place(4)
        tok_g = place(H)
        tok_b = place(H)
        tok_eg = place(H)
        tok_beg = place(H)
        tok_kd = place(H)
        glast = place(H)
        eglast = place(H)
        attn_max = place(8)
        attn_sum = place(8)
        eps_rms = place(1)
        eps_ln = place(1)
        mu = place(NT)
        rstd = place(NT)
        at[0] = -(-at[0] // 8) * 8
        arena0 = at[0]
        qkv = place(CT, NT)
        zs = place(H, NT)
        xq = place(XT_, NT)
        kv0 = at[0]
        kv = place(MT, 2 * DX)
        kT = place(XT_, MEM)
        g0 = at[0]
        attnT = place(H, P)
        AT = place(H, P)
        X = place(H, P)
        XT = place(H, P)
        kdec = place(H, P)
        S = place(H, P)
        tails = place(CONV, base=g0)
        memT = place(KT, MEM, base=g0 + CONV)
        p_att = place(2 * HX, MEM, base=g0)
        pT_att = place(HX, MT, SEQ, base=g0 + 2 * HX * MEM)
        Y = place(H, P, base=sq0)
        AmT = place(H, P, base=sq0 + H * P)
        vb = place(H, P, base=y0)
        kbg = place(H, P, base=y0 + H * P)
        memrows = place(MT, D, base=y0)
        KTs = place(2, XT_, MEM, base=y0)
        hs = place(CT, NS * CW, base=y0 + 1024)
        qpad = place(XT_, NS, 4 * NS, base=y0 + 1600)
        gate_a, gate_n, gate_e, gate_l, gate_g = (mixT[0:H, i, :] for i in range(5))
        state = place(NS * H, P, base=lent0)
        pre = place(CT, PADT + NT, base=lent0 + 6144)
        xrows = place(3, D, base=lent0 + 6144)
        prow = place(2, P, base=lent0)
        krow = place(H, P, base=lent0 + 6144)
        urow = place(H, P, base=lent0 + 6912)
        udiag = place(2, NS * P, base=lent0 + 7680)
        sv0 = lent0 + 9728
        s_eg, s_be, s_sk, s_u, s_o, s_kq = (place(H, NS, base=sv0 + 48 * i) for i in range(6))
        Kc = place(2, MT, DX, base=lent0 + 10950)
        ps_att = place(MEM, base=lent0 + 11974)
        pTs = place(MT, 4 * NS, base=lent0 + 12230 - 64 + 58)
        histrows = place(CONV, base=lent0 + 12288)
        Vc = place(NS, MT, DX, base=lent0 + 12288)
        silu_t = place(2, NT, base=arena0)
        hid_t = alias("hid_t", 2, NT, base=arena0 + 528)
        split_x = [place_r(f"x_{part}", KT, NT, base=arena0 + 1056 + KT * NT * i) for i, part in enumerate(("hi", "lo"))]
        split_h = place_r("split_h", 2, 2, 4, NT, base=arena0 + 1056 + 2 * KT * NT)
        assert 1056 + 4 * KT * NT <= CT * NT + H * NT + XT_ * NT + MT * 2 * DX + XT_ * MEM + 3 * H * P
        uT = place(GB, NT, base=arena0)
        vT = place(GB, NT, base=arena0 + 1584)
        vtok = place(3, D_B, base=arena0 + 3168)
        wsT = place(GB, P, base=arena0 + 5472)
        wsrows = place(GB, P, base=sq0)
        bsrow = place(P, base=arena0 + 12800)
        rowcol = place(2 * GB, base=arena0 + 12928)
        assert arena0 + 5472 + 768 <= kv0
        assert arena0 + 12500 <= total
        x1tok = place(3, D, base=arena0)
        Xe = place(D, base=arena0 + 3072)
        hsil = place(2, FC, base=arena0 + 5120)
        hgu = place(2, FC, base=arena0 + 6144)
        yout = place(D, base=arena0 + 8192)
        router = place(KT, NE, base=arena0 + 9216)
        r0 = arena0 + 9280
        lg, oh1, oh2, Msel, rbase = (place(3, NE, base=r0 + 24 * i) for i in range(5))
        mx8 = place(3, NE, base=r0 + 120)
        idxf = place(3, NE, base=r0 + 144)
        iota8 = place(NE, base=r0 + 168)
        base8 = place(NE, base=r0 + 176)
        valid = place(3, base=r0 + 184)
        dtop = place(3, base=r0 + 187)
        g1 = place(3, base=r0 + 190)
        g2 = place(3, base=r0 + 193)
        den = place(3, base=r0 + 196)
        dstf = place(2, 3, base=r0 + 200)
        tmp24 = place(3, NE, base=r0 + 206)
        Mall = place(NE, base=r0 + 230)
        ln_bc = place(2, D, base=arena0 + 9600)
        idx8 = ctx.enter_context(nc.sbuf_tensor("idx8", [P, 3, NE], U32))
        dst = ctx.enter_context(nc.sbuf_tensor("dst", [P, 2, 3], U32))
        counts = ctx.enter_context(nc.sbuf_tensor("counts", [P, NE], U32))
        turn = ctx.enter_context(nc.sbuf_tensor("turn", [P, 2 * NE + 1], U32))
        zeros = mixT[:, :, :].rearrange("p a b -> p (a b)")[:, 0:D]
        yk = [place(D, base=sq0), place(D, base=y0)]
        acc = place(D, base=sq0 + D)
        stats = place(2, 6, base=r0 + 240)
        mv = place(2, base=r0 + 252)
        rs1 = place(1, base=r0 + 254)
        over = place(2 * NE, base=r0 + 256)
        turns = place(2 * NE + 1, base=r0 + 272)
        assert r0 + 289 <= arena0 + 9600

        bank_full = [sig(f"bank{b}_full") for b in range(8)]
        bank_free = [sig(f"bank{b}_free") for b in range(8)]
        landed = [sig(f"slot{s}_landed") for s in range(SLOTS)]
        half_landed = [sig(f"half{h}_landed") for h in range(HALVES)]
        slabs_used = sig("slabs_used")

        def slab(what):
            return ring[slab_of[what][1]]

        def wait_slab(eng, what):
            _, slot, count, _ = slab_of[what]
            eng.wait_ge(landed[slot], 16 * count)

        def take(eng, *name):
            bank, before = bank_of[name]
            eng.wait_ge(bank_full[bank], before + 1)
            return ps[:, bank, :]

        def free(ins, *name):
            return ins.then_inc(bank_free[bank_of[name][0]], 1)

        def pair(name, i):
            return name[:, 3 * i:3 * i + 3, :].rearrange("p a b -> p (a b)")

        def wait_unit_used(eng, u):
            bank, before = bank_of[unit_bank(u)]
            eng.wait_ge(bank_full[bank], before + 1)

        def unit_bank(u):
            kind, c, i = ORDER[u]
            return (kind, c, 2 * i + 1) if kind != "down" else (kind, c, 4 * i + 3)

        class Chain:

            def __init__(self, eng, name):
                self.eng, self.sem, self.n = eng, sig(name), 0

            def __call__(self, ins):
                self.n += 1
                ins.then_inc(self.sem, 1)
                self.eng.wait_ge(self.sem, self.n)

            def settle(self, name):
                self.eng.sem_inc(sig(name), 1)

        block = ctx.enter_context(nc.Block())

        def w_in_source(what):
            kind = what[0]
            if kind == "kv":
                src = a["w_mem_kv"][what[1]]
                c0, n = 0, 2 * DX
            elif kind == "in":
                src = a["a_w_in" if what[1] == 0 else "b_w_in"][0]
                c0 = what[2] * FC
                n = min(FC, (IN_A if what[1] == 0 else IN_B) - c0)
            else:
                src = a["w_out"][what[1]]
                c0, n = what[2] * FC, FC
            return src[:, c0:c0 + n].rearrange("(k p) n -> p k n", p=P), KT, n

        def as_slab(ap, k, n):
            return ap[:, 0:k * n].rearrange("p (k n) -> p k n", k=k)

        @block.sync
        def _(sp):
            def mixer_slabs(lay):
                for what, (n, slot, count, before) in slab_of.items():
                    if what[1] != lay:
                        continue
                    if before is not None:
                        sp.wait_ge(slabs_used, before + 1)
                    elif lay:
                        sp.wait_ge(sig("unit_split"), UNITS - HALVES + 2 * [1, 2, 0].index(slot) + 2)
                    src, k, cols = w_in_source(what)
                    sp.dma_start(as_slab(ring[slot], k, cols), src).then_inc(landed[slot], 16)

            def last_use(lay, slot):
                return max(n for what, (n, sl, _, _) in slab_of.items() if what[1] == lay and sl == slot) + 1

            def load_unit(u, w_gu, w_down, half, by_rows):
                kind, c, i = ORDER[u]
                w, c0, rows, cols = (w_down, 0, FC, D) if kind == "down" else (w_gu, c * FC + (FF if kind == "up" else 0), D, FC)
                if kind == "down":
                    w = w[c * FC:(c + 1) * FC]
                if by_rows:
                    w = w[i * rows // 2:(i + 1) * rows // 2, c0:c0 + cols]
                else:
                    w = w[:, c0 + i * cols // 2:c0 + (i + 1) * cols // 2]
                k = UNIT // (cols if by_rows else cols // 2)
                sp.dma_start(as_slab(halves[half], k, UNIT // k), w.rearrange("(k p) n -> p k n", p=P)).then_inc(half_landed[half], 16)

            mixer_slabs(0)
            for u in range(UNITS):
                half = DENSE_HALVES[u % HALVES]
                if u >= HALVES:
                    sp.wait_ge(sig("unit_split"), u - HALVES + 1)
                else:
                    sp.wait_ge(slabs_used, last_use(0, half // 2))
                load_unit(u, a["ffn_w_gu"][0], a["ffn_w_down"][0], half, False)
            mixer_slabs(1)

            def expert_unit(e, t, u):
                if t is not None:
                    sp.wait_ge(sig("unit_split"), t * UNITS + (UNITS + u - HALVES + 1))
                load_unit(u, a["moe_w_gu"][0][bass.ds(e, 1)][0], a["moe_w_down"][0][bass.ds(e, 1)][0], EXPERT_HALVES[u % HALVES], True)

            for u in range(HALVES):
                sp.wait_ge(slabs_used, last_use(1, EXPERT_HALVES[u] // 2))
                expert_unit(0, None, u)
            with sp.Fori(0, NE - 1) as e:
                for u in range(HALVES, UNITS):
                    expert_unit(e, e, u)
                for u in range(HALVES):
                    expert_unit(e + 1, e + 1, u)
            for u in range(HALVES, UNITS):
                expert_unit(NE - 1, NE - 1, u)
            sp.wait_ge(sig("routed"), 1)
            for chunk in (1, 2):
                with sp.Fori(0, NE) as e:
                    n_tok = sp.value_load(counts[0:1, bass.ds(e, 1)], min_val=0, max_val=NT)
                    t = sp.value_load(turn[0:1, bass.ds(e + (chunk - 1) * NE, 1)], min_val=NE, max_val=3 * NE)
                    with sp.If(n_tok > chunk * P):
                        for u in range(UNITS):
                            expert_unit(e, t, u)
            sp.wait_ge(sig("y_out"), 16 * 3)
            for s in range(DEPTH):
                sp.wait_ge(sig(f"cache_out{s}"), 32)
            sp.wait_ge(sig("state_out"), 16)
            sp.wait_ge(sig("pstate_out"), 16)
            sp.wait_ge(sig("conv_out"), 48)
            sp.wait_ge(sig("sgu_out"), 16)

        @block.gpsimd
        def _(pool):
            step = Chain(pool, "pool_step")
            pool.memset(ident, 0.0)
            pool.memset(eps_rms, RMS_EPS)
            pool.memset(eps_ln, LN_EPS)
            step(pool.memset(ones, 1.0))
            step(pool.affine_select(out=ident, in_=ident, pattern=[[-1, P]], compare_op=ALU.not_equal, fill=1.0, base=0, channel_multiplier=1))
            pool.sem_inc(sig("consts"), 1)
            sc = a["state_conv"][0].rearrange("b j c -> (b j) c")
            pool.dma_start(histrows[0:NS * PADT, :], sc).then_inc(sig("hist_landed"), 16)
            pool.dma_start(gpar[0:H, 0:1], a["a_A_log"].rearrange("a h -> h a")).then_inc(sig("gpar_landed"), 16)
            pool.dma_start(gpar[0:H, 1:2], a["a_dt_bias"].rearrange("a h -> h a")).then_inc(sig("gpar_landed"), 16)
            pool.dma_start(out["s_state_conv"][0, :, 0:PADT - 1, :], a["state_conv"][0, :, 1:PADT, :]).then_inc(sig("conv_out"), 16)
            step(pool.affine_select(out=strictT, in_=ones, pattern=[[1, P]], compare_op=ALU.is_gt, fill=0.0, base=0, channel_multiplier=-1))
            step(pool.affine_select(out=causalT, in_=ones, pattern=[[1, P]], compare_op=ALU.is_ge, fill=0.0, base=0, channel_multiplier=-1))
            same = [ident] + [stage_mask[:, s, :] for s in range(6)] + [ones]
            for s in range(1, 7):
                b = 1 << s
                v = same[s].rearrange("p (n b) -> p n b", b=b)
                o = ones.rearrange("p (n b) -> p n b", b=b)
                step(pool.affine_select(out=v, in_=o, pattern=[[-b, P // b], [0, b]], compare_op=ALU.is_ge, fill=0.0, base=0, channel_multiplier=1))
                step(pool.affine_select(out=v, in_=v, pattern=[[b, P // b], [0, b]], compare_op=ALU.is_ge, fill=0.0, base=b - 1, channel_multiplier=-1))
            for s in range(6, -1, -1):
                lower = same[s]
                step(pool.tensor_tensor(stage_mask[:, s, :], same[s + 1], lower, ALU.subtract))
                step(pool.tensor_tensor(stage_mask[:, s, :], stage_mask[:, s, :], strictT, ALU.mult))
                if s:
                    pass
            pool.sem_inc(sig("masks"), 1)
            pool.wait_ge(sig("params_in"), 1)
            pool.dma_start(state, a["state_gdn"][0].rearrange("b h k v -> k (b h) v")).then_inc(sig("state_landed"), 16)
            pool.wait_ge(sig("x_in"), 1)
            step(pool.memset(pre[:, :, 0:PADT], 0.0))
            pool.sem_inc(sig("pre_zero"), 1)

            def values(lay):
                for b in range(NS):
                    pool.dma_start(Vc[:, b], a["cache_mem_v"][lay, b].rearrange("(t p) h d -> p t (h d)", p=P)).then_inc(sig(f"v{lay}_landed"), 16)

            def keys(lay):
                for b in range(NS):
                    if b >= 2:
                        pool.wait_ge(bank_full[bank_of[("cacheT", lay, b - 2)][0]], bank_of[("cacheT", lay, b - 2)][1] + 1)
                    pool.dma_start(Kc[:, b % 2], a["cache_mem_k"][lay, b].rearrange("(t p) h d -> p t (h d)", p=P)).then_inc(sig(f"k{b % 2}_landed"), 16)

            def kv_out(lay):
                pool.wait_ge(sig("kv_rows"), lay + 1)
                for name, c0 in (("p_cache_mem_k", 0), ("p_cache_mem_v", DX)):
                    pool.dma_start(out[name][lay, 0].rearrange("(t p) h d -> p t (h d)", p=P), kv[:, :, c0:c0 + DX]).then_inc(sig(f"cache_out{lay}"), 16)

            kv_out(0)
            pool.wait_ge(sig("hist_done"), 1)
            values(0)
            pool.wait_ge(sig("tails_ready"), 1)
            pool.dma_start(out["p_state_conv"][0, 0], tails[0:PADT, :]).then_inc(sig("conv_out"), 16)
            pool.dma_start(out["s_state_conv"][0, :, PADT - 1, :], tails[PADT:PADT + NS, :]).then_inc(sig("conv_out"), 16)
            keys(0)
            pool.wait_ge(sig("state_landed"), 16)
            pool.wait_ge(sig("s_rows"), 1)
            st = state.rearrange("p (b h) v -> p b h v", h=H)
            for h in range(H):
                if h >= 2:
                    pool.wait_ge(bank_full[bank_of[("outer", h - 2, 1)][0]], bank_of[("outer", h - 2, 1)][1] + 1)
                ud = udiag[0:NS, h % 2, :].rearrange("p (b v) -> p b v", b=NS)
                pool.tensor_tensor(ud, urow[0:NS, h, :].unsqueeze(1).to_broadcast([NS, NS, P]),
                                   ident[0:NS, 0:NS].unsqueeze(2).to_broadcast([NS, NS, P]), ALU.mult).then_inc(sig("udiag_ready"), 1)
                pool.tensor_tensor(st[:, :, h, :], st[:, :, h, :], s_eg[:, h, :].unsqueeze(2).to_broadcast([P, NS, P]), ALU.mult).then_inc(sig("state_decayed"), 1)
            pool.wait_ge(sig("state_new"), H)
            pool.dma_start(out["s_state_gdn"][0].rearrange("b h k v -> k (b h) v"), state).then_inc(sig("state_out"), 16)
            for n in range(TT):
                pool.wait_ge(sig("A_ready"), n + 1)
                for s in range(1, 7):
                    if s > 1 or n:
                        prev = ("Y", n, s - 1, 1) if s > 1 else ("Y", n - 1, 6, 1)
                        pool.wait_ge(bank_full[bank_of[prev][0]], bank_of[prev][1] + 1)
                    if s == 1 and n:
                        pool.wait_ge(sig("w_done"), n)
                    pool.tensor_tensor(AmT, AT, stage_mask[:, s, :].unsqueeze(1).to_broadcast([P, H, P]), ALU.mult).then_inc(sig("AmT_ready"), 1)
            pool.wait_ge(sig("S_ready"), TT)
            pool.dma_start(out["p_state_gdn"][0, 0].rearrange("h k v -> k h v"), S).then_inc(sig("pstate_out"), 16)
            pool.wait_ge(sig("state_out"), 16)
            pool.wait_ge(sig("attn_done"), 1)
            pool.sem_inc(sig("gdn_lent_back"), 1)
            wait_unit_used(pool, UNITS - 1)
            pool.wait_ge(sig("pstate_out"), 16)
            pool.dma_start(bsrow[0:GB, :], a["b_b_s"][0]).then_inc(sig("bs_landed"), 16)
            pool.wait_ge(sig("x_ready"), 2)
            pool.dma_start(memrows, a["mem_prompt"][0].rearrange("(t p) d -> p t d", p=P)).then_inc(sig("mem1_landed"), 16)
            pool.dma_start(wsrows, a["b_w_s"][0].rearrange("g i j -> i g j")).then_inc(sig("ws_landed"), 16)
            pool.wait_ge(sig("mem_in"), 2)
            kv_out(1)
            values(1)
            keys(1)
            pool.wait_ge(sig("vtok_ready"), 1)
            pool.dma_start(out["s_sgu_v"][0].rearrange("b t d -> (b t) d"), vtok[0:NS, 2, :]).then_inc(sig("sgu_out"), 16)
            pool.wait_ge(sig("attn_done"), 2)
            pool.sem_inc(sig("attn1_lent_back"), 1)
            pool.wait_ge(sig("mix_ready"), 2)
            pool.dma_start(router, a["moe_router"][0].rearrange("(k p) e -> p k e", p=P)).then_inc(sig("router_landed"), 16)
            pool.iota(iota8, [[1, NE]], base=0, channel_multiplier=0, allow_small_or_imprecise_dtypes=True)
            pool.iota(base8, [[CAP, NE]], base=0, channel_multiplier=0, allow_small_or_imprecise_dtypes=True)
            step(pool.memset(valid, 1.0))
            step(pool.affine_select(out=valid[:, 2:3], in_=valid[:, 2:3], pattern=[[0, 1]], compare_op=ALU.is_ge, fill=0.0, base=NS - 1, channel_multiplier=-1))
            pool.sem_inc(sig("route_consts"), 1)
            pool.wait_ge(sig("fill_done"), 16)
            pool.wait_ge(sig("routed"), 1)
            pool.wait_ge(sig("x1tok_ready"), 6)
            for tt in range(3):
                np_ = P if tt < 2 else NS
                for k in range(2):
                    pool.indirect_dma_start(out=xy[:, :], out_offset=bass.IndirectOffsetOnAxis(ap=dst[0:np_, k, tt:tt + 1], axis=0),
                                            in_=x1tok[0:np_, tt, :], in_offset=None).then_inc(sig("scattered"), 16)
            pool.wait_ge(sig("scattered"), 16 * 6)

            pool.sem_inc(sig("rows_sorted"), 1)
            pool.wait_ge(sig("routed"), 1)
            runs = pool.value_load(turn[0:1, 2 * NE:2 * NE + 1], min_val=NE, max_val=3 * NE)
            pool.wait_ge(sig("y_stored"), runs * 16 + 16)
            pool.sem_inc(sig("pool_turn"), 1)
            for tt in range(3):
                np_ = P if tt < 2 else NS
                if tt:
                    pool.wait_ge(sig("yk_read"), tt)
                for k in range(2):
                    pool.indirect_dma_start(out=yk[k][0:np_, :], out_offset=None, in_=xy[:, :],
                                            in_offset=bass.IndirectOffsetOnAxis(ap=dst[0:np_, k, tt:tt + 1], axis=0)).then_inc(sig("gathered"), 16)
                pool.wait_ge(sig("gathered"), 32 * (tt + 1))

        @block.scalar
        def _(act):
            step = Chain(act, "act_step")
            conv_rows = a["a_conv_w"][0].rearrange("j (c p) -> (j c) p", p=P)
            act.dma_start(prow[0:72, 0, :], conv_rows).then_inc(sig("params_landed"), 16)
            act.dma_start(prow[72:78, 0, :], a["b_ln_g"][0].rearrange("(k p) -> k p", p=P)).then_inc(sig("params_landed"), 16)
            act.dma_start(prow[78:84, 0, :], a["b_ln_b"][0].rearrange("(k p) -> k p", p=P)).then_inc(sig("params_landed"), 16)
            act.dma_start(prow[84:85, 0, :], a["a_norm_w"]).then_inc(sig("params_landed"), 16)
            for w, name in enumerate(("ln1_g", "ln1_b", "ln2_g", "ln2_b")):
                act.dma_start(prow[16 * w:16 * w + 16, 1, :], a[name].rearrange("l (k p) -> (l k) p", p=P)).then_inc(sig("params_landed"), 16)
            act.dma_start(xrows[:, 0:TT, :], a["x_prompt"][0].rearrange("(t p) d -> p t d", p=P)).then_inc(sig("x_landed"), 16)
            act.dma_start(xrows[0:NS, TT, :], a["x_sample"].rearrange("b t d -> (b t) d")).then_inc(sig("x_landed"), 16)
            act.dma_start(memrows, a["mem_prompt"][0].rearrange("(t p) d -> p t d", p=P)).then_inc(sig("mem0_landed"), 16)

            def mem_kv(lay):
                for mt in range(MT):
                    src = take(act, "kv", lay, mt)
                    if mt == 0 and lay:
                        act.wait_ge(sig("cache_out0"), 32)
                    ins = free(act.activation(kv[:, mt, :], src, ACT.Copy), "kv", lay, mt)
                bank, before = bank_of[("kv", lay, MT - 1)]
                act.wait_ge(bank_free[bank], before + 1)
                bank, before = bank_of[("kv", lay, 0)]
                act.wait_ge(bank_free[bank], before + 1)
                act.sem_inc(sig("kv_rows"), 1)

            mem_kv(0)
            act.wait_ge(sig("pre_zero"), 1)
            for c in range(CT):
                free(act.activation(pre[:, c, PADT:], take(act, "proj", 0, c)[:, 0:NT], ACT.Copy), "proj", 0, c)
                bank, before = bank_of[("proj", 0, c)]
                act.wait_ge(bank_free[bank], before + 1)
                act.activation(qkv[:, c, 0:SEQ], pre[:, c, 0:SEQ], ACT.Copy, scale=conv_col[:, 0, c:c + 1]).then_inc(sig("conv_begun"), 1)
            for h in range(H):
                free(act.activation(zs[:, h, :], take(act, "proj", 0, CT + h)[:, 0:NT], ACT.Silu), "proj", 0, CT + h)
            for c in range(CT):
                act.wait_ge(sig("conv_sum"), c + 1)
                act.activation(qkv[:, c, 0:SEQ], qkv[:, c, 0:SEQ], ACT.Silu).then_inc(sig("conv_silu"), 1)
            act.wait_ge(sig("conv_sample"), 1)
            act.activation(qkv[:, :, SEQ:], qkv[:, :, SEQ:], ACT.Silu).then_inc(sig("conv_silu"), 1)
            act.wait_ge(sig("gate_abs"), 1)
            step(act.activation(gate_e, gate_n, ACT.Exp))
            act.activation(gate_l, gate_e, ACT.Ln, bias=1.0).then_inc(sig("gate_log"), 1)
            act.activation(gpar[0:H, 2:3], gpar[0:H, 0:1], ACT.Exp).then_inc(sig("gate_log"), 1)
            free(act.activation(beta[0:H, :], take(act, "projx", 0, "b")[0:H, 0:NT], ACT.Exp, scale=-1.0), "projx", 0, "b")
            act.wait_ge(bank_free[bank_of[("projx", 0, "b")][0]], bank_of[("projx", 0, "b")][1] + 1)
            act.sem_inc(sig("beta_exp"), 1)
            for half in range(2):
                act.wait_ge(sig("conv_silu"), CT + 1)
                if half:
                    bank, before = bank_of[("norm", H - 1)]
                    act.wait_ge(bank_full[bank], before + 1)
                    act.wait_ge(sig("qk_normed"), 1)
                act.activation(sq[:, 0:H, :], qkv[:, H * half:H * half + H, :], ACT.Square).then_inc(sig("qk_squared"), 1)
                for h in range(H):
                    src = take(act, "norm", H * half + h)
                    free(act.activation(sq[:, h, :], src[:, 0:NT], ACT.Sqrt, bias=eps_rms), "norm", H * half + h)
                for h in range(H):
                    bank, before = bank_of[("norm", H * half + h)]
                    act.wait_ge(bank_free[bank], before + 1)
                act.sem_inc(sig("qk_root"), 1)

            def attend(lay):
                for h in range(HX):
                    act.wait_ge(sig("attn_max_ready"), HX * lay + h + 1)
                    if h == 0 and lay == 0:
                        act.wait_ge(sig("conv_out"), 48)
                    src = take(act, "score", lay, h).rearrange("p (t m) -> p t m", t=TT)
                    for tt in range(TT):
                        n = TT * h + tt
                        ins = act.activation(p_att[:, n, :], src[:, tt, :], ACT.Exp, bias=attn_max[:, n:n + 1], scale=DH ** -0.5, accum_out=attn_sum[:, n:n + 1])
                        if tt == TT - 1:
                            free(ins, "score", lay, h)
                for h in range(HX):
                    bank, before = bank_of[("score", lay, h)]
                    act.wait_ge(bank_free[bank], before + 1)
                act.sem_inc(sig("attn_exp"), 1)
                for h in range(HX):
                    free(act.activation(pT_att[:, h].rearrange("p m t -> p (m t)"), take(act, "pT", lay, h), ACT.Copy), "pT", lay, h)
                for b in range(NS):
                    src = take(act, "cacheT", lay, b)
                    if b >= 2:
                        act.wait_ge(sig("sscored"), NS * lay + b - 1)
                    free(act.activation(KTs[:, b % 2].rearrange("p k m -> p (k m)"), src, ACT.Copy), "cacheT", lay, b)
                act.wait_ge(sig("ss_max"), lay + 1)
                src = take(act, "sscore", lay)
                free(act.activation(ps_att[0:4 * NS, :], src[0:4 * NS, 0:MEM], ACT.Exp, bias=attn_max[0:4 * NS, 0:1], scale=DH ** -0.5, accum_out=attn_sum[0:4 * NS, 0:1]), "sscore", lay)
                act.wait_ge(bank_free[bank_of[("sscore", lay)][0]], bank_of[("sscore", lay)][1] + 1)
                act.sem_inc(sig("ss_exp"), 1)

            attend(0)
            src = take(act, "sgate")
            act.activation(s_eg.rearrange("p h b -> p (h b)"), src[:, 0:H * NS], ACT.Exp).then_inc(sig("s_eg_ready"), 1)
            for n in range(TT):
                act.wait_ge(sig("diff_ready"), n + 1)
                act.activation(attnT, attnT, ACT.Exp).then_inc(sig("decay_exp"), 1)
                for i in range(2):
                    free(act.activation(pair(Y, i), take(act, "gb", n, i)[:, 0:3 * P], ACT.Exp), "gb", n, i)
                    bank, before = bank_of[("gb", n, i)]
                    act.wait_ge(bank_free[bank], before + 1)
                act.sem_inc(sig("q_scale"), 1)
                act.wait_ge(sig("tok_ready"), n + 1)
                act.activation(tok_eg, tok_g, ACT.Exp)
                act.activation(tok_kd, tok_kd, ACT.Exp)
                act.activation(eglast, glast, ACT.Exp).then_inc(sig("tok_exp"), 1)
                for s in range(1, 7):
                    for i in range(2):
                        src = take(act, "Y", n, s, i)[:, 0:3 * P]
                        if s == 1:
                            act.wait_ge(sig("q_scaled"), n + 1)
                        free(act.activation(pair(Y, i), src, ACT.Copy), "Y", n, s, i)
                if n:
                    for i in range(2):
                        src = take(act, "wT", n, i)[:, 0:3 * P]
                        free(act.activation(pair(AmT, i), src, ACT.Copy, scale=-1.0), "wT", n, i)
                for i in range(2):
                    src = take(act, "vnew", n, i)[:, 0:3 * P]
                    free(act.activation(pair(Y, i), src, ACT.Copy), "vnew", n, i)
                for i in range(2):
                    src = take(act, "o", n, i)[:, 0:3 * P].rearrange("p (h t) -> p h t", h=3)
                    free(act.activation(mixT[:, 3 * i:3 * i + 3, n * P:(n + 1) * P], src, ACT.Copy), "o", n, i)
            for i in range(2):
                bank, before = bank_of[("o", TT - 1, i)]
                act.wait_ge(bank_free[bank], before + 1)
            act.wait_ge(sig("s_mixed"), 1)
            act.wait_ge(sig("S_ready"), TT)
            act.activation(sq[:, 0:H, :], mixT[:, 0:H, :], ACT.Square).then_inc(sig("o_squared"), 1)
            for h in range(H):
                free(act.activation(sq[:, h, :], take(act, "rms", h)[:, 0:NT], ACT.Sqrt, bias=eps_rms, scale=1.0 / P), "rms", h)
            for h in range(H):
                bank, before = bank_of[("rms", h)]
                act.wait_ge(bank_free[bank], before + 1)
            act.sem_inc(sig("o_root"), 1)

            def norm(lay, which, count):
                free(act.activation(mu, take(act, "ln_mean", lay, which)[:, 0:NT], ACT.Copy, scale=1.0 / D), "ln_mean", lay, which)
                bank, before = bank_of[("ln_mean", lay, which)]
                act.wait_ge(bank_free[bank], before + 1)
                act.sem_inc(sig("ln_mu"), 1)
                act.wait_ge(sig("ln_centered"), count + lay)
                act.activation(sq, yT, ACT.Square).then_inc(sig("ln_squared"), 1)
                free(act.activation(rstd, take(act, "ln_var", lay, which)[:, 0:NT], ACT.Sqrt, bias=eps_ln, scale=1.0 / D), "ln_var", lay, which)
                bank, before = bank_of[("ln_var", lay, which)]
                act.wait_ge(bank_free[bank], before + 1)
                act.sem_inc(sig("ln_root"), 1)
                act.wait_ge(sig("ln_scaled"), count + lay)
                for k in range(KT):
                    ins = act.activation(xT[:, k, :], yT[:, k, :], ACT.Identity, bias=ln_col[:, 2 * which + 1, lay, k:k + 1], scale=ln_col[:, 2 * which, lay, k:k + 1])
                ins.then_inc(sig("x_ready"), 1)

            norm(0, 0, 1)
            act.wait_ge(sig("x_ready"), 1)
            for i in range(2):
                act.activation(split_x[0][:, 4 * i:4 * i + 4, :], xT[:, 4 * i:4 * i + 4, :], ACT.Copy).then_inc(sig("x_hi"), 1)
            act.wait_ge(sig("gdn_lent_back"), 1)
            for u in range(UNITS):
                if u >= SPLITS:
                    kind, c, i = ORDER[u - SPLITS]
                    if kind == "gate":
                        for f in (2 * i, 2 * i + 1):
                            n = 4 * c + f
                            src = take(act, "gate", c, f)
                            if n >= 2:
                                act.wait_ge(sig("silu_read"), n - 1)
                            free(act.activation(silu_t[:, f % 2, :], src[:, 0:NT], ACT.Silu), "gate", c, f)
                    wait_unit_used(act, u - SPLITS)
                half = DENSE_HALVES[u % HALVES]
                act.wait_ge(half_landed[half], 16 * (u // HALVES + 1))
                act.activation(split_w[:, u % SPLITS, 0, :], halves[half], ACT.Copy).then_inc(sig("unit_hi"), 1)
            norm(0, 1, 2)
            mem_kv(1)
            for c in range(2 * GB):
                dst_t = uT[:, c, :] if c < GB else vT[:, c - GB, :]
                free(act.activation(dst_t, take(act, "proj", 1, c)[:, 0:NT], ACT.Gelu_apprx_tanh), "proj", 1, c)
            for c in range(GB, 2 * GB):
                bank, before = bank_of[("proj", 1, c)]
                act.wait_ge(bank_free[bank], before + 1)
            act.sem_inc(sig("uv_ready"), 1)
            attend(1)
            free(act.activation(mu, take(act, "vmean")[:, 0:NT], ACT.Copy, scale=1.0 / D_B), "vmean")
            act.wait_ge(bank_free[bank_of[("vmean",)][0]], bank_of[("vmean",)][1] + 1)
            act.sem_inc(sig("ln_mu"), 1)
            act.wait_ge(sig("ln_centered"), 3)
            act.wait_ge(sig("ws_ready"), 1)
            act.activation(sq[:, 0:GB, :], vT, ACT.Square).then_inc(sig("ln_squared"), 1)
            free(act.activation(rstd, take(act, "vvar")[:, 0:NT], ACT.Sqrt, bias=eps_ln, scale=1.0 / D_B), "vvar")
            act.wait_ge(bank_free[bank_of[("vvar",)][0]], bank_of[("vvar",)][1] + 1)
            act.sem_inc(sig("ln_root"), 1)
            act.wait_ge(sig("ln_scaled"), 3)
            for k in range(GB):
                ins = act.activation(vT[:, k, :], vT[:, k, :], ACT.Identity, bias=bln_b[:, k:k + 1], scale=bln_g[:, k:k + 1])
            ins.then_inc(sig("v_ready"), 1)
            norm(1, 0, 3)
            act.wait_ge(sig("mix_ready"), 2)
            act.dma_start(ln_bc[:, 0, :], a["ln2_g"][DEPTH - 1].partition_broadcast(P)).then_inc(sig("ln_bc_landed"), 16)
            act.dma_start(ln_bc[:, 1, :], a["ln2_b"][DEPTH - 1].partition_broadcast(P)).then_inc(sig("ln_bc_landed"), 16)
            act.wait_ge(sig("zeros_ready"), 1)
            act.dma_start(xy.rearrange("(p r) d -> p r d", p=P), zeros.unsqueeze(1).to_broadcast([P, NE * CAP // P, D])).then_inc(sig("fill_done"), 16)
            act.wait_ge(sig("top_diff"), 1)
            act.activation(dtop, dtop, ACT.Exp).then_inc(sig("top_exp"), 1)

            def unit_hi(t, u):
                if t is not None:
                    act.wait_ge(sig("units_used"), t * UNITS + (UNITS + u - SPLITS + 1))
                half = EXPERT_HALVES[u % HALVES]
                act.wait_ge(half_landed[half], (0 if t is None else t * 16 * NG) + 16 * (NG + u // HALVES + 1))
                act.activation(split_w[:, u % SPLITS, 0, :], halves[half], ACT.Copy).then_inc(sig("unit_hi"), 1)

            def hidden_T(t, c):
                act.wait_ge(sig("T_done"), t * (NG + 2) + (c + 3))
                act.activation(split_he[:, c % 2, 0].rearrange("p f s -> p (f s)"), ps[:, 4 + c % 2, :], ACT.Copy).then_inc(sig("hT_hi"), 1)

            def expert(t, then=None):
                for n in range(2):
                    act.wait_ge(sig("T_done"), t * (NG + 2) + (n + 1))
                    act.activation(split_xe[:, 0, 4 * n:4 * n + 4, :].rearrange("p k s -> p (k s)"), ps[:, 4 + n, :], ACT.Copy).then_inc(sig("xeT_hi"), 1)
                for u in range(SPLITS, UNITS):
                    kind, c, i = ORDER[u - SPLITS]
                    if (kind, i) == ("gate", 1):
                        act.wait_ge(sig("units_used"), t * UNITS + (UNITS + u - SPLITS + 1))
                        act.wait_ge(sig("h_ready"), t * NG + (c - 2 + NG + 1))
                        act.activation(hsil[:, c % 2, :], ps[:, c % 2, :], ACT.Silu).then_inc(sig("silu_ready"), 1)
                        if c:
                            hidden_T(t, c - 1)
                        if c == 1 and then:
                            then()
                    unit_hi(t, u)
                hidden_T(t, NG - 1)

            def load_x(e, chunk, done):
                act.wait_ge(sig("xe_read"), done)
                act.dma_start(Xe, xy[bass.ds(e * CAP + chunk * P, P), :]).then_inc(sig("xe_landed"), 16)

            def store_y(e, chunk, t):
                act.wait_ge(sig("y_copied"), t + 2)
                act.dma_start(xy[bass.ds(e * CAP + chunk * P, P), :], yout).then_inc(sig("y_stored"), 16)

            act.wait_ge(sig("attn1_lent_back"), 1)
            for u in range(SPLITS):
                unit_hi(None, u)
            act.wait_ge(sig("rows_sorted"), 1)
            load_x(0, 0, 1)
            with act.Fori(0, NE - 1) as e:
                expert(e, lambda: load_x(e + 1, 0, e + 2))
                for u in range(SPLITS):
                    unit_hi(e + 1, u)
                store_y(e, 0, e)
            expert(NE - 1)
            store_y(NE - 1, 0, NE - 1)
            for chunk in (1, 2):
                with act.Fori(0, NE) as e:
                    n_tok = act.value_load(counts[0:1, bass.ds(e, 1)], min_val=0, max_val=NT)
                    t = act.value_load(turn[0:1, bass.ds(e + (chunk - 1) * NE, 1)], min_val=NE, max_val=3 * NE)
                    with act.If(n_tok > chunk * P):
                        load_x(e, chunk, t + 1)
                        for u in range(SPLITS):
                            unit_hi(t, u)
                        expert(t)
                        store_y(e, chunk, t)
            for tt in range(3):
                np_ = P if tt < 2 else NS
                act.wait_ge(sig("fin_var"), tt + 1)
                act.activation(rs1[0:np_, :], mv[0:np_, 1:2], ACT.Sqrt, bias=eps_ln[0:np_, :]).then_inc(sig("fin_root"), 1)
                act.wait_ge(sig("fin_ready"), tt + 1)
                dstp = out["y_prompt"][0, tt * P:(tt + 1) * P, :] if tt < 2 else out["y_sample"].rearrange("b t d -> (b t) d")
                act.dma_start(dstp, acc[0:np_, :]).then_inc(sig("y_out"), 16)

        @block.vector
        def _(dve):
            step = Chain(dve, "dve_step")

            def tt_(o, x0, x1, op):
                return dve.tensor_tensor(o, x0, x1, op)

            def settle(name, *uses):
                for u in uses:
                    bank, before = bank_of[u]
                    dve.wait_ge(bank_free[bank], before + 1)
                dve.sem_inc(sig(name), 1)

            free(dve.tensor_copy(pcol1, take(dve, "params", 0)[:, 0:85]), "params", 0)
            free(dve.tensor_copy(pcol2, take(dve, "params", 1)[:, 0:64]), "params", 1)
            settle("params_in", ("params", 0), ("params", 1))
            for n in range(2 * TT):
                tt, kg = divmod(n, 2)
                src = take(dve, "x", n).rearrange("p (k t) -> p k t", k=4)
                free(dve.tensor_copy(xT[:, 4 * kg:4 * kg + 4, tt * P:(tt + 1) * P], src), "x", n)
            free(dve.tensor_copy(xT[:, :, SEQ:NT], take(dve, "xs")[:, 0:KT * NS].rearrange("p (k t) -> p k t", k=KT)), "xs")
            settle("x_in", *[("x", n) for n in range(2 * TT)], ("xs",))

            def mem_rows(lay):
                for n in range(2 * MT):
                    tt, kg = divmod(n, 2)
                    src = take(dve, "mem", lay, n).rearrange("p (k t) -> p k t", k=4)
                    free(dve.tensor_copy(memT[:, 4 * kg:4 * kg + 4, tt * P:(tt + 1) * P], src), "mem", lay, n)
                settle("mem_in", *[("mem", lay, n) for n in range(2 * MT)])
                free(dve.tensor_copy(kT.rearrange("p a b -> p (a b)"), take(dve, "kT", lay)), "kT", lay)
                settle("kT_ready", ("kT", lay))

            mem_rows(0)
            hs4 = hs.rearrange("p c (b j) -> p c b j", j=CW)
            for n in range(5):
                nt_ = min(4, CT - 4 * n)
                src = take(dve, "hist", n)[:, 0:nt_ * NS * PADT].rearrange("p (c b j) -> p c b j", c=nt_, b=NS)
                for q in range(nt_):
                    ins = dve.tensor_copy(hs4[:, 4 * n + q, :, 0:PADT], src[:, q])
                free(ins, "hist", n)
            settle("hist_done", *[("hist", n) for n in range(5)])
            for c in range(CT):
                dve.wait_ge(sig("conv_begun"), c + 1)
                for j in range(1, CW):
                    ins = dve.scalar_tensor_tensor(qkv[:, c, 0:SEQ], pre[:, c, j:j + SEQ], conv_col[:, j, c:c + 1], qkv[:, c, 0:SEQ], ALU.mult, ALU.add)
                    if j < CW - 1:
                        step(ins)
                ins.then_inc(sig("conv_sum"), 1)
            step(dve.tensor_copy(hs4[:, :, :, PADT], pre[:, :, PADT + SEQ:]))
            scr = mixT.rearrange("p a b -> p (a b)")[:, 1400:1400 + CT * NS].rearrange("p (c b) -> p c b", c=CT)
            smp = qkv[:, :, SEQ:]
            for j in range(CW):
                w = conv_col[:, j, :].unsqueeze(2).to_broadcast([P, CT, NS])
                step(tt_(smp if j == 0 else scr, hs4[:, :, :, j], w, ALU.mult))
                if j:
                    step(tt_(smp, smp, scr, ALU.add))
            dve.sem_inc(sig("conv_sample"), 1)
            dve.wait_ge(sig("gpar_landed"), 32)
            step(free(dve.tensor_scalar(gate_a, take(dve, "projx", 0, "a")[0:H, 0:NT], gpar[0:H, 1:2], None, ALU.add), "projx", 0, "a")
                 if False else dve.tensor_scalar(gate_a, take(dve, "projx", 0, "a")[0:H, 0:NT], gpar[0:H, 1:2], None, ALU.add))
            free(dve.scalar_tensor_tensor(gate_n, gate_a, -1.0, gate_a, ALU.mult, ALU.min), "projx", 0, "a")
            settle("gate_abs", ("projx", 0, "a"))
            dve.wait_ge(sig("gate_log"), 2)
            step(dve.scalar_tensor_tensor(gate_g, gate_a, 0.0, gate_l, ALU.max, ALU.add))
            step(dve.tensor_scalar(gate_g, gate_g, gpar[0:H, 2:3], -1.0, ALU.mult, ALU.mult))
            for n in range(TT):
                dve.tensor_tensor_scan(gc[0:H, n * P:(n + 1) * P], ones[0:H, :], gate_g[:, n * P:(n + 1) * P], 0.0, ALU.mult, ALU.add)
            step(dve.tensor_copy(gc[0:H, SEQ:], gate_g[:, SEQ:]))
            dve.wait_ge(sig("beta_exp"), 1)
            step(dve.tensor_scalar(beta[0:H, :], beta[0:H, :], 1.0, None, ALU.add))
            step(dve.reciprocal(beta[0:H, :], beta[0:H, :]))
            dve.sem_inc(sig("gates_ready"), 1)
            for i in range(2):
                free(dve.tensor_copy(xq[:, i, :], take(dve, "projx", 0, i)[:, 0:NT]), "projx", 0, i)
            settle("xq_ready", ("projx", 0, 0), ("projx", 0, 1))
            nr = PADT + NS
            for n in range(5):
                nt_ = min(4, CT - 4 * n)
                free(dve.tensor_copy(tails[0:nr, 4 * n * P:(4 * n + nt_) * P], take(dve, "tail", n)[0:nr, 0:nt_ * P]), "tail", n)
            settle("tails_ready", *[("tail", n) for n in range(5)])
            for half in range(2):
                dve.wait_ge(sig("qk_root"), half + 1)
                step(dve.reciprocal(sq[:, 0:H, :], sq[:, 0:H, :]))
                v = qkv[:, H * half:H * half + H, :]
                step(dve.scalar_tensor_tensor(v.rearrange("p a b -> p (a b)"), v.rearrange("p a b -> p (a b)"), P ** -0.5 if half == 0 else 1.0,
                                              sq[:, 0:H, :].rearrange("p a b -> p (a b)"), ALU.mult, ALU.mult))
                dve.sem_inc(sig("qk_normed"), 1)

            def attend(lay):
                for h in range(HX):
                    src = take(dve, "score", lay, h).rearrange("p (t m) -> p t m", t=TT)
                    step(dve.tensor_reduce(attn_max[:, TT * h:TT * h + TT], src, AX_X, ALU.max))
                    dve.tensor_scalar(attn_max[:, TT * h:TT * h + TT], attn_max[:, TT * h:TT * h + TT], -DH ** -0.5, None, ALU.mult).then_inc(sig("attn_max_ready"), 1)
                dve.wait_ge(sig("attn_exp"), lay + 1)
                step(dve.reciprocal(attn_sum, attn_sum))
                step(tt_(p_att, p_att, attn_sum.unsqueeze(2).to_broadcast([P, 2 * HX, MEM]), ALU.mult))
                dve.sem_inc(sig("attn_p"), 1)
                step(dve.memset(qpad, 0.0))
                for h in range(HX):
                    r = slice(DH * (h % 2), DH * (h % 2) + DH)
                    q0 = y0 + 1600 + (h // 2) * NS * 4 * NS
                    diag = sb[r, q0 + h:q0 + h + 36 * (NS - 1) + 1:36]
                    ins = dve.tensor_copy(diag, xq[r, h // 2, SEQ:NT])
                step(ins)
                dve.sem_inc(sig("qpad_ready"), 1)
                for n in range(2):
                    free(dve.tensor_copy(mixT[:, 6 + n, 0:SEQ], take(dve, "pv", lay, n)[:, 0:SEQ]), "pv", lay, n)
                r = slice(0, 4 * NS)
                src = take(dve, "sscore", lay)
                step(dve.tensor_reduce(attn_max[r, 0:1], src[r, 0:MEM], AX_X, ALU.max))
                step(dve.tensor_scalar(attn_max[r, 0:1], attn_max[r, 0:1], -DH ** -0.5, None, ALU.mult))
                dve.sem_inc(sig("ss_max"), 1)
                dve.wait_ge(sig("ss_exp"), lay + 1)
                step(dve.reciprocal(attn_sum[r, 0:1], attn_sum[r, 0:1]))
                step(dve.tensor_scalar(ps_att[r, :], ps_att[r, :], attn_sum[r, 0:1], None, ALU.mult))
                dve.sem_inc(sig("ss_p"), 1)
                free(dve.tensor_copy(pTs.rearrange("p a b -> p (a b)"), take(dve, "spT", lay)[:, 0:MT * 4 * NS]), "spT", lay)
                settle("ss_pT", ("spT", lay))
                src = take(dve, "spv", lay)[:, 0:XT_ * NS * 4].rearrange("p (k b h) -> p k b h", k=XT_, h=4)
                for h in range(HX):
                    r = slice(DH * (h % 2), DH * (h % 2) + DH)
                    ins = dve.tensor_copy(mixT[r, 6 + h // 2, SEQ:NT], src[r, h // 2, :, h])
                free(ins, "spv", lay)
                settle("attn_done", ("spv", lay), ("pv", lay, 0), ("pv", lay, 1))

            attend(0)
            q_s, k_s, v_s = (qkv[:, H * i:H * i + H, SEQ:] for i in range(3))
            src = take(dve, "sgate")
            dve.wait_ge(sig("s_eg_ready"), 1)
            free(dve.tensor_copy(s_be, src[:, H * NS:2 * H * NS].rearrange("p (h b) -> p h b", h=H)), "sgate")
            step(tt_(s_kq, q_s, k_s, ALU.mult))
            dve.sem_inc(sig("s_prod"), 1)
            rd = take(dve, "sread")[:, 0:2 * H * NS].rearrange("p (h b r) -> p h b r", h=H, r=2)
            step(tt_(s_sk, rd[:, :, :, 1], s_eg, ALU.mult))
            step(free(tt_(s_o, rd[:, :, :, 0], s_eg, ALU.mult), "sread") if False else tt_(s_o, rd[:, :, :, 0], s_eg, ALU.mult))
            step(tt_(s_u, v_s, s_sk, ALU.subtract))
            step(tt_(s_u, s_u, s_be, ALU.mult))
            dot = take(dve, "sdot")[:, 0:H * NS].rearrange("p (h b) -> p h b", h=H)
            step(tt_(s_sk, dot, s_u, ALU.mult))
            free(tt_(mixT[:, 0:H, SEQ:], s_o, s_sk, ALU.add), "sread")
            settle("s_mixed", ("sread",))
            bank, before = bank_of[("sdot",)]
            dve.sem_inc(bank_free[bank], 1)
            for n in range(2):
                free(dve.tensor_copy(krow[0:NS, 3 * n:3 * n + 3, :].rearrange("p a b -> p (a b)"), take(dve, "krow", n)[0:NS, 0:3 * P]), "krow", n)
            for n in range(2):
                free(dve.tensor_copy(urow[0:NS, 3 * n:3 * n + 3, :].rearrange("p a b -> p (a b)"), take(dve, "urow", n)[0:NS, 0:3 * P]), "urow", n)
            settle("s_rows", ("krow", 0), ("krow", 1), ("urow", 0), ("urow", 1))
            st = state.rearrange("p (b h) v -> p b h v", h=H)
            for h in range(H):
                dve.wait_ge(sig("state_decayed"), h + 1)
                for n in range(2):
                    half = st[:, 4 * n:4 * n + 4, h, :]
                    free(tt_(half, half, take(dve, "outer", h, n).rearrange("p (b v) -> p b v", b=4), ALU.add), "outer", h, n)
                settle("state_new", ("outer", h, 0), ("outer", h, 1))
            for n in range(TT):
                chunk = slice(n * P, (n + 1) * P)
                src = take(dve, "gcol", n)
                dve.tensor_copy(tok_g, src[:, 0:H])
                free(dve.tensor_copy(tok_b, src[:, H:2 * H]), "gcol", n)
                for i in range(2):
                    gbp = take(dve, "gb", n, i)[:, 0:3 * P].rearrange("p (h t) -> p h t", h=3)
                    dve.tensor_copy(glast[:, 3 * i:3 * i + 3], gbp[:, :, P - 1])
                bank, before = bank_of[("gcol", n)]
                dve.wait_ge(bank_free[bank], before + 1)
                for i in range(2):
                    gbp = take(dve, "gb", n, i)[:, 0:3 * P].rearrange("p (h t) -> p h t", h=3)
                    for h in range(3):
                        ins = dve.tensor_scalar(attnT[:, 3 * i + h, :], gbp[:, h, :], tok_g[:, 3 * i + h:3 * i + h + 1], 0.0, ALU.subtract, ALU.min)
                step(ins)
                dve.sem_inc(sig("diff_ready"), 1)
                step(tt_(tok_kd, glast, tok_g, ALU.subtract))
                dve.sem_inc(sig("tok_ready"), 1)
                dve.wait_ge(sig("decay_exp"), n + 1)
                for i in range(2):
                    step(free(tt_(pair(AT, i), pair(attnT, i), take(dve, "bb", n, i)[:, 0:3 * P], ALU.mult), "bb", n, i) if False else tt_(pair(AT, i), pair(attnT, i), take(dve, "bb", n, i)[:, 0:3 * P], ALU.mult))
                    bank, before = bank_of[("bb", n, i)]
                    dve.sem_inc(bank_free[bank], 1)
                for i in range(2):
                    free(tt_(pair(AT, i), pair(AT, i), take(dve, "kk", n, i)[:, 0:3 * P], ALU.mult), "kk", n, i)
                settle("A_ready", ("kk", n, 0), ("kk", n, 1))
                step(tt_(XT, AT, stage_mask[:, 0, :].unsqueeze(1).to_broadcast([P, H, P]), ALU.mult))
                step(tt_(XT, ident.unsqueeze(1).to_broadcast([P, H, P]), XT, ALU.subtract))
                dve.sem_inc(sig("XT_ready"), 1)
                step(tt_(attnT, attnT, causalT.unsqueeze(1).to_broadcast([P, H, P]), ALU.mult))
                for i in range(2):
                    free(tt_(pair(attnT, i), pair(attnT, i), take(dve, "qk", n, i)[:, 0:3 * P], ALU.mult), "qk", n, i)
                dve.wait_ge(sig("q_scale"), n + 1)
                bank, before = bank_of[("qk", n, 1)]
                dve.wait_ge(bank_full[bank], before + 1)
                tt_(qkv[:, 0:H, chunk], qkv[:, 0:H, chunk], Y, ALU.mult).then_inc(sig("q_scaled"), 1)
                dve.wait_ge(sig("tok_exp"), n + 1)
                step(tt_(tok_beg, tok_b, tok_eg, ALU.mult))
                for i in range(2):
                    src = take(dve, "ktok", n, i)[:, 0:3 * P].rearrange("p (h t) -> p h t", h=3)
                    tt_(kdec[:, 3 * i:3 * i + 3, :], src, tok_kd[:, 3 * i:3 * i + 3].unsqueeze(2).to_broadcast([P, 3, P]), ALU.mult)
                    free(tt_(kbg[:, 3 * i:3 * i + 3, :], src, tok_beg[:, 3 * i:3 * i + 3].unsqueeze(2).to_broadcast([P, 3, P]), ALU.mult), "ktok", n, i)
                for i in range(2):
                    src = take(dve, "vtok", n, i)[:, 0:3 * P].rearrange("p (h t) -> p h t", h=3)
                    free(tt_(vb[:, 3 * i:3 * i + 3, :], src, tok_b[:, 3 * i:3 * i + 3].unsqueeze(2).to_broadcast([P, 3, P]), ALU.mult), "vtok", n, i)
                for i in range(2):
                    free(dve.tensor_copy(pair(X, i), take(dve, "xinit", n, i)[:, 0:3 * P]), "xinit", n, i)
                settle("X_ready", ("xinit", n, 0), ("xinit", n, 1))
                for s in range(1, 7):
                    if s < 6:
                        for i in range(2):
                            free(tt_(pair(X, i), pair(X, i), take(dve, "dX", n, s, i)[:, 0:3 * P], ALU.subtract), "dX", n, s, i)
                    for i in range(2):
                        free(tt_(pair(XT, i), pair(XT, i), take(dve, "dXT", n, s, i)[:, 0:3 * P], ALU.subtract), "dXT", n, s, i)
                for i in range(2):
                    src = take(dve, "S", n, i)[:, 0:3 * P]
                    if n == 0:
                        ins = free(dve.tensor_copy(pair(S, i), src), "S", n, i)
                    else:
                        for h in range(3):
                            ins = dve.scalar_tensor_tensor(S[:, 3 * i + h, :], S[:, 3 * i + h, :], eglast[:, 3 * i + h:3 * i + h + 1], src[:, h * P:(h + 1) * P], ALU.mult, ALU.add)
                        free(ins, "S", n, i)
                settle("S_ready", ("S", n, 0), ("S", n, 1))
            dve.wait_ge(sig("o_root"), 1)
            step(dve.reciprocal(sq[:, 0:H, :], sq[:, 0:H, :]))
            om = mixT[:, 0:H, :].rearrange("p a b -> p (a b)")
            step(tt_(om, om, sq[:, 0:H, :].rearrange("p a b -> p (a b)"), ALU.mult))
            step(dve.scalar_tensor_tensor(om, om, norm_w, zs.rearrange("p a b -> p (a b)"), ALU.mult, ALU.mult))
            dve.sem_inc(sig("mix_ready"), 1)

            def residual(lay):
                for c in range(KT):
                    free(dve.scalar_tensor_tensor(yT[:, c, :], xT[:, c, :], ALPHA, take(dve, "out", lay, c)[:, 0:NT], ALU.mult, ALU.add), "out", lay, c)
                settle("res_ready", *[("out", lay, c) for c in range(KT)])

            def norm(lay, count):
                dve.wait_ge(sig("ln_mu"), count + lay)
                step(tt_(yT, yT, mu.unsqueeze(1).to_broadcast([P, KT, NT]), ALU.subtract))
                dve.sem_inc(sig("ln_centered"), 1)
                dve.wait_ge(sig("ln_root"), count + lay)
                step(dve.reciprocal(rstd, rstd))
                step(tt_(yT, yT, rstd.unsqueeze(1).to_broadcast([P, KT, NT]), ALU.mult))
                dve.sem_inc(sig("ln_scaled"), 1)

            residual(0)
            norm(0, 1)
            dve.wait_ge(sig("x_ready"), 1)
            for i in range(2):
                dve.wait_ge(sig("x_hi"), i + 1)
                k = slice(4 * i, 4 * i + 4)
                tt_(split_x[1][:, k, :], xT[:, k, :], split_x[0][:, k, :].bitcast(F32), ALU.subtract).then_inc(sig("x_lo"), 1)

            def after_unit(kind, c, i):
                if kind == "up":
                    for f in (2 * i, 2 * i + 1):
                        bank, before = bank_of[("gate", c, f)]
                        dve.wait_ge(bank_free[bank], before + 1)
                        if f == 0 and c >= 2:
                            wait_unit_used(dve, ORDER.index(("down", c - 2, 1)))
                        free(tt_(hid_t[:, f % 2, :], silu_t[:, f % 2, :], take(dve, "up", c, f)[:, 0:NT], ALU.mult), "up", c, f)
                        bank, before = bank_of[("up", c, f)]
                        dve.wait_ge(bank_free[bank], before + 1)
                        dve.sem_inc(sig("silu_read"), 1)
                        step(dve.tensor_copy(split_h[:, c % 2, 0, f, :], hid_t[:, f % 2, :]))
                        tt_(split_h[:, c % 2, 1, f, :], hid_t[:, f % 2, :], split_h[:, c % 2, 0, f, :].bitcast(F32), ALU.subtract).then_inc(sig("hid_ready"), 1)
                if kind == "down":
                    for d in range(4 * i, 4 * i + 4):
                        src = take(dve, "down", c, d)[:, 0:NT]
                        if c == 0:
                            free(dve.scalar_tensor_tensor(yT[:, d, :], xT[:, d, :], ALPHA, src, ALU.mult, ALU.add), "down", c, d)
                        else:
                            free(tt_(yT[:, d, :], yT[:, d, :], src, ALU.add), "down", c, d)

            for u in range(UNITS + SPLITS):
                if u >= SPLITS:
                    after_unit(*ORDER[u - SPLITS])
                if u < UNITS:
                    dve.wait_ge(sig("unit_hi"), u + 1)
                    tt_(split_w[:, u % SPLITS, 1, :], halves[DENSE_HALVES[u % HALVES]], split_w[:, u % SPLITS, 0, :].bitcast(F32), ALU.subtract).then_inc(sig("unit_split"), 1)
            settle("res_ready", *[("down", NG - 1, d) for d in range(KT)])
            norm(0, 2)
            mem_rows(1)
            for i in range(2):
                free(dve.tensor_copy(xq[:, i, :], take(dve, "projx", 1, i)[:, 0:NT]), "projx", 1, i)
            settle("xq_ready", ("projx", 1, 0), ("projx", 1, 1))
            attend(1)
            dve.wait_ge(sig("ln_mu"), 3)
            step(tt_(vT, vT, mu.unsqueeze(1).to_broadcast([P, GB, NT]), ALU.subtract))
            dve.sem_inc(sig("ln_centered"), 1)
            for n in range(2):
                free(tt_(wsT[:, 3 * n:3 * n + 3, :], take(dve, "wsT", n)[:, 0:3 * P].rearrange("p (g t) -> p g t", g=3), causalT.unsqueeze(1).to_broadcast([P, 3, P]), ALU.mult), "wsT", n)
            settle("ws_ready", ("wsT", 0), ("wsT", 1))
            dve.wait_ge(sig("ln_root"), 3)
            step(dve.reciprocal(rstd, rstd))
            step(tt_(vT, vT, rstd.unsqueeze(1).to_broadcast([P, GB, NT]), ALU.mult))
            dve.sem_inc(sig("ln_scaled"), 1)
            for n in range(4):
                tt, half = divmod(n, 2)
                free(dve.tensor_copy(vtok[:, tt, 3 * P * half:3 * P * half + 3 * P], take(dve, "vtokT", n)[:, 0:3 * P]), "vtokT", n)
            for n in range(2):
                free(dve.tensor_copy(vtok[0:NS, 2, 3 * P * n:3 * P * n + 3 * P], take(dve, "vtokS", n)[0:NS, 0:3 * P]), "vtokS", n)
            settle("vtok_ready", *[("vtokT", n) for n in range(4)], ("vtokS", 0), ("vtokS", 1))
            step(free(dve.tensor_copy(rowcol, take(dve, "mixrow")[:, 0:2 * GB]), "mixrow") if False else dve.tensor_copy(rowcol, take(dve, "mixrow")[:, 0:2 * GB]))
            bank, before = bank_of[("mixrow",)]
            dve.sem_inc(bank_free[bank], 1)
            for g in range(GB):
                dve.tensor_scalar(mixT[:, g, SEQ:], vT[:, g, SEQ:], rowcol[:, g:g + 1], rowcol[:, GB + g:GB + g + 1], ALU.mult, ALU.add)
                free(tt_(mixT[:, g, 0:SEQ], take(dve, "mixed", g)[:, 0:SEQ], uT[:, g, 0:SEQ], ALU.mult), "mixed", g)
                bank, before = bank_of[("mixed", g)]
                dve.wait_ge(bank_free[bank], before + 1)
            step(tt_(mixT[:, 0:GB, SEQ:], mixT[:, 0:GB, SEQ:], uT[:, :, SEQ:], ALU.mult))
            dve.sem_inc(sig("mix_ready"), 1)
            residual(1)
            step(dve.memset(zeros, 0.0))
            dve.sem_inc(sig("zeros_ready"), 1)
            norm(1, 3)
            for n in range(2 * TT):
                tt, kg = divmod(n, 2)
                src = take(dve, "x1tok", n)
                free(dve.tensor_copy(x1tok[:, tt, 512 * kg:512 * kg + 512], src), "x1tok", n)
                dve.wait_ge(bank_free[bank_of[("x1tok", n)][0]], bank_of[("x1tok", n)][1] + 1)
                dve.sem_inc(sig("x1tok_ready"), 1)
            for n in range(2):
                free(dve.tensor_copy(x1tok[0:NS, 2, 512 * n:512 * n + 512], take(dve, "x1tokS", n)[0:NS, :]), "x1tokS", n)
                dve.wait_ge(bank_free[bank_of[("x1tokS", n)][0]], bank_of[("x1tokS", n)][1] + 1)
                dve.sem_inc(sig("x1tok_ready"), 1)
            step(dve.memset(lg, 0.0))
            src = take(dve, "logits")[:, 0:3 * NE].rearrange("p (t e) -> p t e", t=3)
            dve.tensor_copy(lg[:, 0:2, :], src[:, 0:2, :])
            step(dve.tensor_copy(lg[0:NS, 2, :], src[0:NS, 2, :]))
            bank, before = bank_of[("logits",)]
            dve.sem_inc(bank_free[bank], 1)
            for t in range(3):
                step(dve.max(mx8[:, t, :], lg[:, t, :]))
                step(dve.max_index(idx8[:, t, :], mx8[:, t, :], lg[:, t, :]))
            step(dve.tensor_copy(idxf, idx8[:, :, :]))
            step(tt_(dtop, mx8[:, :, 1], mx8[:, :, 0], ALU.subtract))
            dve.sem_inc(sig("top_diff"), 1)
            dve.wait_ge(sig("route_consts"), 1)
            for t in range(3):
                dve.tensor_scalar(oh1[:, t, :], iota8, idxf[:, t, 0:1], valid[:, t:t + 1], ALU.is_equal, ALU.mult)
                step(dve.tensor_scalar(oh2[:, t, :], iota8, idxf[:, t, 1:2], valid[:, t:t + 1], ALU.is_equal, ALU.mult))
            step(tt_(Msel, oh1, oh2, ALU.add))
            step(tt_(Mall, Msel[:, 0, :], Msel[:, 1, :], ALU.add))
            step(tt_(Mall, Mall, Msel[:, 2, :], ALU.add))
            dve.sem_inc(sig("sel_ready"), 1)
            dve.wait_ge(sig("top_exp"), 1)
            step(dve.tensor_scalar(den, dtop, 1.0, None, ALU.add))
            step(dve.reciprocal(g1, den))
            step(tt_(g2, dtop, g1, ALU.mult))
            src = take(dve, "rank")[:, 0:4 * NE].rearrange("p (t e) -> p t e", t=4)
            dve.tensor_copy(counts[:, :], src[:, 3, :])
            for chunk in (1, 2):
                ins = dve.tensor_scalar(over[:, (chunk - 1) * NE:chunk * NE], src[:, 3, :], float(chunk * P), None, ALU.is_gt)
            step(ins)
            step(dve.tensor_tensor_scan(turns[:, 1:], ones[:, 0:2 * NE], over, float(NE), ALU.mult, ALU.add))
            step(dve.memset(turns[:, 0:1], float(NE)))
            step(dve.tensor_copy(turn[:, :], turns))
            step(tt_(rbase, src[:, 0:3, :], base8.unsqueeze(1).to_broadcast([P, 3, NE]), ALU.add))
            for k, oh in enumerate((oh1, oh2)):
                step(tt_(tmp24, oh, rbase, ALU.mult))
                step(dve.tensor_reduce(dstf[:, k, :], tmp24, AX_X, ALU.add))
            step(dve.tensor_copy(dst[:, :, :], dstf))
            dve.sem_inc(bank_free[bank_of[("rank",)][0]], 1)
            dve.sem_inc(sig("routed"), 1)
            dve.sem_inc(sig("h_ready"), NG)
            dve.sem_inc(sig("xe_evac"), 2)
            dve.sem_inc(sig("y_copied"), 1)
            dve.sem_inc(sig("y_stored"), 16)

            def unit_lo(t, u):
                dve.wait_ge(sig("unit_hi"), t * UNITS + (UNITS + u + 1))
                tt_(split_w[:, u % SPLITS, 1, :], halves[EXPERT_HALVES[u % HALVES]], split_w[:, u % SPLITS, 0, :].bitcast(F32), ALU.subtract).then_inc(sig("unit_split"), 1)

            def hidden_T(t, c):
                dve.wait_ge(sig("hT_hi"), t * NG + (c + 1))
                tt_(split_he[:, c % 2, 1].rearrange("p f s -> p (f s)"), ps[:, 4 + c % 2, :],
                    split_he[:, c % 2, 0].rearrange("p f s -> p (f s)").bitcast(F32), ALU.subtract).then_inc(sig("hT_ready"), 1)

            def copy_y(t):
                dve.wait_ge(sig("units_used"), t * UNITS + 2 * UNITS)
                dve.wait_ge(sig("y_stored"), t * 16 + 16)
                dve.tensor_copy(yout.rearrange("p (a b) -> p a b", a=2), ps[:, 6:8, :]).then_inc(sig("y_copied"), 1)

            def expert(t):
                for n in range(2):
                    dve.wait_ge(sig("xeT_hi"), t * 2 + (n + 1))
                    tt_(split_xe[:, 1, 4 * n:4 * n + 4, :].rearrange("p k s -> p (k s)"), ps[:, 4 + n, :],
                        split_xe[:, 0, 4 * n:4 * n + 4, :].rearrange("p k s -> p (k s)").bitcast(F32), ALU.subtract).then_inc(sig("xe_evac"), 1)
                for u in range(SPLITS, UNITS):
                    kind, c, i = ORDER[u - SPLITS]
                    if (kind, i) == ("gate", 1) and c:
                        hidden_T(t, c - 1)
                    if (kind, i) == ("up", 1):
                        dve.wait_ge(sig("silu_ready"), t * NG + (c + 1))
                        dve.wait_ge(sig("units_used"), t * UNITS + (UNITS + u - SPLITS + 1))
                        if c >= 2:
                            dve.wait_ge(sig("T_done"), t * (NG + 2) + (c + 1))
                        tt_(hgu[:, c % 2, :], hsil[:, c % 2, :], ps[:, 2 + c % 2, :], ALU.mult).then_inc(sig("h_ready"), 1)
                    unit_lo(t, u)
                hidden_T(t, NG - 1)

            for u in range(SPLITS):
                unit_lo(0, u)
            with dve.Fori(0, NE - 1) as e:
                expert(e)
                for u in range(SPLITS - 1):
                    unit_lo(e + 1, u)
                copy_y(e)
                unit_lo(e + 1, SPLITS - 1)
            expert(NE - 1)
            copy_y(NE - 1)
            for chunk in (1, 2):
                with dve.Fori(0, NE) as e:
                    n_tok = dve.value_load(counts[0:1, bass.ds(e, 1)], min_val=0, max_val=NT)
                    t = dve.value_load(turn[0:1, bass.ds(e + (chunk - 1) * NE, 1)], min_val=NE, max_val=3 * NE)
                    with dve.If(n_tok > chunk * P):
                        for u in range(SPLITS):
                            unit_lo(t, u)
                        expert(t)
                        copy_y(t)
            dve.wait_ge(sig("ln_bc_landed"), 32)
            for t in range(3):
                r = slice(0, P if t < 2 else NS)
                dve.wait_ge(sig("gathered"), 32 * (t + 1))
                if t:
                    dve.wait_ge(sig("y_out"), 16 * t)
                step(dve.tensor_scalar(acc[r, :], x1tok[r, t, :], ALPHA, None, ALU.mult))
                step(dve.scalar_tensor_tensor(acc[r, :], yk[0][r, :], g1[r, t:t + 1], acc[r, :], ALU.mult, ALU.add))
                step(dve.scalar_tensor_tensor(acc[r, :], yk[1][r, :], g2[r, t:t + 1], acc[r, :], ALU.mult, ALU.add))
                dve.sem_inc(sig("yk_read"), 1)
                for i in range(2):
                    ins = dve.bn_stats(stats[r, i, :], acc[r, 512 * i:512 * i + 512])
                step(ins)
                step(dve.bn_aggr(mv[r, :], stats[r].rearrange("p a b -> p (a b)")))
                dve.sem_inc(sig("fin_var"), 1)
                dve.wait_ge(sig("fin_root"), t + 1)
                step(dve.reciprocal(rs1[r, :], rs1[r, :]))
                step(dve.tensor_scalar(acc[r, :], acc[r, :], mv[r, 0:1], rs1[r, :], ALU.subtract, ALU.mult))
                step(tt_(acc[r, :], acc[r, :], ln_bc[r, 0, :], ALU.mult))
                step(tt_(acc[r, :], acc[r, :], ln_bc[r, 1, :], ALU.add))
                dve.sem_inc(sig("fin_ready"), 1)

        @block.tensor
        def _(pe):
            def bank(*name):
                b, before = bank_of[name]
                if before:
                    pe.wait_ge(bank_free[b], before)
                return ps[:, b, :]

            def full(ins, *name):
                ins.then_inc(bank_full[bank_of[name][0]], 1)

            def used(ins):
                ins.then_inc(slabs_used, 1)

            def tr(o, i, n=P):
                return pe.transpose(o, i, ident[0:n, 0:n])

            def mm(o, l, r, start, stop):
                return pe.matmul(o, l, r, start=start, stop=stop)

            pe.wait_ge(sig("consts"), 1)
            pe.wait_ge(sig("params_landed"), 16 * 8)
            full(tr(bank("params", 0)[:, 0:85], prow[0:85, 0, :], 85), "params", 0)
            full(tr(bank("params", 1)[:, 0:64], prow[0:64, 1, :], 64), "params", 1)
            pe.wait_ge(sig("x_landed"), 32)
            for n in range(2 * TT):
                tt, kg = divmod(n, 2)
                o = bank("x", n)
                for q in range(4):
                    ins = tr(o[:, q * P:(q + 1) * P], xrows[:, tt, (4 * kg + q) * P:(4 * kg + q + 1) * P])
                full(ins, "x", n)
            o = bank("xs")
            for k in range(KT):
                ins = tr(o[:, k * NS:(k + 1) * NS], xrows[0:NS, TT, k * P:(k + 1) * P], NS)
            full(ins, "xs")

            def mem_kv(lay):
                pe.wait_ge(sig(f"mem{lay}_landed"), 16)
                for n in range(2 * MT):
                    tt, kg = divmod(n, 2)
                    o = bank("mem", lay, n)
                    for q in range(4):
                        ins = tr(o[:, q * P:(q + 1) * P], memrows[:, tt, (4 * kg + q) * P:(4 * kg + q + 1) * P])
                    full(ins, "mem", lay, n)
                pe.wait_ge(sig("mem_in"), lay + 1)
                wait_slab(pe, ("kv", lay))
                w = as_slab(slab(("kv", lay)), KT, 2 * DX)
                for mt in range(MT):
                    o = bank("kv", lay, mt)
                    for k in range(KT):
                        ins = mm(o, memT[:, k, mt * P:(mt + 1) * P], w[:, k, :], k == 0, k == KT - 1)
                    full(ins, "kv", lay, mt)
                b, before = bank_of[("kv", lay, MT - 1)]
                pe.wait_ge(sig("kv_rows"), lay + 1)
                used(pe.nop()) if False else pe.sem_inc(slabs_used, 1)
                o = bank("kT", lay)
                for ft in range(XT_):
                    for mt in range(MT):
                        ins = tr(o[:, (ft * MT + mt) * P:(ft * MT + mt + 1) * P], kv[:, mt, ft * P:(ft + 1) * P])
                full(ins, "kT", lay)

            def project(o, w, c0, m, act_t):
                for k in range(KT):
                    ins = mm(o[0:m, 0:NT], w[:, k, c0:c0 + m], act_t[:, k, :], k == 0, k == KT - 1)
                return ins

            mem_kv(0)
            pe.wait_ge(sig("hist_landed"), 16)
            for n in range(5):
                o = bank("hist", n)
                for q in range(min(4, CT - 4 * n)):
                    ins = tr(o[:, q * 24:(q + 1) * 24], histrows[0:24, (4 * n + q) * P:(4 * n + q + 1) * P], 24)
                full(ins, "hist", n)
            pe.wait_ge(sig("x_in"), 1)
            for c in range(CT + H):
                what = ("in", 0, c // 4)
                if c % 4 == 0:
                    wait_slab(pe, what)
                ins = project(bank("proj", 0, c), as_slab(slab(what), KT, FC), (c % 4) * P, P, xT)
                full(ins, "proj", 0, c)
                if c % 4 == 3:
                    b, before = bank_of[("proj", 0, c)]
                    pe.wait_ge(bank_full[b], before + 1)
                    pe.sem_inc(slabs_used, 1)
            wait_slab(pe, ("in", 0, 6))
            w = as_slab(slab(("in", 0, 6)), KT, IN_A - 6 * FC)
            for name, c0, m in (("a", 0, H), ("b", H, H), (0, 2 * H, P), (1, 2 * H + P, P)):
                full(project(bank("projx", 0, name), w, c0, m, xT), "projx", 0, name)
            b, before = bank_of[("projx", 0, 1)]
            pe.wait_ge(bank_full[b], before + 1)
            pe.sem_inc(slabs_used, 1)
            nr = PADT + NS
            pe.wait_ge(sig("conv_begun"), CT)
            for n in range(5):
                o = bank("tail", n)
                for q in range(min(4, CT - 4 * n)):
                    ins = tr(o[0:nr, q * P:(q + 1) * P], pre[:, 4 * n + q, SEQ:SEQ + nr])
                full(ins, "tail", n)
            for c in range(2 * H):
                if c % H == 0:
                    pe.wait_ge(sig("qk_squared"), c // H + 1)
                full(mm(bank("norm", c)[:, 0:NT], ones, sq[:, c % H, :], True, True), "norm", c)

            def attend(lay):
                pe.wait_ge(sig("xq_ready"), lay + 1)
                pe.wait_ge(sig("kT_ready"), lay + 1)
                for h in range(HX):
                    r = slice(DH * (h % 2), DH * (h % 2) + DH)
                    o = bank("score", lay, h)
                    for tt in range(TT):
                        ins = mm(o[:, tt * MEM:(tt + 1) * MEM], xq[r, h // 2, tt * P:(tt + 1) * P], kT[r, h // 2, :], True, True)
                    full(ins, "score", lay, h)
                pe.wait_ge(sig("attn_p"), lay + 1)
                for h in range(HX):
                    o = bank("pT", lay, h)
                    for mt in range(MT):
                        for tt in range(TT):
                            ins = tr(o[:, mt * SEQ + tt * P:mt * SEQ + (tt + 1) * P], p_att[:, TT * h + tt, mt * P:(mt + 1) * P])
                    full(ins, "pT", lay, h)
                for n in range(2):
                    o = bank("pv", lay, n)
                    for h in (2 * n, 2 * n + 1):
                        b, before = bank_of[("pT", lay, h)]
                        pe.wait_ge(bank_free[b], before + 1)
                        r = slice(DH * (h % 2), DH * (h % 2) + DH)
                        for mt in range(MT):
                            ins = mm(o[r, 0:SEQ], kv[:, mt, DX + h * DH:DX + (h + 1) * DH], pT_att[:, h, mt, :], mt == 0, mt == MT - 1)
                    full(ins, "pv", lay, n)
                pe.wait_ge(sig("qpad_ready"), lay + 1)

                def keys(b):
                    pe.wait_ge(sig(f"k{b % 2}_landed"), 16 * (NS // 2 * lay + b // 2 + 1))
                    o = bank("cacheT", lay, b)
                    for k in range(XT_):
                        for mt in range(MT):
                            ins = tr(o[:, (k * MT + mt) * P:(k * MT + mt + 1) * P], Kc[:, b % 2, mt, k * P:(k + 1) * P])
                    full(ins, "cacheT", lay, b)

                keys(0)
                o = bank("sscore", lay)
                for b in range(NS):
                    if b + 1 < NS:
                        keys(b + 1)
                    bk, before = bank_of[("cacheT", lay, b)]
                    pe.wait_ge(bank_free[bk], before + 1)
                    for k in range(XT_):
                        last = b == NS - 1 and k == XT_ - 1
                        ins = pe.matmul(o[0:4 * NS, 0:MEM], qpad[:, k, b, :], KTs[:, b % 2, k, :], start=(b == 0 and k == 0), stop=last)
                        if k == XT_ - 1 and not last:
                            ins.then_inc(sig("sscored"), 1)
                full(ins, "sscore", lay)
                pe.wait_ge(bank_full[bank_of[("sscore", lay)][0]], bank_of[("sscore", lay)][1] + 1)
                pe.sem_inc(sig("sscored"), 1)
                pe.wait_ge(sig("ss_p"), lay + 1)
                o = bank("spT", lay)
                for mt in range(MT):
                    ins = tr(o[:, mt * 4 * NS:(mt + 1) * 4 * NS], ps_att[0:4 * NS, mt * P:(mt + 1) * P], 4 * NS)
                full(ins, "spT", lay)
                pe.wait_ge(sig("ss_pT"), lay + 1)
                pe.wait_ge(sig(f"v{lay}_landed"), 16 * NS)
                o = bank("spv", lay)
                for k in range(XT_):
                    for b in range(NS):
                        for mt in range(MT):
                            ins = mm(o[:, (k * NS + b) * 4:(k * NS + b) * 4 + 4], Vc[:, b, mt, k * P:(k + 1) * P], pTs[:, mt, 4 * b:4 * b + 4], mt == 0, mt == MT - 1)
                full(ins, "spv", lay)

            attend(0)
            pe.wait_ge(sig("gates_ready"), 1)
            pe.wait_ge(sig("qk_normed"), 2)
            o = bank("sgate")
            for i, v in enumerate((gc, beta)):
                for h in range(H):
                    ins = mm(o[:, (i * H + h) * NS:(i * H + h + 1) * NS], ident[0:H, h:h + 1].to_broadcast([H, P]), v[0:H, SEQ:NT], True, True)
            full(ins, "sgate")
            pe.wait_ge(sig("s_prod"), 1)
            full(mm(bank("sdot")[:, 0:H * NS], ones, s_kq.rearrange("p h b -> p (h b)"), True, True), "sdot")
            pe.wait_ge(sig("state_landed"), 16)
            o = bank("sread")
            for h in range(H):
                for b in range(NS):
                    n = (h * NS + b) * 2
                    ins = mm(o[:, n:n + 2], state[:, b * H + h, :], qkv[:, h:h + H + 1:H, SEQ + b], True, True)
            full(ins, "sread")
            for n in range(2):
                o = bank("krow", n)
                for q in range(3):
                    ins = tr(o[0:NS, q * P:(q + 1) * P], qkv[:, H + 3 * n + q, SEQ:NT])
                full(ins, "krow", n)
            pe.wait_ge(sig("s_mixed"), 1)
            for n in range(2):
                o = bank("urow", n)
                for q in range(3):
                    ins = tr(o[0:NS, q * P:(q + 1) * P], s_u[:, 3 * n + q, :])
                full(ins, "urow", n)
            pe.wait_ge(sig("s_rows"), 1)
            for h in range(H):
                pe.wait_ge(sig("udiag_ready"), h + 1)
                for n in range(2):
                    full(mm(bank("outer", h, n), krow[0:NS, h, :], udiag[0:NS, h % 2, 512 * n:512 * n + 512], True, True), "outer", h, n)
            pe.wait_ge(sig("masks"), 1)
            for n in range(TT):
                chunk = slice(n * P, (n + 1) * P)
                for name, v in (("gb", gc), ("bb", beta)):
                    for i in range(2):
                        o = bank(name, n, i)
                        for q in range(3):
                            ins = mm(o[:, q * P:(q + 1) * P], ident[0:H, 3 * i + q:3 * i + q + 1].to_broadcast([H, P]), v[0:H, chunk], True, True)
                        full(ins, name, n, i)
                o = bank("gcol", n)
                tr(o[:, 0:H], gc[0:H, chunk], H)
                full(tr(o[:, H:2 * H], beta[0:H, chunk], H), "gcol", n)

                def heads(name, left, right, trans=False, more=None):
                    for i in range(2):
                        o = bank(*name, i)
                        for q in range(3):
                            h = 3 * i + q
                            oh = o[:, q * P:(q + 1) * P]
                            if trans:
                                ins = tr(oh, left(h))
                            else:
                                ins = mm(oh, left(h), right(h), True, more is None)
                                if more is not None:
                                    ins = mm(oh, more[0](h), more[1](h), False, True)
                        full(ins, *name, i)

                kT_h = lambda h: qkv[:, H + h, chunk]
                heads(("kk", n), kT_h, kT_h)
                heads(("qk", n), kT_h, lambda h: qkv[:, h, chunk])
                heads(("ktok", n), kT_h, None, True)
                heads(("vtok", n), lambda h: qkv[:, 2 * H + h, chunk], None, True)
                pe.wait_ge(sig("XT_ready"), n + 1)
                heads(("xinit", n), lambda h: XT[:, h, :], None, True)
                pe.wait_ge(sig("X_ready"), n + 1)
                for s in range(1, 7):
                    pe.wait_ge(sig("AmT_ready"), 6 * n + s)
                    if s > 1:
                        for i in range(2):
                            for nm in ("dX", "dXT"):
                                b, before = bank_of[(nm, n, s - 1, i)]
                                pe.wait_ge(bank_free[b], before + 1)
                    heads(("Y", n, s), lambda h: AmT[:, h, :], lambda h: X[:, h, :])
                    for i in range(2):
                        b, before = bank_of[("Y", n, s, i)]
                        pe.wait_ge(bank_free[b], before + 1)
                    if s < 6:
                        heads(("dX", n, s), lambda h: XT[:, h, :], lambda h: Y[:, h, :])
                    heads(("dXT", n, s), lambda h: Y[:, h, :], lambda h: XT[:, h, :])
                for i in range(2):
                    b, before = bank_of[("dXT", n, 6, i)]
                    pe.wait_ge(bank_free[b], before + 1)
                if n:
                    heads(("wT", n), lambda h: kbg[:, h, :], lambda h: XT[:, h, :])
                    for i in range(2):
                        b, before = bank_of[("wT", n, i)]
                        pe.wait_ge(bank_free[b], before + 1)
                    pe.wait_ge(sig("S_ready"), n)
                    heads(("vnew", n), lambda h: XT[:, h, :], lambda h: vb[:, h, :], more=(lambda h: AmT[:, h, :], lambda h: S[:, h, :]))
                else:
                    heads(("vnew", n), lambda h: XT[:, h, :], lambda h: vb[:, h, :])
                for i in range(2):
                    b, before = bank_of[("vnew", n, i)]
                    pe.wait_ge(bank_free[b], before + 1)
                pe.sem_inc(sig("w_done"), 1)
                heads(("o", n), lambda h: Y[:, h, :], lambda h: attnT[:, h, :],
                      more=(lambda h: S[:, h, :], lambda h: qkv[:, h, chunk]) if n else None)
                heads(("S", n), lambda h: kdec[:, h, :], lambda h: Y[:, h, :])
            pe.wait_ge(sig("o_squared"), 1)
            for h in range(H):
                full(mm(bank("rms", h)[:, 0:NT], ones, sq[:, h, :], True, True), "rms", h)

            def w_out(lay):
                pe.wait_ge(sig("mix_ready"), lay + 1)
                pe.wait_ge(sig("attn_done"), lay + 1)
                for c in range(KT):
                    what = ("out", lay, c // 4)
                    if c % 4 == 0:
                        wait_slab(pe, what)
                    full(project(bank("out", lay, c), as_slab(slab(what), KT, FC), (c % 4) * P, P, mixT), "out", lay, c)
                    if c % 4 == 3:
                        b, before = bank_of[("out", lay, c)]
                        pe.wait_ge(bank_full[b], before + 1)
                        pe.sem_inc(slabs_used, 1)

            def norm(lay, which, count):
                pe.wait_ge(sig("res_ready"), count)
                o = bank("ln_mean", lay, which)
                for k in range(KT):
                    ins = mm(o[:, 0:NT], ones, yT[:, k, :], k == 0, k == KT - 1)
                full(ins, "ln_mean", lay, which)
                pe.wait_ge(sig("ln_squared"), count + lay)
                o = bank("ln_var", lay, which)
                for k in range(KT):
                    ins = mm(o[:, 0:NT], ones, sq[:, k, :], k == 0, k == KT - 1)
                full(ins, "ln_var", lay, which)
                pe.wait_ge(sig("x_ready"), count)

            w_out(0)
            norm(0, 0, 1)
            def three(o, w, x, first, last):
                mm(o, w[0], x[0], first, False)
                mm(o, w[1], x[0], False, False)
                return mm(o, w[0], x[1], False, last)

            for u, (kind, c, i) in enumerate(ORDER):
                pe.wait_ge(sig("unit_split"), u + 1)
                if u == 0:
                    pe.wait_ge(sig("x_lo"), 2)
                n_k = KT if kind != "down" else 4
                w = split_w[:, u % SPLITS].rearrange("p s (k n) -> p s k n", k=n_k)
                if kind == "down":
                    pe.wait_ge(sig("hid_ready"), 4 * (c + 1))
                for q in range(UNIT // n_k // P):
                    n = q + i * (UNIT // n_k // P)
                    o = bank(kind, c, n)
                    for k in range(n_k):
                        x = [split_h[:, c % 2, s, k, :] if kind == "down" else split_x[s][:, k, :] for s in range(2)]
                        ins = three(o[:, 0:NT], [w[:, s, k, q * P:(q + 1) * P] for s in range(2)], x, k == 0, k == n_k - 1)
                    full(ins, kind, c, n)
            norm(0, 1, 2)
            mem_kv(1)
            for c in range(2 * GB):
                what = ("in", 1, c // 4)
                if c % 4 == 0:
                    wait_slab(pe, what)
                full(project(bank("proj", 1, c), as_slab(slab(what), KT, FC), (c % 4) * P, P, xT), "proj", 1, c)
                if c % 4 == 3:
                    b, before = bank_of[("proj", 1, c)]
                    pe.wait_ge(bank_full[b], before + 1)
                    pe.sem_inc(slabs_used, 1)
            wait_slab(pe, ("in", 1, 3))
            w = as_slab(slab(("in", 1, 3)), KT, 2 * P)
            for i in range(2):
                full(project(bank("projx", 1, i), w, i * P, P, xT), "projx", 1, i)
            b, before = bank_of[("projx", 1, 1)]
            pe.wait_ge(bank_full[b], before + 1)
            pe.sem_inc(slabs_used, 1)
            attend(1)
            pe.wait_ge(sig("uv_ready"), 1)
            o = bank("vmean")
            for k in range(GB):
                ins = mm(o[:, 0:NT], ones, vT[:, k, :], k == 0, k == GB - 1)
            full(ins, "vmean")
            pe.wait_ge(sig("ws_landed"), 16)
            for n in range(2):
                o = bank("wsT", n)
                for q in range(3):
                    ins = tr(o[:, q * P:(q + 1) * P], wsrows[:, 3 * n + q, :])
                full(ins, "wsT", n)
            pe.wait_ge(sig("ln_squared"), 3)
            o = bank("vvar")
            for k in range(GB):
                ins = mm(o[:, 0:NT], ones, sq[:, k, :], k == 0, k == GB - 1)
            full(ins, "vvar")
            pe.wait_ge(sig("v_ready"), 1)
            for n in range(4):
                tt, half = divmod(n, 2)
                o = bank("vtokT", n)
                for q in range(3):
                    ins = tr(o[:, q * P:(q + 1) * P], vT[:, 3 * half + q, tt * P:(tt + 1) * P])
                full(ins, "vtokT", n)
            for n in range(2):
                o = bank("vtokS", n)
                for q in range(3):
                    ins = tr(o[0:NS, q * P:(q + 1) * P], vT[:, 3 * n + q, SEQ:NT])
                full(ins, "vtokS", n)
            pe.wait_ge(sig("ws_ready"), 1)
            pe.wait_ge(sig("bs_landed"), 16)
            o = bank("mixrow")
            mm(o[:, 0:GB], ones[0:1, :], wsT[0:1, :, 0], True, True)
            for g in range(GB):
                ins = mm(o[:, GB + g:GB + g + 1], ident[0:GB, g:g + 1].to_broadcast([GB, P]), bsrow[0:GB, 0:1], True, True)
            full(ins, "mixrow")
            pe.wait_ge(sig("vtok_ready"), 1)
            for g in range(GB):
                o = bank("mixed", g)
                for tt in range(TT):
                    mm(o[:, tt * P:(tt + 1) * P], vtok[:, tt, g * P:(g + 1) * P], wsT[:, g, :], True, False)
                    ins = mm(o[:, tt * P:(tt + 1) * P], ident[0:GB, g:g + 1].to_broadcast([GB, P]), bsrow[0:GB, :], False, True)
                full(ins, "mixed", g)
            w_out(1)
            norm(1, 0, 3)
            pe.wait_ge(sig("mix_ready"), 2)
            for n in range(2 * TT):
                tt, kg = divmod(n, 2)
                o = bank("x1tok", n)
                for q in range(4):
                    ins = tr(o[:, q * P:(q + 1) * P], xT[:, 4 * kg + q, tt * P:(tt + 1) * P])
                full(ins, "x1tok", n)
            for n in range(2):
                o = bank("x1tokS", n)
                for q in range(4):
                    ins = tr(o[0:NS, q * P:(q + 1) * P], xT[:, 4 * n + q, SEQ:NT])
                full(ins, "x1tokS", n)
            pe.wait_ge(sig("router_landed"), 16)
            o = bank("logits")
            for t in range(3):
                m = P if t < 2 else NS
                for k in range(KT):
                    ins = mm(o[0:m, t * NE:(t + 1) * NE], xT[:, k, t * P:t * P + m], router[:, k, :], k == 0, k == KT - 1)
            full(ins, "logits")
            pe.wait_ge(sig("sel_ready"), 1)
            o = bank("rank")
            for t in range(3):
                for u in range(t):
                    mm(o[:, t * NE:(t + 1) * NE], ones, Msel[:, u, :], u == 0, False)
                mm(o[:, t * NE:(t + 1) * NE], strictT, Msel[:, t, :], t == 0, True)
            full(mm(o[:, 3 * NE:4 * NE], ones, Mall, True, True), "rank")
            pe.wait_ge(sig("routed"), 1)
            for n in range(8):
                count = max([before for (bk, before) in bank_of.values() if bk == n]) + 1
                pe.wait_ge(bank_free[n], count)
            pe.sem_inc(sig("xe_read"), 1)
            pe.sem_inc(sig("units_used"), UNITS)

            def expert(t):
                pe.wait_ge(sig("xe_landed"), t * 16 + 16)
                for n in range(2):
                    for q in range(4):
                        ins = tr(ps[:, 4 + n, q * P:(q + 1) * P], Xe[:, (4 * n + q) * P:(4 * n + q + 1) * P])
                    ins.then_inc(sig("T_done"), 1)
                pe.wait_ge(sig("xe_evac"), t * 2 + 4)
                pe.sem_inc(sig("xe_read"), 1)
                for u, (kind, c, i) in enumerate(ORDER):
                    if kind == "down" and i == 0 and c == NG - 1:
                        transpose_h(t, c)
                    if kind == "gate" and i == 0:
                        pe.wait_ge(sig("h_ready"), t * NG + (NG + c - 1))
                    if kind == "down" and i == 0:
                        pe.wait_ge(sig("hT_ready"), t * NG + (c + 1))
                        if c == 0:
                            pe.wait_ge(sig("y_copied"), t + 1)
                    pe.wait_ge(sig("unit_split"), t * UNITS + (UNITS + u + 1))
                    w = split_w[:, u % SPLITS]
                    if kind == "down":
                        for q in range(2):
                            x = [split_he[:, c % 2, s, 2 * i + q, :] for s in range(2)]
                            for half in range(2):
                                c0 = q * D + 512 * half
                                ins = three(ps[:, 6 + half, :], x, [w[:, s, c0:c0 + 512] for s in range(2)], c == 0 and i == 0 and q == 0, c == NG - 1 and i == 1 and q == 1)
                    else:
                        b = c % 2 + (2 if kind == "up" else 0)
                        for k in range(4):
                            x = [split_xe[:, s, 4 * i + k, :] for s in range(2)]
                            ins = three(ps[:, b, :], x, [w[:, s, k * FC:(k + 1) * FC] for s in range(2)], i == 0 and k == 0, i == 1 and k == 3)
                    ins.then_inc(sig("units_used"), 1)
                    if kind == "gate" and i == 1 and c:
                        transpose_h(t, c - 1)

            def transpose_h(t, c):
                pe.wait_ge(sig("h_ready"), t * NG + (NG + c + 1))
                for q in range(4):
                    ins = tr(ps[:, 4 + c % 2, q * P:(q + 1) * P], hgu[:, c % 2, q * P:(q + 1) * P])
                ins.then_inc(sig("T_done"), 1)

            with pe.Fori(0, NE) as e:
                expert(e)
            for chunk in (1, 2):
                with pe.Fori(0, NE) as e:
                    n_tok = pe.value_load(counts[0:1, bass.ds(e, 1)], min_val=0, max_val=NT)
                    t = pe.value_load(turn[0:1, bass.ds(e + (chunk - 1) * NE, 1)], min_val=NE, max_val=3 * NE)
                    with pe.If(n_tok > chunk * P):
                        expert(t)


_INS = ["x_prompt", "x_sample", "state_gdn", "state_conv", "cache_mem_k", "cache_mem_v", "mem_prompt",
        "a_w_in", "a_conv_w", "a_A_log", "a_dt_bias", "a_norm_w", "b_w_in", "b_ln_g", "b_ln_b", "b_w_s",
        "b_b_s", "w_mem_kv", "w_out", "ln1_g", "ln1_b", "ln2_g", "ln2_b", "ffn_w_gu", "ffn_w_down",
        "moe_router", "moe_w_gu", "moe_w_down"]
_OUTS = {
    "y_prompt": (1, SEQ, D), "y_sample": (NS, 1, D), "p_state_gdn": (1, 1, H, P, P),
    "p_state_conv": (1, 1, PADT, CONV), "p_cache_mem_k": (DEPTH, 1, MEM, HX, DH),
    "p_cache_mem_v": (DEPTH, 1, MEM, HX, DH), "s_state_gdn": (1, NS, H, P, P),
    "s_state_conv": (1, NS, PADT, CONV), "s_sgu_v": (1, NS, 1, D_B),
}


def kernel(**inputs):
    import numpy as _np
    import concourse.bacc as _bacc
    from concourse.bass_utils import run_bass_kernel_spmd as _run

    nc = _bacc.Bacc("TRN2", target_bir_lowering=False, num_devices=1)
    arrays, a, out = {}, {}, {}
    for name in _INS:
        arrays[f"in_{name}"] = _np.ascontiguousarray(inputs[name])
        a[name] = nc.dram_tensor(f"in_{name}", arrays[f"in_{name}"].shape, F32, kind="ExternalInput").ap()
    for name, shape in _OUTS.items():
        out[name] = nc.dram_tensor(f"out_{name}", shape, F32, kind="ExternalOutput").ap()
    xy = nc.dram_tensor("sorted_rows", (NE * CAP, D), F32, kind="Internal").ap()
    hybrid_step(nc, a, out, xy)
    r = _run(nc, [arrays], core_ids=[0])
    return tuple(r.results[0][f"out_{name}"] for name in _OUTS)
```

```python
from contextlib import ExitStack

import concourse.bass as bass
from concourse import mybir

F32 = mybir.dt.float32
F32R = mybir.dt.float32r
U32 = mybir.dt.uint32
ALU = mybir.AluOpType
ACT = mybir.ActivationFunctionType
AX_X = mybir.AxisListType.X

P = 128
D = 1024
KT = D // P
SEQ = 256
NS = 8
NT = SEQ + NS
TT = SEQ // P
H = 6
CONV = 3 * H * P
CT = CONV // P
CW = 4
PADT = CW - 1
IN_A = CONV + H * P + 2 * H + 256
D_B = 768
GB = D_B // P
IN_B = 2 * D_B + 256
MEM = 256
MT = MEM // P
HX = 4
DH = 64
DX = HX * DH
XT_ = DX // P
FF = 3584
FC = 512
NG = FF // FC
NE = 8
DEPTH = 2
ALPHA = (2 * DEPTH) ** 0.25
LN_EPS = 1e-5
RMS_EPS = 1e-6
SLAB = KT * FC
SLOTS = 3
UNIT = SLAB // 2
HALVES = 2 * SLOTS
UNITS = 6 * NG
SPLITS = 3


class Banks:

    def __init__(self):
        self.count = [0] * 8
        self.of = {}

    def add(self, name, bank):
        assert name not in self.of
        self.of[name] = (bank, self.count[bank])
        self.count[bank] += 1


def plan_banks():
    banks = Banks()
    add = banks.add
    for n in range(2 * TT):
        add(("x", n), 2 + n)
    add(("xs",), 6)
    for n in range(2):
        add(("params", n), n)
    for lay in range(DEPTH):
        for n in range(2 * MT):
            add(("mem", lay, n), (7, 2, 3, 4)[n])
        for mt in range(MT):
            add(("kv", lay, mt), 5 + mt)
        add(("kT", lay), 7)
        if lay == 0:
            for c in range(5):
                add(("hist", c), (6, 7, 0, 1, 2)[c])
            steps = [("proj", 0, c) for c in range(CT + 3)] + [("norm", c) for c in range(H)] + [("proj", 0, CT + 3)]
            steps += [("norm", H + c) for c in range(H)] + [("proj", 0, CT + 4), ("proj", 0, CT + 5)]
            steps += [("projx", 0, c) for c in ("a", "b", 0, 1)] + [("tail", c) for c in range(5)]
            for n, name in enumerate(steps):
                add(name, n % 8)
        else:
            for n, c in enumerate(PROJ_B[:8]):
                add(("proj", 1, c), n)
            for n in range(2):
                add(("wsT", n), n)
            add(("vmean",), 2)
            for n, c in enumerate(PROJ_B[8:]):
                add(("proj", 1, c), 3 + n)
                if n == 1:
                    add(("vvar",), 7)
            for c in range(2):
                add(("projx", 1, c), c)
            for n in range(4):
                add(("vtokT", n), 2 + n)
            for n in range(2):
                add(("vtokS", n), 6 + n)
            add(("mixrow",), 0)
        for h in range(HX):
            add(("score", lay, h), h)
        for h in range(HX):
            add(("pT", lay, h), 4 + h)
        for n in range(2):
            add(("pv", lay, n), n)
        for b in range(NS):
            add(("cacheT", lay, b), 4 + b % 2)
            if b == 0:
                add(("sscore", lay), 2)
        add(("spT", lay), 3)
        add(("spv", lay), 6)
        if lay == 0:
            add(("sgate",), 7)
            add(("sdot",), 0)
            add(("sread",), 1)
            for n in range(2):
                add(("krow", n), 2 + n)
                add(("urow", n), 4 + n)
            for h in range(H):
                for n in range(2):
                    add(("outer", h, n), (6 + n) if h % 2 == 0 else n)
            for n in range(TT):
                for i in range(2):
                    add(("gb", n, i), i)
                for i in range(2):
                    add(("bb", n, i), 2 + i)
                add(("gcol", n), 4)
                for i in range(2):
                    add(("kk", n, i), 5 + i)
                for i in range(2):
                    add(("qk", n, i), (7, 0)[i])
                for i in range(2):
                    add(("ktok", n, i), 1 + i)
                for i in range(2):
                    add(("vtok", n, i), 3 + i)
                for i in range(2):
                    add(("xinit", n, i), 5 + i)
                for s in range(1, 7):
                    for i in range(2):
                        add(("Y", n, s, i), i)
                    if s < 6:
                        for i in range(2):
                            add(("dX", n, s, i), 2 + i)
                    for i in range(2):
                        add(("dXT", n, s, i), 4 + i)
                if n:
                    for i in range(2):
                        add(("wT", n, i), 6 + i)
                for i in range(2):
                    add(("vnew", n, i), i)
                for i in range(2):
                    add(("o", n, i), 2 + i)
                for i in range(2):
                    add(("S", n, i), 4 + i)
            for h in range(H):
                add(("rms", h), h)
        else:
            for g in range(GB):
                add(("mixed", g), g)
        for c in range(KT):
            add(("out", lay, c), c)
        add(("ln_mean", lay, 0), 0)
        add(("ln_var", lay, 0), 1)
        if lay == 0:
            for c in range(NG + 1):
                if c < NG:
                    for f in range(4):
                        add(("gate", c, f), 2 * (f % 2))
                        add(("up", c, f), 2 * (f % 2) + 1)
                if c:
                    for d in range(KT):
                        add(("down", c - 1, d), 4 + d % 4)
            add(("ln_mean", lay, 1), 0)
            add(("ln_var", lay, 1), 1)
    add(("logits",), 0)
    for n in range(2 * TT):
        add(("x1tok", n), 2 + n)
    for n in range(2):
        add(("x1tokS", n), 6 + n)
    add(("rank",), 1)
    return banks.of


def plan_slabs():
    mixer = [[("kv", lay)] + [("in", lay, c) for c in (range(7) if lay == 0 else (1, 2, 0, 3))] + [("out", lay, c) for c in range(2)]
             for lay in range(DEPTH)]
    plan, landed, n = {}, [0] * SLOTS, 0
    for lay in range(DEPTH):
        last = {}
        for j, what in enumerate(mixer[lay]):
            slot = j % SLOTS if lay == 0 else (1, 2, 0)[j % SLOTS]
            landed[slot] += 1
            plan[what] = (n, slot, landed[slot], last.get(slot))
            last[slot] = n
            n += 1
    return plan


def unit_order():
    order = []
    for c in range(NG + 1):
        if c < NG:
            order += [("gate", c, 0), ("up", c, 0), ("gate", c, 1), ("up", c, 1)]
        if c:
            order += [("down", c - 1, 0), ("down", c - 1, 1)]
    return order


ORDER = unit_order()
LN_PARTS = {(0, 0): 0, (0, 1): KT // 2, "v": KT, (1, 0): KT + GB // 2}
PROJ_B = list(range(4, 2 * GB)) + list(range(4))
DENSE_HALVES = (2, 3, 4, 5, 0, 1)
EXPERT_HALVES = (4, 5, 0, 1, 2, 3)


def hybrid_step(nc, a, out):
    bank_of = plan_banks()
    slab_of = plan_slabs()

    with ExitStack() as ctx:
        names = {}

        def sig(name):
            if name not in names:
                names[name] = ctx.enter_context(nc.semaphore(name))
            return names[name]

        total = 53000
        sb = ctx.enter_context(nc.sbuf_tensor("sb", [P, total], F32))
        sb_base = nc.sbuf_base - 4 * total
        ps = ctx.enter_context(nc.psum_tensor("ps", [P, 8, 512], F32))
        at = [0]

        def place(*shape, base=None):
            n = 1
            for s in shape:
                n *= s
            if base is None:
                off = at[0]
                at[0] += n
            else:
                off = base
            assert off + n <= total, (off, n)
            ap = sb[:, off:off + n]
            if len(shape) == 2:
                ap = ap.rearrange("p (a b) -> p a b", a=shape[0])
            if len(shape) == 3:
                ap = ap.rearrange("p (a b c) -> p a b c", a=shape[0], b=shape[1])
            return ap

        def alias(name, *shape, base, dtype=F32):
            return nc.alloc_sbuf_tensor_at(name, [P, *shape], dtype, offset=sb_base + 4 * base)

        def place_r(name, *shape, base):
            return alias(name, *shape, base=base, dtype=F32R)

        ring = [place(SLAB) for _ in range(SLOTS)]
        lent0 = at[0]
        at[0] += 4 * SLAB
        half_slots = alias("half_slots", HALVES, UNIT, base=0)
        halves = [half_slots[:, h, :] for h in range(HALVES)]
        split_w = place_r("split_w", SPLITS, 2, UNIT, base=lent0)
        ex0 = lent0 + SPLITS * 2 * UNIT
        split_xe = place_r("split_xe", 2, KT, P, base=ex0)
        split_he = place_r("split_he", 2, 2, 4, P, base=ex0 + 2 * D)
        xT = place(KT, NT)
        mixT = place(KT, NT)
        y0 = at[0]
        yT = place(KT, NT)
        sq0 = at[0]
        sq = place(KT, NT)
        ident = place(P)
        ones = place(P)
        strictT = place(P)
        causalT = place(P)
        stage_mask = place(7, P)
        pcol1 = place(85)
        pcol2 = place(64)
        conv_col = pcol1[:, 0:CW * CT].rearrange("p (j c) -> p j c", j=CW)
        bln_g, bln_b, norm_w = pcol1[:, 72:78], pcol1[:, 78:84], pcol1[:, 84:85]
        ln_col = pcol2.rearrange("p (w l k) -> p w l k", w=4, l=DEPTH)
        gc = place(NT)
        beta = place(NT)
        gpar = place(4)
        tok_g = place(H)
        tok_b = place(H)
        tok_eg = place(H)
        tok_beg = place(H)
        tok_kd = place(H)
        glast = place(H)
        eglast = place(H)
        attn_max = place(8)
        attn_sum = place(8)
        eps_rms = place(1)
        eps_ln = place(1)
        mu = place(NT)
        rstd = place(NT)
        at[0] = -(-at[0] // 8) * 8
        arena0 = at[0]
        qkv = place(CT, NT)
        zs = place(H, NT)
        xq = place(XT_, NT)
        kv0 = at[0]
        kv = place(MT, 2 * DX)
        kT = place(XT_, MEM)
        g0 = at[0]
        attnT = place(H, P)
        AT = place(H, P)
        X = place(H, P)
        XT = place(H, P)
        kdec = place(H, P)
        S = place(H, P)
        tails = place(CONV, base=g0)
        memT = place(KT, MEM, base=g0 + CONV)
        p_att = place(2 * HX, MEM, base=g0)
        pT_att = place(HX, MT, SEQ, base=g0 + 2 * HX * MEM)
        Y = place(H, P, base=sq0)
        AmT = place(H, P, base=sq0 + H * P)
        vb = place(H, P, base=y0)
        kbg = place(H, P, base=y0 + H * P)
        memrows = [place(MT, D, base=b) for b in (y0, g0)]
        KTs = place(2, XT_, MEM, base=y0)
        hs = place(CT, NS * CW, base=y0 + 1024)
        qpad = place(XT_, NS, 4 * NS, base=y0 + 1600)
        sqk = [sq[:, 0:H, :], place(H, NT, base=y0)]
        gate_a, gate_n, gate_e, gate_l, gate_g = (mixT[0:H, i, :] for i in range(5))
        state = place(NS * H, P, base=lent0)
        pre = place(CT, PADT + NT, base=lent0 + 6144)
        xrows = place(3, D, base=lent0 + 6144)
        prow = place(2, P, base=lent0)
        krow = place(H, P, base=lent0 + 6144)
        urow = place(H, P, base=lent0 + 6912)
        udiag = place(2, NS * P, base=lent0 + 7680)
        sv0 = lent0 + 9728
        s_eg, s_be, s_sk, s_u, s_o, s_kq = (place(H, NS, base=sv0 + 48 * i) for i in range(6))
        Kc = place(NS, MT, DX, base=lent0 + 6144)
        ps_att = place(MEM, base=lent0 + 11974)
        pTs = place(MT, 4 * NS, base=lent0 + 12230 - 64 + 58)
        histrows = place(CONV, base=lent0 + 12288)
        Vc = place(NS, MT, DX, base=lent0 + 12288)
        silu_t = place(2, NT, base=arena0)
        hid_t = alias("hid_t", 2, NT, base=arena0 + 528)
        split_x = [place_r(f"x_{part}", KT, NT, base=arena0 + 1056 + KT * NT * i) for i, part in enumerate(("hi", "lo"))]
        split_h = place_r("split_h", 2, 2, 4, NT, base=arena0 + 1056 + 2 * KT * NT)
        assert 1056 + 4 * KT * NT <= CT * NT + H * NT + XT_ * NT + MT * 2 * DX + XT_ * MEM + 3 * H * P
        uT = place(GB, NT, base=arena0)
        vT = place(GB, NT, base=arena0 + 1584)
        vtok = place(3, D_B, base=arena0 + 3168)
        wsT = place(GB, P, base=arena0 + 5472)
        wsrows = place(GB, P, base=sq0)
        bsrow = place(P, base=arena0 + 12800)
        rowcol = place(2 * GB, base=arena0 + 12928)
        assert arena0 + 5472 + 768 <= kv0
        assert arena0 + 12500 <= total
        acc = place(TT, D, base=arena0)
        acc_s = place(KT, NS, base=arena0 + 2048)
        split_xt = place_r("split_xt", 3, 2, D, base=arena0 + 2112)
        sel = place_r("sel", 3, P, base=arena0 + 8256)
        selT = place_r("selT", NT, base=arena0 + 8640)
        pos = place(3, NE, base=arena0 + 8904)
        gates = place(3, NE, base=arena0 + 8928)
        gate_now = place(3, base=arena0 + 8952)
        gate_slot = place(1, base=arena0 + 8955)
        slot_iota = place(P, base=arena0 + 8960)
        hsil = place(2, FC, base=y0)
        hgu = place(2, FC, base=y0 + 2 * FC)
        split_y = place_r("split_y", 2, D, base=sq0)
        acc_st = place(D, base=y0)
        router = place(KT, NE, base=arena0 + 9216)
        r0 = arena0 + 9280
        lg, oh1, oh2, Msel, _ = (place(3, NE, base=r0 + 24 * i) for i in range(5))
        mx8 = place(3, NE, base=r0 + 120)
        idxf = place(3, NE, base=r0 + 144)
        iota8 = place(NE, base=r0 + 168)
        valid = place(3, base=r0 + 184)
        dtop = place(3, base=r0 + 187)
        g1 = place(3, base=r0 + 190)
        g2 = place(3, base=r0 + 193)
        den = place(3, base=r0 + 196)
        tmp24 = place(3, NE, base=r0 + 256 + 33)
        Mall = place(NE, base=r0 + 176)
        ln_bc = mixT.rearrange("p a b -> p (a b)")[:, 0:2 * D].rearrange("p (a b) -> p a b", a=2)
        idx8 = ctx.enter_context(nc.sbuf_tensor("idx8", [P, 3, NE], U32))
        counts = ctx.enter_context(nc.sbuf_tensor("counts", [P, NE], U32))
        turn = ctx.enter_context(nc.sbuf_tensor("turn", [P, 2 * NE + 1], U32))
        stats = place(3, 2, 6, base=r0 + 206)
        mv = place(3, 2, base=r0 + 242)
        rs3 = place(3, base=r0 + 248)
        over = place(2 * NE, base=r0 + 256)
        turns = place(2 * NE + 1, base=r0 + 272)
        assert r0 + 313 <= total

        bank_full = [sig(f"bank{b}_full") for b in range(8)]
        bank_free = [sig(f"bank{b}_free") for b in range(8)]
        landed = [sig(f"slot{s}_landed") for s in range(SLOTS)]
        half_landed = [sig(f"half{h}_landed") for h in range(HALVES)]
        slabs_used = sig("slabs_used")

        def slab(what):
            return ring[slab_of[what][1]]

        def wait_slab(eng, what):
            _, slot, count, _ = slab_of[what]
            eng.wait_ge(landed[slot], 16 * count)

        def take(eng, *name):
            bank, before = bank_of[name]
            eng.wait_ge(bank_full[bank], before + 1)
            return ps[:, bank, :]

        def free(ins, *name):
            return ins.then_inc(bank_free[bank_of[name][0]], 1)

        def pair(name, i):
            return name[:, 3 * i:3 * i + 3, :].rearrange("p a b -> p (a b)")

        def wait_unit_used(eng, u):
            bank, before = bank_of[unit_bank(u)]
            eng.wait_ge(bank_full[bank], before + 1)

        def unit_bank(u):
            kind, c, i = ORDER[u]
            return (kind, c, 2 * i + 1) if kind != "down" else (kind, c, 4 * i + 3)

        class Chain:

            def __init__(self, eng, name):
                self.eng, self.sem, self.n = eng, sig(name), 0

            def __call__(self, ins):
                self.n += 1
                ins.then_inc(self.sem, 1)
                self.eng.wait_ge(self.sem, self.n)

            def settle(self, name):
                self.eng.sem_inc(sig(name), 1)

        block = ctx.enter_context(nc.Block())

        def w_in_source(what):
            kind = what[0]
            if kind == "kv":
                src = a["w_mem_kv"][what[1]]
                c0, n = 0, 2 * DX
            elif kind == "in":
                src = a["a_w_in" if what[1] == 0 else "b_w_in"][0]
                c0 = what[2] * FC
                n = min(FC, (IN_A if what[1] == 0 else IN_B) - c0)
            else:
                src = a["w_out"][what[1]]
                c0, n = what[2] * FC, FC
            return src[:, c0:c0 + n].rearrange("(k p) n -> p k n", p=P), KT, n

        def as_slab(ap, k, n):
            return ap[:, 0:k * n].rearrange("p (k n) -> p k n", k=k)

        @block.sync
        def _(sp):
            def mixer_slabs(lay):
                for what, (n, slot, count, before) in slab_of.items():
                    if what[1] != lay:
                        continue
                    if before is not None:
                        sp.wait_ge(slabs_used, before + 1)
                    elif lay:
                        sp.wait_ge(sig("unit_split"), UNITS - HALVES + 2 * [1, 2, 0].index(slot) + 2)
                    src, k, cols = w_in_source(what)
                    sp.dma_start(as_slab(ring[slot], k, cols), src).then_inc(landed[slot], 16)

            def last_use(lay, slot):
                return max(n for what, (n, sl, _, _) in slab_of.items() if what[1] == lay and sl == slot) + 1

            def load_unit(u, w_gu, w_down, half, by_rows):
                kind, c, i = ORDER[u]
                w, c0, rows, cols = (w_down, 0, FC, D) if kind == "down" else (w_gu, c * FC + (FF if kind == "up" else 0), D, FC)
                if kind == "down":
                    w = w[c * FC:(c + 1) * FC]
                if by_rows:
                    w = w[i * rows // 2:(i + 1) * rows // 2, c0:c0 + cols]
                else:
                    w = w[:, c0 + i * cols // 2:c0 + (i + 1) * cols // 2]
                k = UNIT // (cols if by_rows else cols // 2)
                sp.dma_start(as_slab(halves[half], k, UNIT // k), w.rearrange("(k p) n -> p k n", p=P)).then_inc(half_landed[half], 16)

            sp.dma_start(memrows[0], a["mem_prompt"][0].rearrange("(t p) d -> p t d", p=P)).then_inc(sig("mem0_landed"), 16)
            mixer_slabs(0)
            for u in range(UNITS):
                half = DENSE_HALVES[u % HALVES]
                if u >= HALVES:
                    sp.wait_ge(sig("unit_split"), u - HALVES + 1)
                else:
                    sp.wait_ge(slabs_used, last_use(0, half // 2))
                load_unit(u, a["ffn_w_gu"][0], a["ffn_w_down"][0], half, False)
            mixer_slabs(1)

            def expert_unit(e, t, u):
                if t is not None:
                    sp.wait_ge(sig("unit_split"), t * UNITS + (UNITS + u - HALVES + 1))
                load_unit(u, a["moe_w_gu"][0][bass.ds(e, 1)][0], a["moe_w_down"][0][bass.ds(e, 1)][0], EXPERT_HALVES[u % HALVES], True)

            for u in range(HALVES):
                sp.wait_ge(slabs_used, last_use(1, EXPERT_HALVES[u] // 2))
                expert_unit(0, None, u)
            with sp.Fori(0, NE - 1) as e:
                for u in range(HALVES, UNITS):
                    expert_unit(e, e, u)
                for u in range(HALVES):
                    expert_unit(e + 1, e + 1, u)
            for u in range(HALVES, UNITS):
                expert_unit(NE - 1, NE - 1, u)
            sp.wait_ge(sig("routed"), 1)
            runs = sp.value_load(turn[0:1, 2 * NE:2 * NE + 1], min_val=NE, max_val=3 * NE)
            with sp.If(runs > NE):
                for chunk in (1, 2):
                    with sp.Fori(0, NE) as e:
                        n_tok = sp.value_load(counts[0:1, bass.ds(e, 1)], min_val=0, max_val=NT)
                        t = sp.value_load(turn[0:1, bass.ds(e + (chunk - 1) * NE, 1)], min_val=NE, max_val=3 * NE)
                        with sp.If(n_tok > chunk * P):
                            for u in range(UNITS):
                                expert_unit(e, t, u)
            sp.wait_ge(sig("y_out"), 16 * 3)
            for s in range(DEPTH):
                sp.wait_ge(sig(f"cache_out{s}"), 32)
            sp.wait_ge(sig("state_out"), 16)
            sp.wait_ge(sig("pstate_out"), 16)
            sp.wait_ge(sig("conv_out"), 48)
            sp.wait_ge(sig("sgu_out"), 16)

        @block.gpsimd
        def _(pool):
            step = Chain(pool, "pool_step")
            pool.memset(ident, 0.0)
            pool.memset(eps_rms, RMS_EPS)
            pool.memset(eps_ln, LN_EPS)
            step(pool.memset(ones, 1.0))
            step(pool.affine_select(out=ident, in_=ident, pattern=[[-1, P]], compare_op=ALU.not_equal, fill=1.0, base=0, channel_multiplier=1))
            pool.sem_inc(sig("consts"), 1)
            sc = a["state_conv"][0].rearrange("b j c -> (b j) c")
            pool.dma_start(histrows[0:NS * PADT, :], sc).then_inc(sig("hist_landed"), 16)
            pool.dma_start(gpar[0:H, 0:1], a["a_A_log"].rearrange("a h -> h a")).then_inc(sig("gpar_landed"), 16)
            pool.dma_start(gpar[0:H, 1:2], a["a_dt_bias"].rearrange("a h -> h a")).then_inc(sig("gpar_landed"), 16)
            pool.dma_start(out["s_state_conv"][0, :, 0:PADT - 1, :], a["state_conv"][0, :, 1:PADT, :]).then_inc(sig("conv_out"), 16)
            step(pool.affine_select(out=strictT, in_=ones, pattern=[[1, P]], compare_op=ALU.is_gt, fill=0.0, base=0, channel_multiplier=-1))
            step(pool.affine_select(out=causalT, in_=ones, pattern=[[1, P]], compare_op=ALU.is_ge, fill=0.0, base=0, channel_multiplier=-1))
            same = [ident] + [stage_mask[:, s, :] for s in range(6)] + [ones]
            for s in range(1, 7):
                b = 1 << s
                v = same[s].rearrange("p (n b) -> p n b", b=b)
                o = ones.rearrange("p (n b) -> p n b", b=b)
                step(pool.affine_select(out=v, in_=o, pattern=[[-b, P // b], [0, b]], compare_op=ALU.is_ge, fill=0.0, base=0, channel_multiplier=1))
                step(pool.affine_select(out=v, in_=v, pattern=[[b, P // b], [0, b]], compare_op=ALU.is_ge, fill=0.0, base=b - 1, channel_multiplier=-1))
            for s in range(6, -1, -1):
                lower = same[s]
                step(pool.tensor_tensor(stage_mask[:, s, :], same[s + 1], lower, ALU.subtract))
                step(pool.tensor_tensor(stage_mask[:, s, :], stage_mask[:, s, :], strictT, ALU.mult))
                if s:
                    pass
            pool.sem_inc(sig("masks"), 1)
            pool.wait_ge(sig("params_in"), 1)
            pool.dma_start(state, a["state_gdn"][0].rearrange("b h k v -> k (b h) v")).then_inc(sig("state_landed"), 16)
            pool.wait_ge(sig("x_in"), 1)
            step(pool.memset(pre[:, :, 0:PADT], 0.0))
            pool.sem_inc(sig("pre_zero"), 1)

            def values(lay):
                src = a["cache_mem_v"][lay].rearrange("b (t p) h d -> p (b t) (h d)", p=P)
                pool.dma_start(Vc.rearrange("p b t f -> p (b t) f"), src).then_inc(sig("v_landed"), 16)

            def keys(lay):
                src = a["cache_mem_k"][lay].rearrange("b (t p) h d -> p (b t) (h d)", p=P)
                pool.dma_start(Kc.rearrange("p b t f -> p (b t) f"), src).then_inc(sig("k_landed"), 16)

            def kv_out(lay):
                pool.wait_ge(sig("kv_rows"), lay + 1)
                for name, c0 in (("p_cache_mem_k", 0), ("p_cache_mem_v", DX)):
                    pool.dma_start(out[name][lay, 0].rearrange("(t p) h d -> p t (h d)", p=P), kv[:, :, c0:c0 + DX]).then_inc(sig(f"cache_out{lay}"), 16)

            kv_out(0)
            pool.wait_ge(sig("hist_done"), 1)
            values(0)
            pool.wait_ge(sig("tails_ready"), 1)
            pool.dma_start(out["p_state_conv"][0, 0], tails[0:PADT, :]).then_inc(sig("conv_out"), 16)
            pool.dma_start(out["s_state_conv"][0, :, PADT - 1, :], tails[PADT:PADT + NS, :]).then_inc(sig("conv_out"), 16)
            keys(0)
            pool.wait_ge(sig("state_landed"), 16)
            pool.wait_ge(sig("s_rows"), 1)
            st = state.rearrange("p (b h) v -> p b h v", h=H)
            for h in range(H):
                if h >= 2:
                    pool.wait_ge(bank_full[bank_of[("outer", h - 2, 1)][0]], bank_of[("outer", h - 2, 1)][1] + 1)
                ud = udiag[0:NS, h % 2, :].rearrange("p (b v) -> p b v", b=NS)
                pool.tensor_tensor(ud, urow[0:NS, h, :].unsqueeze(1).to_broadcast([NS, NS, P]),
                                   ident[0:NS, 0:NS].unsqueeze(2).to_broadcast([NS, NS, P]), ALU.mult).then_inc(sig("udiag_ready"), 1)
                pool.tensor_tensor(st[:, :, h, :], st[:, :, h, :], s_eg[:, h, :].unsqueeze(2).to_broadcast([P, NS, P]), ALU.mult).then_inc(sig("state_decayed"), 1)
            pool.wait_ge(sig("state_new"), H)
            pool.dma_start(out["s_state_gdn"][0].rearrange("b h k v -> k (b h) v"), state).then_inc(sig("state_out"), 16)
            for n in range(TT):
                pool.wait_ge(sig("A_ready"), n + 1)
                for s in range(1, 7):
                    if s > 1 or n:
                        prev = ("Y", n, s - 1, 1) if s > 1 else ("Y", n - 1, 6, 1)
                        pool.wait_ge(bank_full[bank_of[prev][0]], bank_of[prev][1] + 1)
                    if s == 1 and n:
                        pool.wait_ge(sig("w_done"), n)
                    pool.tensor_tensor(AmT, AT, stage_mask[:, s, :].unsqueeze(1).to_broadcast([P, H, P]), ALU.mult).then_inc(sig("AmT_ready"), 1)
            pool.wait_ge(sig("S_ready"), TT)
            pool.dma_start(out["p_state_gdn"][0, 0].rearrange("h k v -> k h v"), S).then_inc(sig("pstate_out"), 16)
            pool.wait_ge(sig("state_out"), 16)
            pool.wait_ge(sig("attn_done"), 1)
            pool.sem_inc(sig("gdn_lent_back"), 1)
            wait_unit_used(pool, UNITS - 1)
            pool.wait_ge(sig("pstate_out"), 16)
            pool.dma_start(memrows[1], a["mem_prompt"][0].rearrange("(t p) d -> p t d", p=P)).then_inc(sig("mem1_landed"), 16)
            pool.dma_start(bsrow[0:GB, :], a["b_b_s"][0]).then_inc(sig("bs_landed"), 16)
            pool.wait_ge(sig("x_ready"), KT)
            pool.dma_start(wsrows, a["b_w_s"][0].rearrange("g i j -> i g j")).then_inc(sig("ws_landed"), 16)
            pool.wait_ge(sig("mem_in"), 2)
            kv_out(1)
            values(1)
            keys(1)
            pool.wait_ge(sig("vtok_ready"), 1)
            pool.dma_start(out["s_sgu_v"][0].rearrange("b t d -> (b t) d"), vtok[0:NS, 2, :]).then_inc(sig("sgu_out"), 16)
            pool.wait_ge(sig("attn_done"), 2)
            pool.sem_inc(sig("attn1_lent_back"), 1)
            pool.wait_ge(sig("mix_ready"), 2)
            pool.dma_start(router, a["moe_router"][0].rearrange("(k p) e -> p k e", p=P)).then_inc(sig("router_landed"), 16)
            pool.iota(iota8, [[1, NE]], base=0, channel_multiplier=0, allow_small_or_imprecise_dtypes=True)
            pool.iota(slot_iota, [[1, P]], base=0, channel_multiplier=0, allow_small_or_imprecise_dtypes=True)
            step(pool.memset(valid, 1.0))
            step(pool.affine_select(out=valid[:, 2:3], in_=valid[:, 2:3], pattern=[[0, 1]], compare_op=ALU.is_ge, fill=0.0, base=NS - 1, channel_multiplier=-1))
            pool.sem_inc(sig("route_consts"), 1)

        @block.scalar
        def _(act):
            step = Chain(act, "act_step")
            act.dma_start(xrows[:, 0:TT, :], a["x_prompt"][0].rearrange("(t p) d -> p t d", p=P)).then_inc(sig("x_landed"), 16)
            act.dma_start(xrows[0:NS, TT, :], a["x_sample"].rearrange("b t d -> (b t) d")).then_inc(sig("x_landed"), 16)
            conv_rows = a["a_conv_w"][0].rearrange("j (c p) -> (j c) p", p=P)
            act.dma_start(prow[0:72, 0, :], conv_rows).then_inc(sig("params_landed"), 16)
            act.dma_start(prow[72:78, 0, :], a["b_ln_g"][0].rearrange("(k p) -> k p", p=P)).then_inc(sig("params_landed"), 16)
            act.dma_start(prow[78:84, 0, :], a["b_ln_b"][0].rearrange("(k p) -> k p", p=P)).then_inc(sig("params_landed"), 16)
            act.dma_start(prow[84:85, 0, :], a["a_norm_w"]).then_inc(sig("params_landed"), 16)
            for w, name in enumerate(("ln1_g", "ln1_b", "ln2_g", "ln2_b")):
                act.dma_start(prow[16 * w:16 * w + 16, 1, :], a[name].rearrange("l (k p) -> (l k) p", p=P)).then_inc(sig("params_landed"), 16)

            def mem_kv(lay):
                for mt in range(MT):
                    src = take(act, "kv", lay, mt)
                    if mt == 0 and lay:
                        act.wait_ge(sig("cache_out0"), 32)
                    ins = free(act.activation(kv[:, mt, :], src, ACT.Copy), "kv", lay, mt)
                bank, before = bank_of[("kv", lay, MT - 1)]
                act.wait_ge(bank_free[bank], before + 1)
                bank, before = bank_of[("kv", lay, 0)]
                act.wait_ge(bank_free[bank], before + 1)
                act.sem_inc(sig("kv_rows"), 1)

            mem_kv(0)
            act.wait_ge(sig("pre_zero"), 1)
            for c in range(CT):
                free(act.activation(pre[:, c, PADT:], take(act, "proj", 0, c)[:, 0:NT], ACT.Copy), "proj", 0, c)
                bank, before = bank_of[("proj", 0, c)]
                act.wait_ge(bank_free[bank], before + 1)
                act.activation(qkv[:, c, 0:SEQ], pre[:, c, 0:SEQ], ACT.Copy, scale=conv_col[:, 0, c:c + 1]).then_inc(sig("conv_begun"), 1)
            for c in range(CT):
                act.wait_ge(sig("conv_sum"), c + 1)
                act.activation(qkv[:, c, 0:SEQ], qkv[:, c, 0:SEQ], ACT.Silu).then_inc(sig("conv_silu"), 1)
            act.wait_ge(sig("conv_sample"), 1)
            act.activation(qkv[:, :, SEQ:], qkv[:, :, SEQ:], ACT.Silu).then_inc(sig("conv_silu"), 1)
            act.wait_ge(sig("conv_silu"), CT + 1)
            for half in range(2):
                act.activation(sqk[half], qkv[:, H * half:H * half + H, :], ACT.Square).then_inc(sig("qk_squared"), 1)

            def silu_z(h):
                free(act.activation(zs[:, h, :], take(act, "proj", 0, CT + h)[:, 0:NT], ACT.Silu), "proj", 0, CT + h)

            for h in range(3):
                silu_z(h)
            for half in range(2):
                for h in range(H):
                    src = take(act, "norm", H * half + h)
                    free(act.activation(sqk[half][:, h, :], src[:, 0:NT], ACT.Sqrt, bias=eps_rms), "norm", H * half + h)
                for h in range(H):
                    bank, before = bank_of[("norm", H * half + h)]
                    act.wait_ge(bank_free[bank], before + 1)
                act.sem_inc(sig("qk_root"), 1)
                for h in ((3,), (4, 5))[half]:
                    silu_z(h)
            act.wait_ge(sig("gate_abs"), 1)
            step(act.activation(gate_e, gate_n, ACT.Exp))
            act.activation(gate_l, gate_e, ACT.Ln, bias=1.0).then_inc(sig("gate_log"), 1)
            act.activation(gpar[0:H, 2:3], gpar[0:H, 0:1], ACT.Exp).then_inc(sig("gate_log"), 1)
            free(act.activation(beta[0:H, :], take(act, "projx", 0, "b")[0:H, 0:NT], ACT.Exp, scale=-1.0), "projx", 0, "b")
            act.wait_ge(bank_free[bank_of[("projx", 0, "b")][0]], bank_of[("projx", 0, "b")][1] + 1)
            act.sem_inc(sig("beta_exp"), 1)

            def attend(lay):
                for h in range(HX):
                    act.wait_ge(sig("attn_max_ready"), HX * lay + h + 1)
                    if h == 0 and lay == 0:
                        act.wait_ge(sig("conv_out"), 48)
                    src = take(act, "score", lay, h).rearrange("p (t m) -> p t m", t=TT)
                    for tt in range(TT):
                        n = TT * h + tt
                        ins = act.activation(p_att[:, n, :], src[:, tt, :], ACT.Exp, bias=attn_max[:, n:n + 1], scale=DH ** -0.5, accum_out=attn_sum[:, n:n + 1])
                        if tt == TT - 1:
                            free(ins, "score", lay, h)
                for h in range(HX):
                    bank, before = bank_of[("score", lay, h)]
                    act.wait_ge(bank_free[bank], before + 1)
                act.sem_inc(sig("attn_exp"), 1)
                for h in range(HX):
                    free(act.activation(pT_att[:, h].rearrange("p m t -> p (m t)"), take(act, "pT", lay, h), ACT.Copy), "pT", lay, h)
                act.wait_ge(sig("qk_normed"), 2)
                for b in range(NS):
                    src = take(act, "cacheT", lay, b)
                    if b >= 2:
                        act.wait_ge(sig("sscored"), NS * lay + b - 1)
                    free(act.activation(KTs[:, b % 2].rearrange("p k m -> p (k m)"), src, ACT.Copy), "cacheT", lay, b)
                act.wait_ge(sig("ss_max"), lay + 1)
                src = take(act, "sscore", lay)
                free(act.activation(ps_att[0:4 * NS, :], src[0:4 * NS, 0:MEM], ACT.Exp, bias=attn_max[0:4 * NS, 0:1], scale=DH ** -0.5, accum_out=attn_sum[0:4 * NS, 0:1]), "sscore", lay)
                act.wait_ge(bank_free[bank_of[("sscore", lay)][0]], bank_of[("sscore", lay)][1] + 1)
                act.sem_inc(sig("ss_exp"), 1)

            attend(0)
            src = take(act, "sgate")
            act.activation(s_eg.rearrange("p h b -> p (h b)"), src[:, 0:H * NS], ACT.Exp).then_inc(sig("s_eg_ready"), 1)
            for n in range(TT):
                act.wait_ge(sig("diff_ready"), n + 1)
                act.activation(attnT, attnT, ACT.Exp).then_inc(sig("decay_exp"), 1)
                for i in range(2):
                    free(act.activation(pair(Y, i), take(act, "gb", n, i)[:, 0:3 * P], ACT.Exp), "gb", n, i)
                    bank, before = bank_of[("gb", n, i)]
                    act.wait_ge(bank_free[bank], before + 1)
                act.sem_inc(sig("q_scale"), 1)
                act.wait_ge(sig("tok_ready"), n + 1)
                act.activation(tok_eg, tok_g, ACT.Exp)
                act.activation(tok_kd, tok_kd, ACT.Exp)
                act.activation(eglast, glast, ACT.Exp).then_inc(sig("tok_exp"), 1)
                for s in range(1, 7):
                    for i in range(2):
                        src = take(act, "Y", n, s, i)[:, 0:3 * P]
                        if s == 1:
                            act.wait_ge(sig("q_scaled"), n + 1)
                        free(act.activation(pair(Y, i), src, ACT.Copy), "Y", n, s, i)
                if n:
                    for i in range(2):
                        src = take(act, "wT", n, i)[:, 0:3 * P]
                        free(act.activation(pair(AmT, i), src, ACT.Copy, scale=-1.0), "wT", n, i)
                for i in range(2):
                    src = take(act, "vnew", n, i)[:, 0:3 * P]
                    free(act.activation(pair(Y, i), src, ACT.Copy), "vnew", n, i)
                for i in range(2):
                    src = take(act, "o", n, i)[:, 0:3 * P].rearrange("p (h t) -> p h t", h=3)
                    free(act.activation(mixT[:, 3 * i:3 * i + 3, n * P:(n + 1) * P], src, ACT.Copy), "o", n, i)
            for i in range(2):
                bank, before = bank_of[("o", TT - 1, i)]
                act.wait_ge(bank_free[bank], before + 1)
            act.wait_ge(sig("s_mixed"), 1)
            act.wait_ge(sig("S_ready"), TT)
            act.activation(sq[:, 0:H, :], mixT[:, 0:H, :], ACT.Square).then_inc(sig("o_squared"), 1)
            for h in range(H):
                free(act.activation(sq[:, h, :], take(act, "rms", h)[:, 0:NT], ACT.Sqrt, bias=eps_rms, scale=1.0 / P), "rms", h)
            for h in range(H):
                bank, before = bank_of[("rms", h)]
                act.wait_ge(bank_free[bank], before + 1)
            act.sem_inc(sig("o_root"), 1)

            def norm(lay, which, first):
                for q in range(KT // 2):
                    act.wait_ge(sig("ln_centered"), first + q + 1)
                    k = slice(2 * q, 2 * q + 2)
                    act.activation(sq[:, k, :], yT[:, k, :], ACT.Square).then_inc(sig("ln_squared"), 1)
                free(act.activation(rstd, take(act, "ln_var", lay, which)[:, 0:NT], ACT.Sqrt, bias=eps_ln, scale=1.0 / D), "ln_var", lay, which)
                for q in range(KT // 2):
                    act.wait_ge(sig("ln_scaled"), first + q + 1)
                    for k in (2 * q, 2 * q + 1):
                        ins = act.activation(xT[:, k, :], yT[:, k, :], ACT.Identity, bias=ln_col[:, 2 * which + 1, lay, k:k + 1], scale=ln_col[:, 2 * which, lay, k:k + 1])
                    ins.then_inc(sig("x_ready"), 1)

            norm(0, 0, LN_PARTS[0, 0])
            for i in range(2):
                act.wait_ge(sig("x_ready"), 2 * i + 2)
                act.activation(split_x[0][:, 4 * i:4 * i + 4, :], xT[:, 4 * i:4 * i + 4, :], ACT.Copy).then_inc(sig("x_hi"), 1)
            act.wait_ge(sig("gdn_lent_back"), 1)
            for u in range(UNITS):
                if u >= SPLITS:
                    kind, c, i = ORDER[u - SPLITS]
                    if kind == "gate":
                        for f in (2 * i, 2 * i + 1):
                            n = 4 * c + f
                            src = take(act, "gate", c, f)
                            if n >= 2:
                                act.wait_ge(sig("silu_read"), n - 1)
                            free(act.activation(silu_t[:, f % 2, :], src[:, 0:NT], ACT.Silu), "gate", c, f)
                    wait_unit_used(act, u - SPLITS)
                half = DENSE_HALVES[u % HALVES]
                act.wait_ge(half_landed[half], 16 * (u // HALVES + 1))
                act.activation(split_w[:, u % SPLITS, 0, :], halves[half], ACT.Copy).then_inc(sig("unit_hi"), 1)
            norm(0, 1, LN_PARTS[0, 1])
            mem_kv(1)
            def gelu(c):
                dst_t = uT[:, c, :] if c < GB else vT[:, c - GB, :]
                free(act.activation(dst_t, take(act, "proj", 1, c)[:, 0:NT], ACT.Gelu_apprx_tanh), "proj", 1, c)

            for c in PROJ_B[:9]:
                gelu(c)
            act.wait_ge(sig("ws_ready"), 1)
            for q in range(GB // 2):
                act.wait_ge(sig("ln_centered"), LN_PARTS["v"] + q + 1)
                k = slice(2 * q, 2 * q + 2)
                act.activation(sq[:, k, :], vT[:, k, :], ACT.Square).then_inc(sig("ln_squared"), 1)
            gelu(PROJ_B[9])
            gelu(PROJ_B[10])
            free(act.activation(rstd, take(act, "vvar")[:, 0:NT], ACT.Sqrt, bias=eps_ln, scale=1.0 / D_B), "vvar")
            gelu(PROJ_B[11])
            for q in range(GB // 2):
                act.wait_ge(sig("ln_scaled"), LN_PARTS["v"] + q + 1)
                for k in (2 * q, 2 * q + 1):
                    ins = act.activation(vT[:, k, :], vT[:, k, :], ACT.Identity, bias=bln_b[:, k:k + 1], scale=bln_g[:, k:k + 1])
            ins.then_inc(sig("v_ready"), 1)
            attend(1)
            norm(1, 0, LN_PARTS[1, 0])
            act.wait_ge(sig("res_ready"), 3)
            act.dma_start(ln_bc[:, 0, :], a["ln2_g"][DEPTH - 1].partition_broadcast(P)).then_inc(sig("ln_bc_landed"), 16)
            act.dma_start(ln_bc[:, 1, :], a["ln2_b"][DEPTH - 1].partition_broadcast(P)).then_inc(sig("ln_bc_landed"), 16)
            act.wait_ge(sig("cache_out1"), 32)
            act.wait_ge(sig("sgu_out"), 16)
            for n in range(2 * TT):
                tt, kg = divmod(n, 2)
                act.activation(split_xt[:, tt, 0, 512 * kg:512 * kg + 512], take(act, "x1tok", n), ACT.Copy).then_inc(sig("rows_hi"), 1)
            for n in range(2):
                act.activation(split_xt[0:NS, TT, 0, 512 * n:512 * n + 512], take(act, "x1tokS", n)[0:NS, :], ACT.Copy).then_inc(sig("rows_hi"), 1)
            act.wait_ge(sig("top_diff"), 1)
            act.activation(dtop, dtop, ACT.Exp).then_inc(sig("top_exp"), 1)

            def unit_hi(t, u):
                if t is not None:
                    act.wait_ge(sig("units_used"), t * UNITS + (UNITS + u - SPLITS + 1))
                half = EXPERT_HALVES[u % HALVES]
                act.wait_ge(half_landed[half], (0 if t is None else t * 16 * NG) + 16 * (NG + u // HALVES + 1))
                act.activation(split_w[:, u % SPLITS, 0, :], halves[half], ACT.Copy).then_inc(sig("unit_hi"), 1)

            def hidden_T(t, c):
                act.wait_ge(sig("T_done"), t * NG + (c + 1))
                act.activation(split_he[:, c % 2, 0].rearrange("p f s -> p (f s)"), ps[:, 4 + c % 2, :], ACT.Copy).then_inc(sig("hT_hi"), 1)

            def gathered_hi(t):
                for n in range(2):
                    act.wait_ge(sig("gathered"), t * 2 + (n + 1))
                    act.activation(split_xe[:, 0, 4 * n:4 * n + 4, :].rearrange("p k s -> p (k s)"), ps[:, 1 + 2 * n, :], ACT.Copy).then_inc(sig("xeT_hi"), 1)

            def y_hi(t):
                act.wait_ge(sig("units_used"), t * UNITS + 2 * UNITS)
                act.wait_ge(sig("selT_ready"), t * 2 + 2)
                act.activation(split_y[:, 0, :].rearrange("p (a b) -> p a b", a=2), ps[:, 6:8, :], ACT.Copy, scale=gate_slot).then_inc(sig("y_hi"), 1)

            def expert(t):
                for u in range(SPLITS, UNITS):
                    kind, c, i = ORDER[u - SPLITS]
                    if (kind, i) == ("gate", 1):
                        act.wait_ge(sig("units_used"), t * UNITS + (UNITS + u - SPLITS + 1))
                        act.wait_ge(sig("h_ready"), t * NG + (c - 2 + NG + 1))
                        act.activation(hsil[:, c % 2, :], ps[:, c % 2, :], ACT.Silu).then_inc(sig("silu_ready"), 1)
                        if c:
                            hidden_T(t, c - 1)
                    unit_hi(t, u)
                hidden_T(t, NG - 1)

            act.wait_ge(sig("attn1_lent_back"), 1)
            for u in range(SPLITS):
                unit_hi(None, u)
            gathered_hi(0)
            with act.Fori(0, NE - 1) as e:
                expert(e)
                unit_hi(e + 1, 0)
                gathered_hi(e + 1)
                unit_hi(e + 1, 1)
                y_hi(e)
                unit_hi(e + 1, 2)
            expert(NE - 1)
            y_hi(NE - 1)
            runs = act.value_load(turn[0:1, 2 * NE:2 * NE + 1], min_val=NE, max_val=3 * NE)
            with act.If(runs > NE):
                for chunk in (1, 2):
                    with act.Fori(0, NE) as e:
                        n_tok = act.value_load(counts[0:1, bass.ds(e, 1)], min_val=0, max_val=NT)
                        t = act.value_load(turn[0:1, bass.ds(e + (chunk - 1) * NE, 1)], min_val=NE, max_val=3 * NE)
                        with act.If(n_tok > chunk * P):
                            for u in range(SPLITS):
                                unit_hi(t, u)
                            gathered_hi(t)
                            expert(t)
                            y_hi(t)
            for tt in range(3):
                np_ = P if tt < 2 else NS
                act.wait_ge(sig("fin_var"), tt + 1)
                act.activation(rs3[0:np_, tt:tt + 1], mv[0:np_, tt, 1:2], ACT.Sqrt, bias=eps_ln[0:np_, :]).then_inc(sig("fin_root"), 1)
            for tt in range(3):
                act.wait_ge(sig("fin_ready"), tt + 1)
                dstp = out["y_prompt"][0, tt * P:(tt + 1) * P, :] if tt < 2 else out["y_sample"].rearrange("b t d -> (b t) d")
                act.dma_start(dstp, acc[:, tt, :] if tt < 2 else acc_st[0:NS, :]).then_inc(sig("y_out"), 16)

        @block.vector
        def _(dve):
            step = Chain(dve, "dve_step")

            def tt_(o, x0, x1, op):
                return dve.tensor_tensor(o, x0, x1, op)

            def settle(name, *uses):
                for u in uses:
                    bank, before = bank_of[u]
                    dve.wait_ge(bank_free[bank], before + 1)
                dve.sem_inc(sig(name), 1)

            for n in range(2 * TT):
                tt, kg = divmod(n, 2)
                src = take(dve, "x", n).rearrange("p (k t) -> p k t", k=4)
                free(dve.tensor_copy(xT[:, 4 * kg:4 * kg + 4, tt * P:(tt + 1) * P], src), "x", n)
            free(dve.tensor_copy(xT[:, :, SEQ:NT], take(dve, "xs")[:, 0:KT * NS].rearrange("p (k t) -> p k t", k=KT)), "xs")
            settle("x_in", *[("x", n) for n in range(2 * TT)], ("xs",))
            free(dve.tensor_copy(pcol1, take(dve, "params", 0)[:, 0:85]), "params", 0)
            free(dve.tensor_copy(pcol2, take(dve, "params", 1)[:, 0:64]), "params", 1)
            settle("params_in", ("params", 0), ("params", 1))

            def mem_rows(lay):
                for n in range(2 * MT):
                    tt, kg = divmod(n, 2)
                    src = take(dve, "mem", lay, n).rearrange("p (k t) -> p k t", k=4)
                    free(dve.tensor_copy(memT[:, 4 * kg:4 * kg + 4, tt * P:(tt + 1) * P], src), "mem", lay, n)
                settle("mem_in", *[("mem", lay, n) for n in range(2 * MT)])
                free(dve.tensor_copy(kT.rearrange("p a b -> p (a b)"), take(dve, "kT", lay)), "kT", lay)
                settle("kT_ready", ("kT", lay))

            mem_rows(0)
            hs4 = hs.rearrange("p c (b j) -> p c b j", j=CW)
            for n in range(5):
                nt_ = min(4, CT - 4 * n)
                src = take(dve, "hist", n)[:, 0:nt_ * NS * PADT].rearrange("p (c b j) -> p c b j", c=nt_, b=NS)
                for q in range(nt_):
                    ins = dve.tensor_copy(hs4[:, 4 * n + q, :, 0:PADT], src[:, q])
                free(ins, "hist", n)
            settle("hist_done", *[("hist", n) for n in range(5)])
            for c in range(CT):
                dve.wait_ge(sig("conv_begun"), c + 1)
                for j in range(1, CW):
                    ins = dve.scalar_tensor_tensor(qkv[:, c, 0:SEQ], pre[:, c, j:j + SEQ], conv_col[:, j, c:c + 1], qkv[:, c, 0:SEQ], ALU.mult, ALU.add)
                    if j < CW - 1:
                        step(ins)
                ins.then_inc(sig("conv_sum"), 1)
            step(dve.tensor_copy(hs4[:, :, :, PADT], pre[:, :, PADT + SEQ:]))
            scr = mixT.rearrange("p a b -> p (a b)")[:, 1400:1400 + CT * NS].rearrange("p (c b) -> p c b", c=CT)
            smp = qkv[:, :, SEQ:]
            for j in range(CW):
                w = conv_col[:, j, :].unsqueeze(2).to_broadcast([P, CT, NS])
                step(tt_(smp if j == 0 else scr, hs4[:, :, :, j], w, ALU.mult))
                if j:
                    step(tt_(smp, smp, scr, ALU.add))
            dve.sem_inc(sig("conv_sample"), 1)
            for half in range(2):
                dve.wait_ge(sig("qk_root"), half + 1)
                step(dve.reciprocal(sqk[half], sqk[half]))
                v = qkv[:, H * half:H * half + H, :]
                step(dve.scalar_tensor_tensor(v.rearrange("p a b -> p (a b)"), v.rearrange("p a b -> p (a b)"), P ** -0.5 if half == 0 else 1.0,
                                              sqk[half].rearrange("p a b -> p (a b)"), ALU.mult, ALU.mult))
                dve.sem_inc(sig("qk_normed"), 1)
            dve.wait_ge(sig("gpar_landed"), 32)
            step(free(dve.tensor_scalar(gate_a, take(dve, "projx", 0, "a")[0:H, 0:NT], gpar[0:H, 1:2], None, ALU.add), "projx", 0, "a")
                 if False else dve.tensor_scalar(gate_a, take(dve, "projx", 0, "a")[0:H, 0:NT], gpar[0:H, 1:2], None, ALU.add))
            free(dve.scalar_tensor_tensor(gate_n, gate_a, -1.0, gate_a, ALU.mult, ALU.min), "projx", 0, "a")
            settle("gate_abs", ("projx", 0, "a"))
            dve.wait_ge(sig("gate_log"), 2)
            step(dve.scalar_tensor_tensor(gate_g, gate_a, 0.0, gate_l, ALU.max, ALU.add))
            step(dve.tensor_scalar(gate_g, gate_g, gpar[0:H, 2:3], -1.0, ALU.mult, ALU.mult))
            for n in range(TT):
                dve.tensor_tensor_scan(gc[0:H, n * P:(n + 1) * P], ones[0:H, :], gate_g[:, n * P:(n + 1) * P], 0.0, ALU.mult, ALU.add)
            step(dve.tensor_copy(gc[0:H, SEQ:], gate_g[:, SEQ:]))
            dve.wait_ge(sig("beta_exp"), 1)
            step(dve.tensor_scalar(beta[0:H, :], beta[0:H, :], 1.0, None, ALU.add))
            step(dve.reciprocal(beta[0:H, :], beta[0:H, :]))
            dve.sem_inc(sig("gates_ready"), 1)
            for i in range(2):
                free(dve.tensor_copy(xq[:, i, :], take(dve, "projx", 0, i)[:, 0:NT]), "projx", 0, i)
            settle("xq_ready", ("projx", 0, 0), ("projx", 0, 1))
            nr = PADT + NS
            for n in range(5):
                nt_ = min(4, CT - 4 * n)
                free(dve.tensor_copy(tails[0:nr, 4 * n * P:(4 * n + nt_) * P], take(dve, "tail", n)[0:nr, 0:nt_ * P]), "tail", n)
            settle("tails_ready", *[("tail", n) for n in range(5)])
            def attend(lay):
                for h in range(HX):
                    src = take(dve, "score", lay, h).rearrange("p (t m) -> p t m", t=TT)
                    step(dve.tensor_reduce(attn_max[:, TT * h:TT * h + TT], src, AX_X, ALU.max))
                    dve.tensor_scalar(attn_max[:, TT * h:TT * h + TT], attn_max[:, TT * h:TT * h + TT], -DH ** -0.5, None, ALU.mult).then_inc(sig("attn_max_ready"), 1)
                dve.wait_ge(sig("attn_exp"), lay + 1)
                step(dve.reciprocal(attn_sum, attn_sum))
                step(tt_(p_att, p_att, attn_sum.unsqueeze(2).to_broadcast([P, 2 * HX, MEM]), ALU.mult))
                dve.sem_inc(sig("attn_p"), 1)
                step(dve.memset(qpad, 0.0))
                for h in range(HX):
                    r = slice(DH * (h % 2), DH * (h % 2) + DH)
                    q0 = y0 + 1600 + (h // 2) * NS * 4 * NS
                    diag = sb[r, q0 + h:q0 + h + 36 * (NS - 1) + 1:36]
                    ins = dve.tensor_copy(diag, xq[r, h // 2, SEQ:NT])
                step(ins)
                dve.sem_inc(sig("qpad_ready"), 1)
                for n in range(2):
                    free(dve.tensor_copy(mixT[:, 6 + n, 0:SEQ], take(dve, "pv", lay, n)[:, 0:SEQ]), "pv", lay, n)
                r = slice(0, 4 * NS)
                src = take(dve, "sscore", lay)
                step(dve.tensor_reduce(attn_max[r, 0:1], src[r, 0:MEM], AX_X, ALU.max))
                step(dve.tensor_scalar(attn_max[r, 0:1], attn_max[r, 0:1], -DH ** -0.5, None, ALU.mult))
                dve.sem_inc(sig("ss_max"), 1)
                dve.wait_ge(sig("ss_exp"), lay + 1)
                step(dve.reciprocal(attn_sum[r, 0:1], attn_sum[r, 0:1]))
                step(dve.tensor_scalar(ps_att[r, :], ps_att[r, :], attn_sum[r, 0:1], None, ALU.mult))
                dve.sem_inc(sig("ss_p"), 1)
                free(dve.tensor_copy(pTs.rearrange("p a b -> p (a b)"), take(dve, "spT", lay)[:, 0:MT * 4 * NS]), "spT", lay)
                settle("ss_pT", ("spT", lay))
                src = take(dve, "spv", lay)[:, 0:XT_ * NS * 4].rearrange("p (k b h) -> p k b h", k=XT_, h=4)
                for h in range(HX):
                    r = slice(DH * (h % 2), DH * (h % 2) + DH)
                    ins = dve.tensor_copy(mixT[r, 6 + h // 2, SEQ:NT], src[r, h // 2, :, h])
                free(ins, "spv", lay)
                settle("attn_done", ("spv", lay), ("pv", lay, 0), ("pv", lay, 1))

            attend(0)
            q_s, k_s, v_s = (qkv[:, H * i:H * i + H, SEQ:] for i in range(3))
            src = take(dve, "sgate")
            dve.wait_ge(sig("s_eg_ready"), 1)
            free(dve.tensor_copy(s_be, src[:, H * NS:2 * H * NS].rearrange("p (h b) -> p h b", h=H)), "sgate")
            step(tt_(s_kq, q_s, k_s, ALU.mult))
            dve.sem_inc(sig("s_prod"), 1)
            rd = take(dve, "sread")[:, 0:2 * H * NS].rearrange("p (h b r) -> p h b r", h=H, r=2)
            step(tt_(s_sk, rd[:, :, :, 1], s_eg, ALU.mult))
            step(free(tt_(s_o, rd[:, :, :, 0], s_eg, ALU.mult), "sread") if False else tt_(s_o, rd[:, :, :, 0], s_eg, ALU.mult))
            step(tt_(s_u, v_s, s_sk, ALU.subtract))
            step(tt_(s_u, s_u, s_be, ALU.mult))
            dot = take(dve, "sdot")[:, 0:H * NS].rearrange("p (h b) -> p h b", h=H)
            step(tt_(s_sk, dot, s_u, ALU.mult))
            free(tt_(mixT[:, 0:H, SEQ:], s_o, s_sk, ALU.add), "sread")
            settle("s_mixed", ("sread",))
            bank, before = bank_of[("sdot",)]
            dve.sem_inc(bank_free[bank], 1)
            for n in range(2):
                free(dve.tensor_copy(krow[0:NS, 3 * n:3 * n + 3, :].rearrange("p a b -> p (a b)"), take(dve, "krow", n)[0:NS, 0:3 * P]), "krow", n)
            for n in range(2):
                free(dve.tensor_copy(urow[0:NS, 3 * n:3 * n + 3, :].rearrange("p a b -> p (a b)"), take(dve, "urow", n)[0:NS, 0:3 * P]), "urow", n)
            settle("s_rows", ("krow", 0), ("krow", 1), ("urow", 0), ("urow", 1))
            st = state.rearrange("p (b h) v -> p b h v", h=H)
            for h in range(H):
                dve.wait_ge(sig("state_decayed"), h + 1)
                for n in range(2):
                    half = st[:, 4 * n:4 * n + 4, h, :]
                    free(tt_(half, half, take(dve, "outer", h, n).rearrange("p (b v) -> p b v", b=4), ALU.add), "outer", h, n)
                settle("state_new", ("outer", h, 0), ("outer", h, 1))
            for n in range(TT):
                chunk = slice(n * P, (n + 1) * P)
                src = take(dve, "gcol", n)
                dve.tensor_copy(tok_g, src[:, 0:H])
                free(dve.tensor_copy(tok_b, src[:, H:2 * H]), "gcol", n)
                for i in range(2):
                    gbp = take(dve, "gb", n, i)[:, 0:3 * P].rearrange("p (h t) -> p h t", h=3)
                    dve.tensor_copy(glast[:, 3 * i:3 * i + 3], gbp[:, :, P - 1])
                bank, before = bank_of[("gcol", n)]
                dve.wait_ge(bank_free[bank], before + 1)
                for i in range(2):
                    gbp = take(dve, "gb", n, i)[:, 0:3 * P].rearrange("p (h t) -> p h t", h=3)
                    for h in range(3):
                        ins = dve.tensor_scalar(attnT[:, 3 * i + h, :], gbp[:, h, :], tok_g[:, 3 * i + h:3 * i + h + 1], 0.0, ALU.subtract, ALU.min)
                step(ins)
                dve.sem_inc(sig("diff_ready"), 1)
                step(tt_(tok_kd, glast, tok_g, ALU.subtract))
                dve.sem_inc(sig("tok_ready"), 1)
                dve.wait_ge(sig("decay_exp"), n + 1)
                for i in range(2):
                    step(free(tt_(pair(AT, i), pair(attnT, i), take(dve, "bb", n, i)[:, 0:3 * P], ALU.mult), "bb", n, i) if False else tt_(pair(AT, i), pair(attnT, i), take(dve, "bb", n, i)[:, 0:3 * P], ALU.mult))
                    bank, before = bank_of[("bb", n, i)]
                    dve.sem_inc(bank_free[bank], 1)
                for i in range(2):
                    free(tt_(pair(AT, i), pair(AT, i), take(dve, "kk", n, i)[:, 0:3 * P], ALU.mult), "kk", n, i)
                settle("A_ready", ("kk", n, 0), ("kk", n, 1))
                step(tt_(XT, AT, stage_mask[:, 0, :].unsqueeze(1).to_broadcast([P, H, P]), ALU.mult))
                step(tt_(XT, ident.unsqueeze(1).to_broadcast([P, H, P]), XT, ALU.subtract))
                dve.sem_inc(sig("XT_ready"), 1)
                step(tt_(attnT, attnT, causalT.unsqueeze(1).to_broadcast([P, H, P]), ALU.mult))
                for i in range(2):
                    free(tt_(pair(attnT, i), pair(attnT, i), take(dve, "qk", n, i)[:, 0:3 * P], ALU.mult), "qk", n, i)
                dve.wait_ge(sig("q_scale"), n + 1)
                bank, before = bank_of[("qk", n, 1)]
                dve.wait_ge(bank_full[bank], before + 1)
                tt_(qkv[:, 0:H, chunk], qkv[:, 0:H, chunk], Y, ALU.mult).then_inc(sig("q_scaled"), 1)
                dve.wait_ge(sig("tok_exp"), n + 1)
                step(tt_(tok_beg, tok_b, tok_eg, ALU.mult))
                for i in range(2):
                    src = take(dve, "ktok", n, i)[:, 0:3 * P].rearrange("p (h t) -> p h t", h=3)
                    tt_(kdec[:, 3 * i:3 * i + 3, :], src, tok_kd[:, 3 * i:3 * i + 3].unsqueeze(2).to_broadcast([P, 3, P]), ALU.mult)
                    free(tt_(kbg[:, 3 * i:3 * i + 3, :], src, tok_beg[:, 3 * i:3 * i + 3].unsqueeze(2).to_broadcast([P, 3, P]), ALU.mult), "ktok", n, i)
                for i in range(2):
                    src = take(dve, "vtok", n, i)[:, 0:3 * P].rearrange("p (h t) -> p h t", h=3)
                    free(tt_(vb[:, 3 * i:3 * i + 3, :], src, tok_b[:, 3 * i:3 * i + 3].unsqueeze(2).to_broadcast([P, 3, P]), ALU.mult), "vtok", n, i)
                for i in range(2):
                    free(dve.tensor_copy(pair(X, i), take(dve, "xinit", n, i)[:, 0:3 * P]), "xinit", n, i)
                settle("X_ready", ("xinit", n, 0), ("xinit", n, 1))
                for s in range(1, 7):
                    if s < 6:
                        for i in range(2):
                            free(tt_(pair(X, i), pair(X, i), take(dve, "dX", n, s, i)[:, 0:3 * P], ALU.subtract), "dX", n, s, i)
                    for i in range(2):
                        free(tt_(pair(XT, i), pair(XT, i), take(dve, "dXT", n, s, i)[:, 0:3 * P], ALU.subtract), "dXT", n, s, i)
                for i in range(2):
                    src = take(dve, "S", n, i)[:, 0:3 * P]
                    if n == 0:
                        ins = free(dve.tensor_copy(pair(S, i), src), "S", n, i)
                    else:
                        for h in range(3):
                            ins = dve.scalar_tensor_tensor(S[:, 3 * i + h, :], S[:, 3 * i + h, :], eglast[:, 3 * i + h:3 * i + h + 1], src[:, h * P:(h + 1) * P], ALU.mult, ALU.add)
                        free(ins, "S", n, i)
                settle("S_ready", ("S", n, 0), ("S", n, 1))
            dve.wait_ge(sig("o_root"), 1)
            step(dve.reciprocal(sq[:, 0:H, :], sq[:, 0:H, :]))
            om = mixT[:, 0:H, :].rearrange("p a b -> p (a b)")
            step(tt_(om, om, sq[:, 0:H, :].rearrange("p a b -> p (a b)"), ALU.mult))
            step(dve.scalar_tensor_tensor(om, om, norm_w, zs.rearrange("p a b -> p (a b)"), ALU.mult, ALU.mult))
            dve.sem_inc(sig("mix_ready"), 1)

            def residual(lay):
                for c in range(KT):
                    free(dve.scalar_tensor_tensor(yT[:, c, :], xT[:, c, :], ALPHA, take(dve, "out", lay, c)[:, 0:NT], ALU.mult, ALU.add), "out", lay, c)
                    bank, before = bank_of[("out", lay, c)]
                    dve.wait_ge(bank_free[bank], before + 1)
                    if c:
                        step(tt_(mu, yT[:, 0, :] if c == 1 else mu, yT[:, c, :], ALU.add))
                dve.sem_inc(sig("res_ready"), 1)

            def center_and_scale(v, tiles, features, mean, var, first):
                src = take(dve, *mean)[:, 0:NT]
                for q in range(tiles // 2):
                    part = v[:, 2 * q:2 * q + 2, :]
                    dve.scalar_tensor_tensor(part, src.unsqueeze(1).to_broadcast([P, 2, NT]), -1.0 / features, part, ALU.mult, ALU.add).then_inc(sig("ln_centered"), 1)
                dve.wait_ge(sig("ln_centered"), first + tiles // 2)
                dve.sem_inc(bank_free[bank_of[mean][0]], 1)
                bank, before = bank_of[var]
                dve.wait_ge(bank_free[bank], before + 1)
                step(dve.reciprocal(rstd, rstd))
                for q in range(tiles // 2):
                    part = v[:, 2 * q:2 * q + 2, :]
                    tt_(part, part, rstd.unsqueeze(1).to_broadcast([P, 2, NT]), ALU.mult).then_inc(sig("ln_scaled"), 1)

            def norm(lay, which):
                center_and_scale(yT, KT, D, ("ln_mean", lay, which), ("ln_var", lay, which), LN_PARTS[lay, which])

            residual(0)
            norm(0, 0)
            for i in range(2):
                dve.wait_ge(sig("x_ready"), 2 * i + 2)
                dve.wait_ge(sig("x_hi"), i + 1)
                k = slice(4 * i, 4 * i + 4)
                tt_(split_x[1][:, k, :], xT[:, k, :], split_x[0][:, k, :].bitcast(F32), ALU.subtract).then_inc(sig("x_lo"), 1)

            def after_unit(kind, c, i):
                if kind == "up":
                    for f in (2 * i, 2 * i + 1):
                        bank, before = bank_of[("gate", c, f)]
                        dve.wait_ge(bank_free[bank], before + 1)
                        if f == 0 and c >= 2:
                            wait_unit_used(dve, ORDER.index(("down", c - 2, 1)))
                        free(tt_(hid_t[:, f % 2, :], silu_t[:, f % 2, :], take(dve, "up", c, f)[:, 0:NT], ALU.mult), "up", c, f)
                        bank, before = bank_of[("up", c, f)]
                        dve.wait_ge(bank_free[bank], before + 1)
                        dve.sem_inc(sig("silu_read"), 1)
                        step(dve.tensor_copy(split_h[:, c % 2, 0, f, :], hid_t[:, f % 2, :]))
                        tt_(split_h[:, c % 2, 1, f, :], hid_t[:, f % 2, :], split_h[:, c % 2, 0, f, :].bitcast(F32), ALU.subtract).then_inc(sig("hid_ready"), 1)
                if kind == "down":
                    for d in range(4 * i, 4 * i + 4):
                        src = take(dve, "down", c, d)[:, 0:NT]
                        if c == 0:
                            free(dve.scalar_tensor_tensor(yT[:, d, :], xT[:, d, :], ALPHA, src, ALU.mult, ALU.add), "down", c, d)
                        else:
                            free(tt_(yT[:, d, :], yT[:, d, :], src, ALU.add), "down", c, d)
                        if c == NG - 1:
                            bank, before = bank_of[("down", c, d)]
                            dve.wait_ge(bank_free[bank], before + 1)
                            if d:
                                step(tt_(mu, yT[:, 0, :] if d == 1 else mu, yT[:, d, :], ALU.add))

            for u in range(UNITS + SPLITS):
                if u >= SPLITS:
                    after_unit(*ORDER[u - SPLITS])
                if u < UNITS:
                    dve.wait_ge(sig("unit_hi"), u + 1)
                    tt_(split_w[:, u % SPLITS, 1, :], halves[DENSE_HALVES[u % HALVES]], split_w[:, u % SPLITS, 0, :].bitcast(F32), ALU.subtract).then_inc(sig("unit_split"), 1)
            dve.sem_inc(sig("res_ready"), 1)
            norm(0, 1)
            mem_rows(1)
            for n in range(2):
                free(tt_(wsT[:, 3 * n:3 * n + 3, :], take(dve, "wsT", n)[:, 0:3 * P].rearrange("p (g t) -> p g t", g=3), causalT.unsqueeze(1).to_broadcast([P, 3, P]), ALU.mult), "wsT", n)
            settle("ws_ready", ("wsT", 0), ("wsT", 1))
            center_and_scale(vT, GB, D_B, ("vmean",), ("vvar",), LN_PARTS["v"])
            for i in range(2):
                free(dve.tensor_copy(xq[:, i, :], take(dve, "projx", 1, i)[:, 0:NT]), "projx", 1, i)
            settle("xq_ready", ("projx", 1, 0), ("projx", 1, 1))
            for n in range(4):
                tt, half = divmod(n, 2)
                free(dve.tensor_copy(vtok[:, tt, 3 * P * half:3 * P * half + 3 * P], take(dve, "vtokT", n)[:, 0:3 * P]), "vtokT", n)
            for n in range(2):
                free(dve.tensor_copy(vtok[0:NS, 2, 3 * P * n:3 * P * n + 3 * P], take(dve, "vtokS", n)[0:NS, 0:3 * P]), "vtokS", n)
            settle("vtok_ready", *[("vtokT", n) for n in range(4)], ("vtokS", 0), ("vtokS", 1))
            free(dve.tensor_copy(rowcol, take(dve, "mixrow")[:, 0:2 * GB]), "mixrow")
            bank, before = bank_of[("mixrow",)]
            dve.wait_ge(bank_free[bank], before + 1)
            attend(1)
            for g in range(GB):
                dve.tensor_scalar(mixT[:, g, SEQ:], vT[:, g, SEQ:], rowcol[:, g:g + 1], rowcol[:, GB + g:GB + g + 1], ALU.mult, ALU.add)
                free(tt_(mixT[:, g, 0:SEQ], take(dve, "mixed", g)[:, 0:SEQ], uT[:, g, 0:SEQ], ALU.mult), "mixed", g)
                bank, before = bank_of[("mixed", g)]
                dve.wait_ge(bank_free[bank], before + 1)
            step(tt_(mixT[:, 0:GB, SEQ:], mixT[:, 0:GB, SEQ:], uT[:, :, SEQ:], ALU.mult))
            dve.sem_inc(sig("mix_ready"), 1)
            residual(1)
            norm(1, 0)
            step(dve.memset(lg, 0.0))
            src = take(dve, "logits")[:, 0:3 * NE].rearrange("p (t e) -> p t e", t=3)
            dve.tensor_copy(lg[:, 0:2, :], src[:, 0:2, :])
            step(dve.tensor_copy(lg[0:NS, 2, :], src[0:NS, 2, :]))
            bank, before = bank_of[("logits",)]
            dve.sem_inc(bank_free[bank], 1)
            for t in range(3):
                step(dve.max(mx8[:, t, :], lg[:, t, :]))
                step(dve.max_index(idx8[:, t, :], mx8[:, t, :], lg[:, t, :]))
            step(dve.tensor_copy(idxf, idx8[:, :, :]))
            step(tt_(dtop, mx8[:, :, 1], mx8[:, :, 0], ALU.subtract))
            dve.sem_inc(sig("top_diff"), 1)
            dve.wait_ge(sig("route_consts"), 1)
            for t in range(3):
                dve.tensor_scalar(oh1[:, t, :], iota8, idxf[:, t, 0:1], valid[:, t:t + 1], ALU.is_equal, ALU.mult)
                step(dve.tensor_scalar(oh2[:, t, :], iota8, idxf[:, t, 1:2], valid[:, t:t + 1], ALU.is_equal, ALU.mult))
            step(tt_(Msel, oh1, oh2, ALU.add))
            step(tt_(Mall, Msel[:, 0, :], Msel[:, 1, :], ALU.add))
            step(tt_(Mall, Mall, Msel[:, 2, :], ALU.add))
            dve.sem_inc(sig("sel_ready"), 1)
            for n in range(2 * TT):
                tt, kg = divmod(n, 2)
                src = take(dve, "x1tok", n)
                cols = slice(512 * kg, 512 * kg + 512)
                dve.wait_ge(sig("rows_hi"), n + 1)
                dve.tensor_scalar(acc[:, tt, cols], src, ALPHA, None, ALU.mult)
                free(tt_(split_xt[:, tt, 1, cols], src, split_xt[:, tt, 0, cols].bitcast(F32), ALU.subtract), "x1tok", n)
            for n in range(2):
                cols = slice(512 * n, 512 * n + 512)
                dve.wait_ge(sig("rows_hi"), 2 * TT + n + 1)
                free(tt_(split_xt[0:NS, TT, 1, cols], take(dve, "x1tokS", n)[0:NS, :], split_xt[0:NS, TT, 0, cols].bitcast(F32), ALU.subtract), "x1tokS", n)
            step(dve.tensor_scalar(acc_s, xT[:, :, SEQ:NT], ALPHA, None, ALU.mult))
            step(dve.tensor_scalar(split_y.rearrange("p s (a b) -> p (s a) b", b=P), ones.unsqueeze(1).to_broadcast([P, 2 * D // P, P]), 0.0, None, ALU.mult))
            step(dve.tensor_scalar(selT.rearrange("p (a b) -> p a b", b=8), ones[:, 0:8].unsqueeze(1).to_broadcast([P, NT // 8, 8]), 0.0, None, ALU.mult))
            dve.wait_ge(sig("top_exp"), 1)
            step(dve.tensor_scalar(den, dtop, 1.0, None, ALU.add))
            step(dve.reciprocal(g1, den))
            step(tt_(g2, dtop, g1, ALU.mult))
            src = take(dve, "rank")[:, 0:4 * NE].rearrange("p (t e) -> p t e", t=4)
            dve.tensor_copy(counts[:, :], src[:, 3, :])
            for chunk in (1, 2):
                ins = dve.tensor_scalar(over[:, (chunk - 1) * NE:chunk * NE], src[:, 3, :], float(chunk * P), None, ALU.is_gt)
            step(ins)
            step(dve.tensor_tensor_scan(turns[:, 1:], ones[:, 0:2 * NE], over, float(NE), ALU.mult, ALU.add))
            step(dve.memset(turns[:, 0:1], float(NE)))
            step(dve.tensor_copy(turn[:, :], turns))
            step(dve.scalar_tensor_tensor(pos, src[:, 0:3, :], 1.0, Msel, ALU.add, ALU.mult))
            step(dve.tensor_scalar(pos, pos, -1.0, None, ALU.add))
            step(tt_(gates, oh1, g1.unsqueeze(2).to_broadcast([P, 3, NE]), ALU.mult))
            step(tt_(tmp24, oh2, g2.unsqueeze(2).to_broadcast([P, 3, NE]), ALU.mult))
            step(tt_(gates, gates, tmp24, ALU.add))
            dve.sem_inc(bank_free[bank_of[("rank",)][0]], 1)
            dve.sem_inc(sig("routed"), 1)
            dve.sem_inc(sig("h_ready"), NG)
            dve.sem_inc(sig("y_split"), 1)
            dve.sem_inc(sig("summed"), 3)

            def unit_lo(t, u):
                dve.wait_ge(sig("unit_hi"), t * UNITS + (UNITS + u + 1))
                tt_(split_w[:, u % SPLITS, 1, :], halves[EXPERT_HALVES[u % HALVES]], split_w[:, u % SPLITS, 0, :].bitcast(F32), ALU.subtract).then_inc(sig("unit_split"), 1)

            def hidden_T(t, c):
                dve.wait_ge(sig("hT_hi"), t * NG + (c + 1))
                tt_(split_he[:, c % 2, 1].rearrange("p f s -> p (f s)"), ps[:, 4 + c % 2, :],
                    split_he[:, c % 2, 0].rearrange("p f s -> p (f s)").bitcast(F32), ALU.subtract).then_inc(sig("hT_ready"), 1)

            def select(e, chunk, t):
                if t is not None:
                    dve.wait_ge(sig("selT_ready"), t * 2)
                dve.tensor_copy(gate_now, gates[:, :, bass.ds(e, 1)].rearrange("p a b -> p (a b)"))
                dve.scalar_tensor_tensor(sel[:, :, :], pos[:, :, bass.ds(e, 1)].to_broadcast([P, 3, P]), float(-chunk * P),
                                         slot_iota.unsqueeze(1).to_broadcast([P, 3, P]), ALU.add, ALU.is_equal).then_inc(sig("selected"), 1)

            def gathered_lo(t):
                for n in range(2):
                    dve.wait_ge(sig("xeT_hi"), t * 2 + (n + 1))
                    tt_(split_xe[:, 1, 4 * n:4 * n + 4, :].rearrange("p k s -> p (k s)"), ps[:, 1 + 2 * n, :],
                        split_xe[:, 0, 4 * n:4 * n + 4, :].rearrange("p k s -> p (k s)").bitcast(F32), ALU.subtract).then_inc(sig("xe_split"), 1)

            def selection_T(t):
                dve.wait_ge(sig("selT_done"), t + 1)
                dve.tensor_copy(selT[:, :], ps[:, 1, 0:NT]).then_inc(sig("selT_ready"), 1)
                dve.tensor_copy(gate_slot, ps[:, 1, NT:NT + 1]).then_inc(sig("selT_ready"), 1)

            def y_lo(t):
                dve.wait_ge(sig("y_hi"), t + 1)
                dve.wait_ge(sig("selT_ready"), t * 2 + 2)
                dve.scalar_tensor_tensor(split_y[:, 1, :].rearrange("p (a b) -> p a b", a=2), ps[:, 6:8, :], gate_slot,
                                         split_y[:, 0, :].rearrange("p (a b) -> p a b", a=2).bitcast(F32), ALU.mult, ALU.subtract).then_inc(sig("y_split"), 1)

            def add_y(t1, part):
                dve.wait_ge(sig("summed"), t1 * 3 + (part + 1))
                dve.wait_ge(sig("scattered"), t1 * 3 + (part + 1))
                if part:
                    v, src = acc[:, part - 1, :].rearrange("p (a b) -> p a b", a=2), ps[:, 2 + 2 * part:4 + 2 * part, :]
                else:
                    v, src = acc_s.rearrange("p a b -> p (a b)"), ps[:, 3, 0:KT * NS]
                tt_(v, v, src, ALU.add).then_inc(sig("summed"), 1)

            def expert(t, before, following):
                for u in range(SPLITS, UNITS):
                    kind, c, i = ORDER[u - SPLITS]
                    if (kind, i) == ("gate", 1) and c:
                        hidden_T(t, c - 1)
                    if (kind, i) == ("up", 1):
                        dve.wait_ge(sig("silu_ready"), t * NG + (c + 1))
                        dve.wait_ge(sig("units_used"), t * UNITS + (UNITS + u - SPLITS + 1))
                        if c >= 2:
                            dve.wait_ge(sig("T_done"), t * NG + (c - 1))
                        tt_(hgu[:, c % 2, :], hsil[:, c % 2, :], ps[:, 2 + c % 2, :], ALU.mult).then_inc(sig("h_ready"), 1)
                    unit_lo(t, u)
                    if u == 4:
                        if before:
                            add_y(t, 0)
                        selection_T(t)
                    if before and u in (5, 6):
                        add_y(t, u - 4)
                    if following is not None and u == UNITS // 2:
                        select(following, 0, t + 1)
                hidden_T(t, NG - 1)

            select(0, 0, None)
            for u in range(SPLITS):
                unit_lo(0, u)
            gathered_lo(0)
            with dve.Fori(0, NE - 1) as e:
                expert(e, True, e + 1)
                unit_lo(e + 1, 0)
                gathered_lo(e + 1)
                unit_lo(e + 1, 1)
                y_lo(e)
                unit_lo(e + 1, 2)
            expert(NE - 1, True, None)
            y_lo(NE - 1)
            for part in range(3):
                add_y(NE, part)
            runs = dve.value_load(turn[0:1, 2 * NE:2 * NE + 1], min_val=NE, max_val=3 * NE)
            with dve.If(runs > NE):
                for chunk in (1, 2):
                    with dve.Fori(0, NE) as e:
                        n_tok = dve.value_load(counts[0:1, bass.ds(e, 1)], min_val=0, max_val=NT)
                        t = dve.value_load(turn[0:1, bass.ds(e + (chunk - 1) * NE, 1)], min_val=NE, max_val=3 * NE)
                        with dve.If(n_tok > chunk * P):
                            select(e, chunk, t)
                            for u in range(SPLITS):
                                unit_lo(t, u)
                            gathered_lo(t)
                            expert(t, False, None)
                            y_lo(t)
                            for part in range(3):
                                add_y(t + 1, part)
            dve.wait_ge(sig("summed"), runs * 3 + 6)
            dve.sem_inc(sig("sums_ready"), 1)
            rows = [acc[:, 0, :], acc[:, 1, :], acc_st[0:NS, :]]
            for t in range(3):
                r = slice(0, P if t < 2 else NS)
                if t == 2:
                    dve.wait_ge(sig("sample_rows"), 1)
                    step(dve.tensor_copy(rows[2].rearrange("p (a b) -> p a b", a=2), ps[0:NS, 6:8, :]))
                for i in range(2):
                    step(dve.bn_stats(stats[r, t, i, :], rows[t][:, 512 * i:512 * i + 512]))
                step(dve.bn_aggr(mv[r, t, :], stats[r, t].rearrange("p a b -> p (a b)")))
                dve.sem_inc(sig("fin_var"), 1)
            dve.wait_ge(sig("ln_bc_landed"), 32)
            for t in range(3):
                r = slice(0, P if t < 2 else NS)
                dve.wait_ge(sig("fin_root"), t + 1)
                step(dve.reciprocal(rs3[r, t:t + 1], rs3[r, t:t + 1]))
                step(dve.tensor_scalar(rows[t], rows[t], mv[r, t, 0:1], rs3[r, t:t + 1], ALU.subtract, ALU.mult))
                step(tt_(rows[t], rows[t], ln_bc[r, 0, :], ALU.mult))
                step(tt_(rows[t], rows[t], ln_bc[r, 1, :], ALU.add))
                dve.sem_inc(sig("fin_ready"), 1)

        @block.tensor
        def _(pe):
            def bank(*name):
                b, before = bank_of[name]
                if before:
                    pe.wait_ge(bank_free[b], before)
                return ps[:, b, :]

            def full(ins, *name):
                ins.then_inc(bank_full[bank_of[name][0]], 1)

            def used(ins):
                ins.then_inc(slabs_used, 1)

            def tr(o, i, n=P):
                return pe.transpose(o, i, ident[0:n, 0:n])

            def mm(o, l, r, start, stop):
                return pe.matmul(o, l, r, start=start, stop=stop)

            pe.wait_ge(sig("consts"), 1)
            pe.wait_ge(sig("x_landed"), 32)
            for n in range(2 * TT):
                tt, kg = divmod(n, 2)
                o = bank("x", n)
                for q in range(4):
                    ins = tr(o[:, q * P:(q + 1) * P], xrows[:, tt, (4 * kg + q) * P:(4 * kg + q + 1) * P])
                full(ins, "x", n)
            o = bank("xs")
            for k in range(KT):
                ins = tr(o[:, k * NS:(k + 1) * NS], xrows[0:NS, TT, k * P:(k + 1) * P], NS)
            full(ins, "xs")
            pe.wait_ge(sig("params_landed"), 16 * 8)
            full(tr(bank("params", 0)[:, 0:85], prow[0:85, 0, :], 85), "params", 0)
            full(tr(bank("params", 1)[:, 0:64], prow[0:64, 1, :], 64), "params", 1)

            def mem_kv(lay):
                pe.wait_ge(sig(f"mem{lay}_landed"), 16)
                for n in range(2 * MT):
                    tt, kg = divmod(n, 2)
                    o = bank("mem", lay, n)
                    for q in range(4):
                        ins = tr(o[:, q * P:(q + 1) * P], memrows[lay][:, tt, (4 * kg + q) * P:(4 * kg + q + 1) * P])
                    full(ins, "mem", lay, n)
                pe.wait_ge(sig("mem_in"), lay + 1)
                wait_slab(pe, ("kv", lay))
                w = as_slab(slab(("kv", lay)), KT, 2 * DX)
                for mt in range(MT):
                    o = bank("kv", lay, mt)
                    for k in range(KT):
                        ins = mm(o, memT[:, k, mt * P:(mt + 1) * P], w[:, k, :], k == 0, k == KT - 1)
                    full(ins, "kv", lay, mt)
                b, before = bank_of[("kv", lay, MT - 1)]
                pe.wait_ge(sig("kv_rows"), lay + 1)
                used(pe.nop()) if False else pe.sem_inc(slabs_used, 1)
                o = bank("kT", lay)
                for ft in range(XT_):
                    for mt in range(MT):
                        ins = tr(o[:, (ft * MT + mt) * P:(ft * MT + mt + 1) * P], kv[:, mt, ft * P:(ft + 1) * P])
                full(ins, "kT", lay)

            def project(o, w, c0, m, act_t):
                for k in range(KT):
                    ins = mm(o[0:m, 0:NT], w[:, k, c0:c0 + m], act_t[:, k, :], k == 0, k == KT - 1)
                return ins

            mem_kv(0)
            pe.wait_ge(sig("hist_landed"), 16)
            for n in range(5):
                o = bank("hist", n)
                for q in range(min(4, CT - 4 * n)):
                    ins = tr(o[:, q * 24:(q + 1) * 24], histrows[0:24, (4 * n + q) * P:(4 * n + q + 1) * P], 24)
                full(ins, "hist", n)
            pe.wait_ge(sig("x_in"), 1)
            def norm_sums(half):
                pe.wait_ge(sig("qk_squared"), half + 1)
                for h in range(H):
                    full(mm(bank("norm", H * half + h)[:, 0:NT], ones, sqk[half][:, h, :], True, True), "norm", H * half + h)

            for c in range(CT + H):
                if c in (CT + 3, CT + 4):
                    norm_sums(c - CT - 3)
                what = ("in", 0, c // 4)
                if c % 4 == 0:
                    wait_slab(pe, what)
                ins = project(bank("proj", 0, c), as_slab(slab(what), KT, FC), (c % 4) * P, P, xT)
                full(ins, "proj", 0, c)
                if c % 4 == 3:
                    b, before = bank_of[("proj", 0, c)]
                    pe.wait_ge(bank_full[b], before + 1)
                    pe.sem_inc(slabs_used, 1)
            wait_slab(pe, ("in", 0, 6))
            w = as_slab(slab(("in", 0, 6)), KT, IN_A - 6 * FC)
            for name, c0, m in (("a", 0, H), ("b", H, H), (0, 2 * H, P), (1, 2 * H + P, P)):
                full(project(bank("projx", 0, name), w, c0, m, xT), "projx", 0, name)
            b, before = bank_of[("projx", 0, 1)]
            pe.wait_ge(bank_full[b], before + 1)
            pe.sem_inc(slabs_used, 1)
            nr = PADT + NS
            pe.wait_ge(sig("conv_begun"), CT)
            for n in range(5):
                o = bank("tail", n)
                for q in range(min(4, CT - 4 * n)):
                    ins = tr(o[0:nr, q * P:(q + 1) * P], pre[:, 4 * n + q, SEQ:SEQ + nr])
                full(ins, "tail", n)

            def attend(lay):
                pe.wait_ge(sig("xq_ready"), lay + 1)
                pe.wait_ge(sig("kT_ready"), lay + 1)
                for h in range(HX):
                    r = slice(DH * (h % 2), DH * (h % 2) + DH)
                    o = bank("score", lay, h)
                    for tt in range(TT):
                        ins = mm(o[:, tt * MEM:(tt + 1) * MEM], xq[r, h // 2, tt * P:(tt + 1) * P], kT[r, h // 2, :], True, True)
                    full(ins, "score", lay, h)
                pe.wait_ge(sig("attn_p"), lay + 1)
                for h in range(HX):
                    o = bank("pT", lay, h)
                    for mt in range(MT):
                        for tt in range(TT):
                            ins = tr(o[:, mt * SEQ + tt * P:mt * SEQ + (tt + 1) * P], p_att[:, TT * h + tt, mt * P:(mt + 1) * P])
                    full(ins, "pT", lay, h)
                for n in range(2):
                    o = bank("pv", lay, n)
                    for h in (2 * n, 2 * n + 1):
                        b, before = bank_of[("pT", lay, h)]
                        pe.wait_ge(bank_free[b], before + 1)
                        r = slice(DH * (h % 2), DH * (h % 2) + DH)
                        for mt in range(MT):
                            ins = mm(o[r, 0:SEQ], kv[:, mt, DX + h * DH:DX + (h + 1) * DH], pT_att[:, h, mt, :], mt == 0, mt == MT - 1)
                    full(ins, "pv", lay, n)
                pe.wait_ge(sig("qpad_ready"), lay + 1)

                def keys(b):
                    pe.wait_ge(sig("k_landed"), 16 * (lay + 1))
                    o = bank("cacheT", lay, b)
                    for k in range(XT_):
                        for mt in range(MT):
                            ins = tr(o[:, (k * MT + mt) * P:(k * MT + mt + 1) * P], Kc[:, b, mt, k * P:(k + 1) * P])
                    full(ins, "cacheT", lay, b)

                keys(0)
                o = bank("sscore", lay)
                for b in range(NS):
                    if b + 1 < NS:
                        keys(b + 1)
                    bk, before = bank_of[("cacheT", lay, b)]
                    pe.wait_ge(bank_free[bk], before + 1)
                    for k in range(XT_):
                        last = b == NS - 1 and k == XT_ - 1
                        ins = pe.matmul(o[0:4 * NS, 0:MEM], qpad[:, k, b, :], KTs[:, b % 2, k, :], start=(b == 0 and k == 0), stop=last)
                        if k == XT_ - 1 and not last:
                            ins.then_inc(sig("sscored"), 1)
                full(ins, "sscore", lay)
                pe.wait_ge(bank_full[bank_of[("sscore", lay)][0]], bank_of[("sscore", lay)][1] + 1)
                pe.sem_inc(sig("sscored"), 1)
                pe.wait_ge(sig("ss_p"), lay + 1)
                o = bank("spT", lay)
                for mt in range(MT):
                    ins = tr(o[:, mt * 4 * NS:(mt + 1) * 4 * NS], ps_att[0:4 * NS, mt * P:(mt + 1) * P], 4 * NS)
                full(ins, "spT", lay)
                pe.wait_ge(sig("ss_pT"), lay + 1)
                pe.wait_ge(sig("v_landed"), 16 * (lay + 1))
                o = bank("spv", lay)
                for k in range(XT_):
                    for b in range(NS):
                        for mt in range(MT):
                            ins = mm(o[:, (k * NS + b) * 4:(k * NS + b) * 4 + 4], Vc[:, b, mt, k * P:(k + 1) * P], pTs[:, mt, 4 * b:4 * b + 4], mt == 0, mt == MT - 1)
                full(ins, "spv", lay)

            attend(0)
            pe.wait_ge(sig("gates_ready"), 1)
            pe.wait_ge(sig("qk_normed"), 2)
            o = bank("sgate")
            for i, v in enumerate((gc, beta)):
                for h in range(H):
                    ins = mm(o[:, (i * H + h) * NS:(i * H + h + 1) * NS], ident[0:H, h:h + 1].to_broadcast([H, P]), v[0:H, SEQ:NT], True, True)
            full(ins, "sgate")
            pe.wait_ge(sig("s_prod"), 1)
            full(mm(bank("sdot")[:, 0:H * NS], ones, s_kq.rearrange("p h b -> p (h b)"), True, True), "sdot")
            pe.wait_ge(sig("state_landed"), 16)
            o = bank("sread")
            for h in range(H):
                for b in range(NS):
                    n = (h * NS + b) * 2
                    ins = mm(o[:, n:n + 2], state[:, b * H + h, :], qkv[:, h:h + H + 1:H, SEQ + b], True, True)
            full(ins, "sread")
            for n in range(2):
                o = bank("krow", n)
                for q in range(3):
                    ins = tr(o[0:NS, q * P:(q + 1) * P], qkv[:, H + 3 * n + q, SEQ:NT])
                full(ins, "krow", n)
            pe.wait_ge(sig("s_mixed"), 1)
            for n in range(2):
                o = bank("urow", n)
                for q in range(3):
                    ins = tr(o[0:NS, q * P:(q + 1) * P], s_u[:, 3 * n + q, :])
                full(ins, "urow", n)
            pe.wait_ge(sig("s_rows"), 1)
            for h in range(H):
                pe.wait_ge(sig("udiag_ready"), h + 1)
                for n in range(2):
                    full(mm(bank("outer", h, n), krow[0:NS, h, :], udiag[0:NS, h % 2, 512 * n:512 * n + 512], True, True), "outer", h, n)
            pe.wait_ge(sig("masks"), 1)
            for n in range(TT):
                chunk = slice(n * P, (n + 1) * P)
                for name, v in (("gb", gc), ("bb", beta)):
                    for i in range(2):
                        o = bank(name, n, i)
                        for q in range(3):
                            ins = mm(o[:, q * P:(q + 1) * P], ident[0:H, 3 * i + q:3 * i + q + 1].to_broadcast([H, P]), v[0:H, chunk], True, True)
                        full(ins, name, n, i)
                o = bank("gcol", n)
                tr(o[:, 0:H], gc[0:H, chunk], H)
                full(tr(o[:, H:2 * H], beta[0:H, chunk], H), "gcol", n)

                def heads(name, left, right, trans=False, more=None):
                    for i in range(2):
                        o = bank(*name, i)
                        for q in range(3):
                            h = 3 * i + q
                            oh = o[:, q * P:(q + 1) * P]
                            if trans:
                                ins = tr(oh, left(h))
                            else:
                                ins = mm(oh, left(h), right(h), True, more is None)
                                if more is not None:
                                    ins = mm(oh, more[0](h), more[1](h), False, True)
                        full(ins, *name, i)

                kT_h = lambda h: qkv[:, H + h, chunk]
                heads(("kk", n), kT_h, kT_h)
                heads(("qk", n), kT_h, lambda h: qkv[:, h, chunk])
                heads(("ktok", n), kT_h, None, True)
                heads(("vtok", n), lambda h: qkv[:, 2 * H + h, chunk], None, True)
                pe.wait_ge(sig("XT_ready"), n + 1)
                heads(("xinit", n), lambda h: XT[:, h, :], None, True)
                pe.wait_ge(sig("X_ready"), n + 1)
                for s in range(1, 7):
                    pe.wait_ge(sig("AmT_ready"), 6 * n + s)
                    if s > 1:
                        for i in range(2):
                            for nm in ("dX", "dXT"):
                                b, before = bank_of[(nm, n, s - 1, i)]
                                pe.wait_ge(bank_free[b], before + 1)
                    heads(("Y", n, s), lambda h: AmT[:, h, :], lambda h: X[:, h, :])
                    for i in range(2):
                        b, before = bank_of[("Y", n, s, i)]
                        pe.wait_ge(bank_free[b], before + 1)
                    if s < 6:
                        heads(("dX", n, s), lambda h: XT[:, h, :], lambda h: Y[:, h, :])
                    heads(("dXT", n, s), lambda h: Y[:, h, :], lambda h: XT[:, h, :])
                for i in range(2):
                    b, before = bank_of[("dXT", n, 6, i)]
                    pe.wait_ge(bank_free[b], before + 1)
                if n:
                    heads(("wT", n), lambda h: kbg[:, h, :], lambda h: XT[:, h, :])
                    for i in range(2):
                        b, before = bank_of[("wT", n, i)]
                        pe.wait_ge(bank_free[b], before + 1)
                    pe.wait_ge(sig("S_ready"), n)
                    heads(("vnew", n), lambda h: XT[:, h, :], lambda h: vb[:, h, :], more=(lambda h: AmT[:, h, :], lambda h: S[:, h, :]))
                else:
                    heads(("vnew", n), lambda h: XT[:, h, :], lambda h: vb[:, h, :])
                for i in range(2):
                    b, before = bank_of[("vnew", n, i)]
                    pe.wait_ge(bank_free[b], before + 1)
                pe.sem_inc(sig("w_done"), 1)
                heads(("o", n), lambda h: Y[:, h, :], lambda h: attnT[:, h, :],
                      more=(lambda h: S[:, h, :], lambda h: qkv[:, h, chunk]) if n else None)
                heads(("S", n), lambda h: kdec[:, h, :], lambda h: Y[:, h, :])
            pe.wait_ge(sig("o_squared"), 1)
            for h in range(H):
                full(mm(bank("rms", h)[:, 0:NT], ones, sq[:, h, :], True, True), "rms", h)

            def w_out(lay):
                pe.wait_ge(sig("mix_ready"), lay + 1)
                pe.wait_ge(sig("attn_done"), lay + 1)
                for c in range(KT):
                    what = ("out", lay, c // 4)
                    if c % 4 == 0:
                        wait_slab(pe, what)
                    full(project(bank("out", lay, c), as_slab(slab(what), KT, FC), (c % 4) * P, P, mixT), "out", lay, c)
                    if c % 4 == 3:
                        b, before = bank_of[("out", lay, c)]
                        pe.wait_ge(bank_full[b], before + 1)
                        pe.sem_inc(slabs_used, 1)

            def variance(o, tiles, first):
                for k in range(tiles):
                    if k % 2 == 0:
                        pe.wait_ge(sig("ln_squared"), first + k // 2 + 1)
                    ins = mm(o[:, 0:NT], ones, sq[:, k, :], k == 0, k == tiles - 1)
                return ins

            def norm(lay, which, count):
                pe.wait_ge(sig("res_ready"), count)
                full(mm(bank("ln_mean", lay, which)[:, 0:NT], ones, mu, True, True), "ln_mean", lay, which)
                full(variance(bank("ln_var", lay, which), KT, LN_PARTS[lay, which]), "ln_var", lay, which)

            w_out(0)
            norm(0, 0, 1)
            def three(o, w, x, first, last):
                mm(o, w[0], x[0], first, False)
                mm(o, w[1], x[0], False, False)
                return mm(o, w[0], x[1], False, last)

            for u, (kind, c, i) in enumerate(ORDER):
                pe.wait_ge(sig("unit_split"), u + 1)
                if u == 0:
                    pe.wait_ge(sig("x_lo"), 2)
                n_k = KT if kind != "down" else 4
                w = split_w[:, u % SPLITS].rearrange("p s (k n) -> p s k n", k=n_k)
                if kind == "down":
                    pe.wait_ge(sig("hid_ready"), 4 * (c + 1))
                for q in range(UNIT // n_k // P):
                    n = q + i * (UNIT // n_k // P)
                    o = bank(kind, c, n)
                    for k in range(n_k):
                        x = [split_h[:, c % 2, s, k, :] if kind == "down" else split_x[s][:, k, :] for s in range(2)]
                        ins = three(o[:, 0:NT], [w[:, s, k, q * P:(q + 1) * P] for s in range(2)], x, k == 0, k == n_k - 1)
                    full(ins, kind, c, n)
            norm(0, 1, 2)
            mem_kv(1)
            pe.wait_ge(sig("x_ready"), KT)

            def proj_b(c):
                what = ("in", 1, c // 4)
                if c % 4 == 0:
                    wait_slab(pe, what)
                full(project(bank("proj", 1, c), as_slab(slab(what), KT, FC), (c % 4) * P, P, xT), "proj", 1, c)
                if c % 4 == 3:
                    b, before = bank_of[("proj", 1, c)]
                    pe.wait_ge(bank_full[b], before + 1)
                    pe.sem_inc(slabs_used, 1)

            for c in PROJ_B[:8]:
                proj_b(c)
            pe.wait_ge(sig("ws_landed"), 16)
            for n in range(2):
                o = bank("wsT", n)
                for q in range(3):
                    ins = tr(o[:, q * P:(q + 1) * P], wsrows[:, 3 * n + q, :])
                full(ins, "wsT", n)
            o = bank("vmean")
            for k in range(GB):
                b, before = bank_of[("proj", 1, GB + k)]
                pe.wait_ge(bank_free[b], before + 1)
                ins = mm(o[:, 0:NT], ones, vT[:, k, :], k == 0, k == GB - 1)
            full(ins, "vmean")
            proj_b(PROJ_B[8])
            proj_b(PROJ_B[9])
            full(variance(bank("vvar"), GB, LN_PARTS["v"]), "vvar")
            proj_b(PROJ_B[10])
            proj_b(PROJ_B[11])
            wait_slab(pe, ("in", 1, 3))
            w = as_slab(slab(("in", 1, 3)), KT, 2 * P)
            for i in range(2):
                full(project(bank("projx", 1, i), w, i * P, P, xT), "projx", 1, i)
            b, before = bank_of[("projx", 1, 1)]
            pe.wait_ge(bank_full[b], before + 1)
            pe.sem_inc(slabs_used, 1)
            pe.wait_ge(sig("v_ready"), 1)
            for n in range(4):
                tt, half = divmod(n, 2)
                o = bank("vtokT", n)
                for q in range(3):
                    ins = tr(o[:, q * P:(q + 1) * P], vT[:, 3 * half + q, tt * P:(tt + 1) * P])
                full(ins, "vtokT", n)
            for n in range(2):
                o = bank("vtokS", n)
                for q in range(3):
                    ins = tr(o[0:NS, q * P:(q + 1) * P], vT[:, 3 * n + q, SEQ:NT])
                full(ins, "vtokS", n)
            pe.wait_ge(sig("ws_ready"), 1)
            pe.wait_ge(sig("bs_landed"), 16)
            o = bank("mixrow")
            mm(o[:, 0:GB], ones[0:1, :], wsT[0:1, :, 0], True, True)
            for g in range(GB):
                ins = mm(o[:, GB + g:GB + g + 1], ident[0:GB, g:g + 1].to_broadcast([GB, P]), bsrow[0:GB, 0:1], True, True)
            full(ins, "mixrow")
            attend(1)
            pe.wait_ge(sig("vtok_ready"), 1)
            for g in range(GB):
                o = bank("mixed", g)
                for tt in range(TT):
                    mm(o[:, tt * P:(tt + 1) * P], vtok[:, tt, g * P:(g + 1) * P], wsT[:, g, :], True, False)
                    ins = mm(o[:, tt * P:(tt + 1) * P], ident[0:GB, g:g + 1].to_broadcast([GB, P]), bsrow[0:GB, :], False, True)
                full(ins, "mixed", g)
            w_out(1)
            norm(1, 0, 3)
            pe.wait_ge(sig("x_ready"), 3 * KT // 2)
            pe.wait_ge(sig("router_landed"), 16)
            o = bank("logits")
            for t in range(3):
                m = P if t < 2 else NS
                for k in range(KT):
                    ins = mm(o[0:m, t * NE:(t + 1) * NE], xT[:, k, t * P:t * P + m], router[:, k, :], k == 0, k == KT - 1)
            full(ins, "logits")
            for n in range(2 * TT):
                tt, kg = divmod(n, 2)
                o = bank("x1tok", n)
                for q in range(4):
                    ins = tr(o[:, q * P:(q + 1) * P], xT[:, 4 * kg + q, tt * P:(tt + 1) * P])
                full(ins, "x1tok", n)
            for n in range(2):
                o = bank("x1tokS", n)
                for q in range(4):
                    ins = tr(o[0:NS, q * P:(q + 1) * P], xT[:, 4 * n + q, SEQ:NT])
                full(ins, "x1tokS", n)
            pe.wait_ge(sig("sel_ready"), 1)
            o = bank("rank")
            for t in range(3):
                for u in range(t):
                    mm(o[:, t * NE:(t + 1) * NE], ones, Msel[:, u, :], u == 0, False)
                mm(o[:, t * NE:(t + 1) * NE], strictT, Msel[:, t, :], t == 0, True)
            full(mm(o[:, 3 * NE:4 * NE], ones, Mall, True, True), "rank")
            pe.wait_ge(sig("routed"), 1)
            for n in range(8):
                count = max([before for (bk, before) in bank_of.values() if bk == n]) + 1
                pe.wait_ge(bank_free[n], count)
            pe.sem_inc(sig("units_used"), UNITS)

            def gather(t):
                pe.wait_ge(sig("selected"), t + 1)
                for n in range(2):
                    for q in range(4):
                        k = 4 * n + q
                        for tt in range(3):
                            m = P if tt < TT else NS
                            for part in range(2):
                                ins = mm(ps[:, 1 + 2 * n, q * P:(q + 1) * P], split_xt[0:m, tt, part, k * P:(k + 1) * P], sel[0:m, tt, :],
                                         tt == 0 and part == 0, tt == TT and part == 1)
                    ins.then_inc(sig("gathered"), 1)

            def selection_T(t):
                pe.wait_ge(sig("selected"), t + 1)
                for tt in range(3):
                    m = P if tt < TT else NS
                    tr(ps[:, 1, tt * P:tt * P + m], sel[0:m, tt, :].bitcast(F32), m)
                for tt in range(3):
                    m = P if tt < TT else NS
                    ins = mm(ps[:, 1, NT:NT + 1], sel[0:m, tt, :].bitcast(F32), gate_now[0:m, tt:tt + 1], tt == 0, tt == TT)
                ins.then_inc(sig("selT_done"), 1)

            def scatter(t1):
                pe.wait_ge(sig("y_split"), t1 + 1)
                for k in range(KT):
                    for part in range(2):
                        ins = mm(ps[:, 3, k * NS:(k + 1) * NS], split_y[:, part, k * P:(k + 1) * P], selT[:, SEQ:NT], part == 0, part == 1)
                ins.then_inc(sig("scattered"), 1)
                for tt in range(TT):
                    for half in range(2):
                        for part in range(2):
                            ins = mm(ps[:, 4 + 2 * tt + half, :], selT[:, tt * P:(tt + 1) * P], split_y[:, part, 512 * half:512 * half + 512], part == 0, part == 1)
                    ins.then_inc(sig("scattered"), 1)

            def transpose_h(t, c):
                pe.wait_ge(sig("h_ready"), t * NG + (NG + c + 1))
                for q in range(4):
                    ins = tr(ps[:, 4 + c % 2, q * P:(q + 1) * P], hgu[:, c % 2, q * P:(q + 1) * P])
                ins.then_inc(sig("T_done"), 1)

            def expert(t, before, following):
                pe.wait_ge(sig("xe_split"), t * 2 + 2)
                for u, (kind, c, i) in enumerate(ORDER):
                    if u == 2:
                        if before:
                            scatter(t)
                        selection_T(t)
                    if u == 4:
                        pe.wait_ge(sig("selT_ready"), t * 2 + 2)
                        pe.wait_ge(sig("summed"), t * 3 + 4)
                    if u == ORDER.index(("down", 0, 0)):
                        pe.wait_ge(sig("summed"), t * 3 + 6)
                    if kind == "down" and i == 0 and c == NG - 1:
                        transpose_h(t, c)
                        if following:
                            gather(t + 1)
                    if kind == "gate" and i == 0:
                        pe.wait_ge(sig("h_ready"), t * NG + (NG + c - 1))
                    if kind == "down" and i == 0:
                        pe.wait_ge(sig("hT_ready"), t * NG + (c + 1))
                    pe.wait_ge(sig("unit_split"), t * UNITS + (UNITS + u + 1))
                    w = split_w[:, u % SPLITS]
                    if kind == "down":
                        for q in range(2):
                            x = [split_he[:, c % 2, s, 2 * i + q, :] for s in range(2)]
                            for half in range(2):
                                c0 = q * D + 512 * half
                                ins = three(ps[:, 6 + half, :], x, [w[:, s, c0:c0 + 512] for s in range(2)], c == 0 and i == 0 and q == 0, c == NG - 1 and i == 1 and q == 1)
                    else:
                        b = c % 2 + (2 if kind == "up" else 0)
                        for k in range(4):
                            x = [split_xe[:, s, 4 * i + k, :] for s in range(2)]
                            ins = three(ps[:, b, :], x, [w[:, s, k * FC:(k + 1) * FC] for s in range(2)], i == 0 and k == 0, i == 1 and k == 3)
                    ins.then_inc(sig("units_used"), 1)
                    if kind == "gate" and i == 1 and c:
                        if c == 1:
                            pe.wait_ge(sig("summed"), t * 3 + 5)
                        transpose_h(t, c - 1)

            gather(0)
            with pe.Fori(0, NE - 1) as e:
                expert(e, True, True)
            expert(NE - 1, True, False)
            scatter(NE)
            runs = pe.value_load(turn[0:1, 2 * NE:2 * NE + 1], min_val=NE, max_val=3 * NE)
            with pe.If(runs > NE):
                for chunk in (1, 2):
                    with pe.Fori(0, NE) as e:
                        n_tok = pe.value_load(counts[0:1, bass.ds(e, 1)], min_val=0, max_val=NT)
                        t = pe.value_load(turn[0:1, bass.ds(e + (chunk - 1) * NE, 1)], min_val=NE, max_val=3 * NE)
                        with pe.If(n_tok > chunk * P):
                            pe.wait_ge(sig("summed"), t * 3 + 6)
                            gather(t)
                            expert(t, False, False)
                            scatter(t + 1)
            pe.wait_ge(sig("sums_ready"), 1)
            for k in range(KT):
                ins = tr(ps[0:NS, 6 + k // 4, (k % 4) * P:(k % 4 + 1) * P], acc_s[:, k, :])
            ins.then_inc(sig("sample_rows"), 1)


_INS = ["x_prompt", "x_sample", "state_gdn", "state_conv", "cache_mem_k", "cache_mem_v", "mem_prompt",
        "a_w_in", "a_conv_w", "a_A_log", "a_dt_bias", "a_norm_w", "b_w_in", "b_ln_g", "b_ln_b", "b_w_s",
        "b_b_s", "w_mem_kv", "w_out", "ln1_g", "ln1_b", "ln2_g", "ln2_b", "ffn_w_gu", "ffn_w_down",
        "moe_router", "moe_w_gu", "moe_w_down"]
_OUTS = {
    "y_prompt": (1, SEQ, D), "y_sample": (NS, 1, D), "p_state_gdn": (1, 1, H, P, P),
    "p_state_conv": (1, 1, PADT, CONV), "p_cache_mem_k": (DEPTH, 1, MEM, HX, DH),
    "p_cache_mem_v": (DEPTH, 1, MEM, HX, DH), "s_state_gdn": (1, NS, H, P, P),
    "s_state_conv": (1, NS, PADT, CONV), "s_sgu_v": (1, NS, 1, D_B),
}


def kernel(**inputs):
    import numpy as _np
    import concourse.bacc as _bacc
    from concourse.bass_utils import run_bass_kernel_spmd as _run

    nc = _bacc.Bacc("TRN2", target_bir_lowering=False, num_devices=1)
    arrays, a, out = {}, {}, {}
    for name in _INS:
        arrays[f"in_{name}"] = _np.ascontiguousarray(inputs[name])
        a[name] = nc.dram_tensor(f"in_{name}", arrays[f"in_{name}"].shape, F32, kind="ExternalInput").ap()
    for name, shape in _OUTS.items():
        out[name] = nc.dram_tensor(f"out_{name}", shape, F32, kind="ExternalOutput").ap()
    hybrid_step(nc, a, out)
    r = _run(nc, [arrays], core_ids=[0])
    return tuple(r.results[0][f"out_{name}"] for name in _OUTS)
```
